# Optimizing a Trainium2 kernel written in Bass

```python
import math
import jax, jax.numpy as jnp
from jax import lax
import numpy as np

D_MODEL = 1024
BATCH = 1
SEQ = 256
DEPTH = 2

CHUNK = 64
A_HEADS = 8
A_KV_HEADS = 2
A_HEAD_DIM = 64
WINDOW = 128
WINDOW_CHUNKS = WINDOW // CHUNK
B_HEADS = 8
B_Q_LORA = 384
B_KV_LORA = 256
B_NOPE = 64
B_ROPE = 32
B_V = 64
ROPE_THETA = 10000.0
Q_BLOCK = 128
C_HEADS = 4
C_KEY_DIM = 128
C_VAL_DIM = 128
D_CH = 512
CONV_W = 3
D_FF = 3584
N_EXPERTS = 8
TOP_K = 2
EPS = 1e-6
NEG_INF = -1e30

A_Q = A_HEADS * A_HEAD_DIM
A_KV = A_KV_HEADS * A_HEAD_DIM
EVEN_SIZES = (A_Q, A_KV, A_KV, B_Q_LORA, B_KV_LORA, B_ROPE)
EVEN_IN = A_Q + 2 * A_KV + B_Q_LORA + B_KV_LORA + B_ROPE
EVEN_MIX = A_Q + B_HEADS * B_V
C_QK = C_HEADS * C_KEY_DIM
C_WIDTH = C_HEADS * C_VAL_DIM
ODD_SIZES = (C_QK, C_QK, C_WIDTH, C_WIDTH, D_CH, D_CH, D_CH)
ODD_IN = 2 * C_QK + 2 * C_WIDTH + 3 * D_CH
ODD_MIX = C_WIDTH + D_CH
N_EVEN = (DEPTH + 1) // 2
N_ODD = DEPTH // 2

kernel_name = "chunk_causal_hybrid_swa_mla_retnet_shortconv_moe"

def _split(t, sizes):
    outs, start = [], 0
    for s in sizes:
        outs.append(t[..., start:start + s])
        start += s
    return outs

def rmsnorm(x, g):
    xf = x.astype(jnp.float32)
    y = xf * lax.rsqrt(jnp.mean(xf * xf, axis=-1, keepdims=True) + EPS)
    return (y * g.astype(jnp.float32)).astype(x.dtype)

def swiglu(h, w_gate, w_up, w_down):
    return (jax.nn.silu(h @ w_gate) * (h @ w_up)) @ w_down

def rope(t, cos, sin):
    half = t.shape[-1] // 2
    t1, t2 = t[..., :half], t[..., half:]
    return jnp.concatenate([t1 * cos - t2 * sin, t2 * cos + t1 * sin], axis=-1).astype(t.dtype)

def sliding_window_gqa(q, k, v, sinks, slopes):
    Bn, S, Hq, d = q.shape
    Hkv = k.shape[2]
    G = Hq // Hkv
    N = S // CHUNK
    band = (WINDOW_CHUNKS + 1) * CHUNK
    pad = ((0, 0), (WINDOW_CHUNKS * CHUNK, 0), (0, 0), (0, 0))
    kp, vp = jnp.pad(k, pad), jnp.pad(v, pad)

    def banded(t):
        parts = [t[:, j * CHUNK:j * CHUNK + S].reshape(Bn, N, CHUNK, Hkv, d)
                 for j in range(WINDOW_CHUNKS + 1)]
        return jnp.concatenate(parts, axis=2)

    kb, vb = banded(kp), banded(vp)
    qc = q.reshape(Bn, N, CHUNK, Hkv, G, d)
    s = jnp.einsum('bnqhgd,bnkhd->bnhgqk', qc, kb).astype(jnp.float32) * d ** -0.5
    qi = jnp.arange(CHUNK)
    kk = jnp.arange(band)
    dist = jnp.abs(qi[:, None] + WINDOW_CHUNKS * CHUNK - kk[None, :]).astype(jnp.float32)
    bias = -slopes.reshape(Hkv, G)[:, :, None, None] * dist
    key_pos = jnp.arange(N)[:, None] * CHUNK - WINDOW_CHUNKS * CHUNK + kk[None, :]
    valid = (key_pos >= 0)[None, :, None, None, None, :]
    s = jnp.where(valid, s + bias, NEG_INF)
    sink = jnp.broadcast_to(sinks.astype(jnp.float32).reshape(Hkv, G)[:, :, None, None],
                            s.shape[:-1] + (1,))
    p = jax.nn.softmax(jnp.concatenate([s, sink], axis=-1), axis=-1)[..., :-1]
    o = jnp.einsum('bnhgqk,bnkhd->bnqhgd', p.astype(v.dtype), vb)
    return o.reshape(Bn, S, Hq * d)

def mla(c_q, c_kv, k_rope_raw, q_norm, w_uq, kv_norm, w_ukv, cos, sin):
    Bn, S, _ = c_q.shape
    q = (rmsnorm(c_q, q_norm) @ w_uq).reshape(Bn, S, B_HEADS, B_NOPE + B_ROPE)
    q_nope = q[..., :B_NOPE]
    q_rope = rope(q[..., B_NOPE:], cos[:, :, None], sin[:, :, None])
    kv = (rmsnorm(c_kv, kv_norm) @ w_ukv).reshape(Bn, S, B_HEADS, B_NOPE + B_V)
    k_nope, v = kv[..., :B_NOPE], kv[..., B_NOPE:]
    k_rope = rope(k_rope_raw, cos, sin)
    NB = S // Q_BLOCK
    scale = (B_NOPE + B_ROPE) ** -0.5
    key_chunk = jnp.arange(S) // CHUNK

    def to_blocks(t):
        return t.reshape(Bn, NB, Q_BLOCK, *t.shape[2:]).swapaxes(0, 1)

    def block(args):
        qn, qr, bi = args
        s = (jnp.einsum('bqhd,bkhd->bhqk', qn, k_nope)
             + jnp.einsum('bqhd,bkd->bhqk', qr, k_rope)).astype(jnp.float32) * scale
        q_chunk = (bi * Q_BLOCK + jnp.arange(Q_BLOCK)) // CHUNK
        s = jnp.where(key_chunk[None, :] <= q_chunk[:, None], s, NEG_INF)
        p = jax.nn.softmax(s, axis=-1)
        return jnp.einsum('bhqk,bkhd->bqhd', p.astype(v.dtype), v)

    o = lax.map(block, (to_blocks(q_nope), to_blocks(q_rope), jnp.arange(NB)))
    return o.swapaxes(0, 1).reshape(Bn, S, B_HEADS * B_V)

def retention(q, k, v):
    Bn, S, H, dk = q.shape
    dv = v.shape[-1]
    N = S // CHUNK
    f32 = jnp.float32
    q = q.astype(f32)
    k = k.astype(f32) * dk ** -0.5
    v = v.astype(f32)

    def to_chunks(t):
        return t.reshape(Bn, N, CHUNK, H, t.shape[-1]).transpose(1, 0, 3, 2, 4)

    log_g = jnp.log(1.0 - 2.0 ** (-5.0 - jnp.arange(H, dtype=f32)))
    i = jnp.arange(CHUNK, dtype=f32)
    diff = i[:, None] - i[None, :]
    intra_decay = jnp.where(diff >= 0, jnp.exp(log_g[:, None, None] * jnp.maximum(diff, 0.0)), 0.0)
    cross_decay = jnp.exp(log_g[:, None] * (i + 1.0))
    state_decay = jnp.exp(log_g[:, None] * (CHUNK - 1.0 - i))
    chunk_decay = jnp.exp(log_g * CHUNK)

    def step(R, qkv):
        qc, kc, vc = qkv
        scores = jnp.einsum('bhqd,bhkd->bhqk', qc, kc) * intra_decay
        inner = jnp.einsum('bhqk,bhkv->bhqv', scores, vc)
        cross = jnp.einsum('bhqd,bhdv->bhqv', qc, R) * cross_decay[..., None]
        R = chunk_decay[:, None, None] * R + jnp.einsum('bhkd,bhkv->bhdv', kc * state_decay[..., None], vc)
        return R, inner + cross

    R0 = jnp.zeros((Bn, H, dk, dv), f32)
    _, out = lax.scan(step, R0, (to_chunks(q), to_chunks(k), to_chunks(v)))
    return out.transpose(1, 0, 3, 2, 4).reshape(Bn, S, H, dv)

def head_group_norm(y, g):
    mu = jnp.mean(y, axis=-1, keepdims=True)
    var = jnp.mean(jnp.square(y - mu), axis=-1, keepdims=True)
    yn = (y - mu) * lax.rsqrt(var + EPS)
    return yn.reshape(y.shape[0], y.shape[1], -1) * g.astype(jnp.float32)

def short_gated_conv(b_gate, c_gate, h, w):
    S = h.shape[1]
    u = jnp.pad(c_gate * h, ((0, 0), (CONV_W - 1, 0), (0, 0)))
    y = sum(w[j] * u[:, j:j + S] for j in range(CONV_W))
    return b_gate * y

def moe(h, router, we_gate, we_up, we_down):
    logits = jnp.einsum('bsd,de->bse', h, router).astype(jnp.float32)
    top_val, top_idx = lax.top_k(logits, TOP_K)
    gates = jax.nn.softmax(top_val, axis=-1)
    combine = jnp.sum(jax.nn.one_hot(top_idx, N_EXPERTS, dtype=jnp.float32) * gates[..., None], axis=-2)
    out = jnp.zeros(h.shape, jnp.float32)
    for e in range(N_EXPERTS):
        out = out + combine[..., e:e + 1] * swiglu(h, we_gate[e], we_up[e], we_down[e]).astype(jnp.float32)
    return out.astype(h.dtype)

def setup_inputs(seed: int = 0) -> dict:
    key = jax.random.key(seed)
    ks = iter(jax.random.split(key, 32))
    f32 = jnp.float32

    def w(shape, fan_in):
        return jax.random.normal(next(ks), shape, f32) * fan_in ** -0.5

    def gain(shape):
        return 1.0 + 0.1 * jax.random.normal(next(ks), shape, f32)

    x = jax.random.normal(next(ks), (BATCH, SEQ, D_MODEL), f32)
    offsets = jax.random.randint(next(ks), (BATCH, 1), 0, 64, dtype=jnp.int32) * CHUNK
    positions = (offsets + jnp.arange(SEQ, dtype=jnp.int32)[None, :]).astype(jnp.int32)
    return {
        "x": x,
        "positions": positions,
        "even_norm_mix": gain((N_EVEN, D_MODEL)),
        "even_w_in": w((N_EVEN, D_MODEL, EVEN_IN), D_MODEL),
        "even_sinks": jax.random.normal(next(ks), (N_EVEN, A_HEADS), f32),
        "even_q_norm": gain((N_EVEN, B_Q_LORA)),
        "even_w_uq": w((N_EVEN, B_Q_LORA, B_HEADS * (B_NOPE + B_ROPE)), B_Q_LORA),
        "even_kv_norm": gain((N_EVEN, B_KV_LORA)),
        "even_w_ukv": w((N_EVEN, B_KV_LORA, B_HEADS * (B_NOPE + B_V)), B_KV_LORA),
        "even_w_out": w((N_EVEN, EVEN_MIX, D_MODEL), EVEN_MIX),
        "even_norm_ffn": gain((N_EVEN, D_MODEL)),
        "even_w_gate": w((N_EVEN, D_MODEL, D_FF), D_MODEL),
        "even_w_up": w((N_EVEN, D_MODEL, D_FF), D_MODEL),
        "even_w_down": w((N_EVEN, D_FF, D_MODEL), D_FF),
        "odd_norm_mix": gain((N_ODD, D_MODEL)),
        "odd_w_in": w((N_ODD, D_MODEL, ODD_IN), D_MODEL),
        "odd_ret_gn": gain((N_ODD, C_WIDTH)),
        "odd_conv_w": w((N_ODD, CONV_W, D_CH), CONV_W),
        "odd_w_out": w((N_ODD, ODD_MIX, D_MODEL), ODD_MIX),
        "odd_norm_ffn": gain((N_ODD, D_MODEL)),
        "odd_router": w((N_ODD, D_MODEL, N_EXPERTS), D_MODEL),
        "odd_we_gate": w((N_ODD, N_EXPERTS, D_MODEL, D_FF), D_MODEL),
        "odd_we_up": w((N_ODD, N_EXPERTS, D_MODEL, D_FF), D_MODEL),
        "odd_we_down": w((N_ODD, N_EXPERTS, D_FF, D_MODEL), D_FF),
        "final_norm": gain((D_MODEL,)),
    }

def reference(x, positions, even_norm_mix, even_w_in, even_sinks, even_q_norm, even_w_uq,
              even_kv_norm, even_w_ukv, even_w_out, even_norm_ffn, even_w_gate, even_w_up,
              even_w_down, odd_norm_mix, odd_w_in, odd_ret_gn, odd_conv_w, odd_w_out,
              odd_norm_ffn, odd_router, odd_we_gate, odd_we_up, odd_we_down, final_norm):
    Bn, S, _ = x.shape
    inv_freq = ROPE_THETA ** (-jnp.arange(0, B_ROPE, 2, dtype=jnp.float32) / B_ROPE)
    ang = positions.astype(jnp.float32)[..., None] * inv_freq
    cos, sin = jnp.cos(ang), jnp.sin(ang)
    slopes = 2.0 ** (-8.0 * (jnp.arange(A_HEADS, dtype=jnp.float32) + 1.0) / A_HEADS)

    for layer in range(DEPTH):
        i = layer // 2
        if layer % 2 == 0:
            h = rmsnorm(x, even_norm_mix[i])
            qa, ka, va, cq, ckv, kr = _split(h @ even_w_in[i], EVEN_SIZES)
            ya = sliding_window_gqa(qa.reshape(Bn, S, A_HEADS, A_HEAD_DIM),
                                    ka.reshape(Bn, S, A_KV_HEADS, A_HEAD_DIM),
                                    va.reshape(Bn, S, A_KV_HEADS, A_HEAD_DIM),
                                    even_sinks[i], slopes)
            yb = mla(cq, ckv, kr, even_q_norm[i], even_w_uq[i], even_kv_norm[i], even_w_ukv[i], cos, sin)
            x = x + (jnp.concatenate([ya.astype(x.dtype), yb.astype(x.dtype)], axis=-1) @ even_w_out[i])
            x = x + swiglu(rmsnorm(x, even_norm_ffn[i]), even_w_gate[i], even_w_up[i], even_w_down[i])
        else:
            h = rmsnorm(x, odd_norm_mix[i])
            qc, kc, vc, gc, bd, cd, hd = _split(h @ odd_w_in[i], ODD_SIZES)
            yr = retention(qc.reshape(Bn, S, C_HEADS, C_KEY_DIM),
                           kc.reshape(Bn, S, C_HEADS, C_KEY_DIM),
                           vc.reshape(Bn, S, C_HEADS, C_VAL_DIM))
            yc = (jax.nn.silu(gc.astype(jnp.float32)) * head_group_norm(yr, odd_ret_gn[i])).astype(x.dtype)
            yd = short_gated_conv(bd, cd, hd, odd_conv_w[i]).astype(x.dtype)
            x = x + (jnp.concatenate([yc, yd], axis=-1) @ odd_w_out[i])
            x = x + moe(rmsnorm(x, odd_norm_ffn[i]), odd_router[i], odd_we_gate[i], odd_we_up[i], odd_we_down[i])
    return rmsnorm(x, final_norm)


_drawn_inputs = setup_inputs


def setup_inputs(seed=0):
    import zlib

    import numpy as np

    out = dict(_drawn_inputs(seed))
    spreads = {}
    factors = {}
    for name, (base, spread) in spreads.items():
        noise = np.random.default_rng([zlib.crc32(name.encode()), seed]).standard_normal(out[name].shape)
        drawn = base * np.exp(spread * noise) if base else spread * noise
        out[name] = __import__('jax').numpy.asarray(drawn.astype(out[name].dtype))
    for name, factor in factors.items():
        out[name] = (out[name] * factor).astype(out[name].dtype)
    return out
```

```python
import math
from contextlib import ExitStack

import numpy as np

import concourse.bass as bass
from concourse import mybir

F32 = mybir.dt.float32
F32R = mybir.dt.float32r
I32 = mybir.dt.int32
U32 = mybir.dt.uint32
ALU = mybir.AluOpType
ACT = mybir.ActivationFunctionType
AX = mybir.AxisListType

P = 128
SEQ = 256
NT = SEQ // P
D = 1024
KD = D // P
CHUNK = 64
EPS = 1e-6
HALF = 512
A_HEADS, A_KV, A_DIM = 8, 2, 64
B_HEADS, B_NOPE, B_ROPE, B_V = 8, 64, 32, 64
B_DIM = B_NOPE + B_ROPE
Q_LORA, KV_LORA = 384, 256
ROPE_HALF = B_ROPE // 2
ROPE_THETA = 10000.0
EVEN_IN = A_HEADS * A_DIM + 2 * A_KV * A_DIM + Q_LORA + KV_LORA + B_ROPE
COL_K = A_HEADS * A_DIM
COL_V = COL_K + A_KV * A_DIM
COL_CQ = COL_V + A_KV * A_DIM
COL_CKV = COL_CQ + Q_LORA
COL_KR = COL_CKV + KV_LORA
IN_CHUNK = EVEN_IN // 3
A_SCALE = float(A_DIM) ** -0.5
B_SCALE = float(B_DIM) ** -0.5
MASKED = 1.0e32
C_HEADS, C_DIM = 4, 128
CONV_W = 3
D_FF = 3584
FC = D_FF // HALF
EXPERTS = 8
SLOTS = 128

RING = 6
AHEAD = 6
UNIT = 2048
PIECE = 1024
GATE_UNITS, DOWN_UNITS = 4, 2
CHUNK_UNITS = GATE_UNITS + DOWN_UNITS
CHUNK_PIECES = 2 * CHUNK_UNITS
PASS_UNITS = FC * CHUNK_UNITS
PASS_PIECES = 2 * PASS_UNITS
U_IN, U_UQ, U_UKV, U_OUT = 6, 2, 1, 4
FFN_UNIT = U_IN + U_UQ + U_UKV + U_OUT
ODD_UNIT = FFN_UNIT + PASS_UNITS
ODD_IN_CHUNKS = 7
MOE_UNIT = ODD_UNIT + 2 * ODD_IN_CHUNKS + U_OUT
assert CHUNK_UNITS == RING and EVEN_IN % 3 == 0
LOOP_FIRST = 2


class FfnSignals:

    def __init__(self, sem, name, tiles, gate, up, turned, y):
        self.tiles = tiles
        self.gate_banks, self.up_banks, self.turned_banks, self.y_banks = gate, up, turned, y
        self.silu_done = sem(f"{name}_silu_done")
        self.act_done = sem(f"{name}_act_done")
        self.turned = sem(f"{name}_turned")
        self.turned_hi = sem(f"{name}_turned_hi")
        self.turned_lo = sem(f"{name}_turned_lo")


def build_trunk(nc, ins, out):
    g = ins
    with ExitStack() as ctx:
        def sb(name, shape, dt=F32):
            return ctx.enter_context(nc.sbuf_tensor(name, shape, dt))

        def sem(name):
            return ctx.enter_context(nc.semaphore(name))

        raw = sb("raw", [P, RING, UNIT])
        w_hi = sb("w_hi", [P, RING, PIECE], F32R)
        w_lo = sb("w_lo", [P, RING, PIECE], F32R)
        x = sb("x", [P, NT, D])
        tok_hi = sb("tok_hi", [P, KD, SEQ], F32R)
        tok_lo = sb("tok_lo", [P, KD, SEQ], F32R)
        fT_hi = sb("fT_hi", [P, 4, SEQ], F32R)
        fT_lo = sb("fT_lo", [P, 4, SEQ], F32R)
        gain = sb("gain", [P, D])
        lat_gain = sb("lat_gain", [P, Q_LORA + KV_LORA])
        gn_gain = lat_gain[:, 0:C_HEADS * C_DIM]
        ident = sb("ident", [P, P])
        xn = sb("xn", [P, NT, D])
        spare = sb("spare", [P, 2 * D])
        hid = spare[:, 0:D].rearrange("p (t n) -> p t n", t=NT)
        y_sb = spare[:, D:2 * D]
        arena = sb("arena", [P, 11648])

        taken = [0]

        def part(shape):
            n = int(np.prod(shape))
            at = taken[0]
            taken[0] += n
            assert taken[0] <= 11648, taken[0]
            v = arena[:, at:at + n]
            if len(shape) == 2:
                v = v.rearrange("p (a b) -> p a b", a=shape[0])
            if len(shape) == 3:
                v = v.rearrange("p (a b c) -> p a b c", a=shape[0], b=shape[1])
            return v

        proj = part([NT, EVEN_IN])
        q96 = part([NT, B_HEADS, B_DIM])
        k96 = part([NT, B_HEADS, B_DIM])
        qaT = part([4, SEQ])
        kaT = part([A_KV, SEQ])
        bias = part([A_HEADS, SEQ])
        kbT = bias
        qbT = part([B_HEADS, SEQ])
        v64 = proj[:, :, 0:B_HEADS * B_V].rearrange("p t (h d) -> p t h d", h=B_HEADS)
        latkv_hi, latkv_lo = tok_hi[:, 4:6, :], tok_lo[:, 4:6, :]
        ka_twice = q96[:, :, :, :].rearrange("p t h n -> p t (h n)")[:, :, 0:2 * A_KV * A_DIM]
        pT_flat = spare[:, :]
        probs_flat = xn[:, :, :].rearrange("p t d -> p (t d)")
        taken[0] = 0
        val = part([NT, C_HEADS, C_DIM])
        gate = part([NT, HALF])
        qT = part([C_HEADS, SEQ])
        kT = part([C_HEADS, SEQ])
        bT = part([4, SEQ])
        uT = part([4, SEQ])
        decay = part([C_HEADS, SEQ])
        sT0 = part([C_HEADS, SEQ])
        sT1 = part([C_HEADS, P])
        conv = part([4, SEQ])
        yr = part([NT, HALF])
        qk_nat = xn[:, :, :].rearrange("p a (t n) -> p a t n", t=NT)
        bc_nat = spare[:, :].rearrange("p (a t n) -> p a t n", a=2, t=NT)
        before = part([P])
        ones = part([P])
        iota_slot = part([SLOTS])
        taken[0] = 0
        pick = part([NT, SLOTS])
        weigh = part([NT, SLOTS])
        weigh_T = part([SEQ])

        small = sb("small", [P, 704])
        used = [0]

        def bit(shape):
            n = int(np.prod(shape))
            at = used[0]
            used[0] += n
            assert used[0] <= 704, used[0]
            v = small[:, at:at + n]
            if len(shape) == 2:
                v = v.rearrange("p (a b) -> p a b", a=shape[0])
            if len(shape) == 3:
                v = v.rearrange("p (a b c) -> p a b c", a=shape[0], b=shape[1])
            return v

        sumsq = bit([NT])
        inv = bit([NT])
        rstd = bit([NT])
        lat_sumsq = bit([NT, 2])
        lat_rstd = bit([NT, 2])
        angle = bit([NT, ROPE_HALF])
        turns = bit([NT, ROPE_HALF])
        cos = bit([NT, ROPE_HALF])
        sin = bit([NT, ROPE_HALF])
        inv_freq = bit([ROPE_HALF])
        pos_f = bit([NT])
        sinks = bit([A_HEADS])
        row_max = bit([A_HEADS])
        neg_max = bit([A_HEADS])
        den = bit([A_HEADS])
        sink_e = bit([A_HEADS])
        kr_rot = bit([NT, B_ROPE])
        conv_rows = sb("conv_rows", [CONV_W * 4, P])
        conv_w = bit([CONV_W, 4])
        bn = bit([NT * C_HEADS, 6])
        mv = bit([NT * C_HEADS, 2])
        gn_rstd = bit([NT * C_HEADS])
        logits = bit([NT, EXPERTS])
        top = bit([NT, 8])
        idx_f = bit([NT, 2])
        gap = bit([NT])
        gate1 = bit([NT])
        gate2 = bit([NT])
        pick1 = bit([NT, EXPERTS])
        pick2 = bit([NT, EXPERTS])
        chosen = bit([NT, EXPERTS])
        iota8 = bit([EXPERTS])
        place1 = bit([NT, EXPERTS])
        most = bit([1])
        N_PASS = 2 * EXPERTS + 1
        place = bit([NT, N_PASS])
        share = bit([NT, N_PASS])
        pos_i = sb("pos_i", [P, NT], I32)
        idx_u = sb("idx_u", [P, NT, 8], U32)
        most_i = sb("most_i", [P, 1], I32)
        router = sb("router", [P, KD, EXPERTS])
        router_hi = sb("router_hi", [P, KD, EXPERTS], F32R)
        router_lo = sb("router_lo", [P, KD, EXPERTS], F32R)
        dist = sb("dist", [P, SEQ])
        rope_tmp = sb("rope_tmp", [P, SEQ])

        ps = ctx.enter_context(nc.psum_tensor("ps", [P, 8, HALF], F32))

        raw_landed = [sem(f"raw_landed{i}") for i in range(RING)]
        hi_done = sem("hi_done")
        lo_done = sem("lo_done")
        piece_used = sem("piece_used")
        x_landed = [sem(f"x_landed{t}") for t in range(NT)]
        gain_landed = sem("gain_landed")
        lat_gain_landed = sem("lat_gain_landed")
        gn_gain_landed = sem("gn_gain_landed")
        pos_landed = sem("pos_landed")
        sinks_landed = sem("sinks_landed")
        conv_landed = sem("conv_landed")
        router_landed = sem("router_landed")
        pool_step = sem("pool_step")
        dve_step = sem("dve_step")
        act_step = sem("act_step")
        ident_done = sem("ident_done")
        bias_done = sem("bias_done")
        route_consts = sem("route_consts")
        dist_done = sem("dist_done")
        decay_exp = sem("decay_exp")
        freq_done = sem("freq_done")
        angle_done = sem("angle_done")
        trig_done = sem("trig_done")
        sumsq_done = sem("sumsq_done")
        inv_done = sem("inv_done")
        rstd_done = sem("rstd_done")
        xn_done = sem("xn_done")
        xnT_done = sem("xnT_done")
        tok_hi_done = sem("tok_hi_done")
        tok_lo_done = sem("tok_lo_done")
        x_updated = sem("x_updated")
        in_act = sem("in_act")
        in_dve = sem("in_dve")
        lat_sq = sem("lat_sq")
        lat_inv = sem("lat_inv")
        lat_std = sem("lat_std")
        lat_done = sem("lat_done")
        latT_done = sem("latT_done")
        latT_hi = sem("latT_hi")
        latT_lo = sem("latT_lo")
        qaT_done = sem("qaT_done")
        qaT_act = sem("qaT_act")
        qaT_dve = sem("qaT_dve")
        ka_doubled = sem("ka_doubled")
        uq_act = sem("uq_act")
        uq_dve = sem("uq_dve")
        ukv_act = sem("ukv_act")
        ukv_dve = sem("ukv_dve")
        kr_done = sem("kr_done")
        rope_done = sem("rope_done")
        kqT_done = sem("kqT_done")
        kqT_act = sem("kqT_act")
        kqT_dve = sem("kqT_dve")
        scored = sem("scored")
        biased = sem("biased")
        max_done = sem("max_done")
        sink_arg = sem("sink_arg")
        exp_done = sem("exp_done")
        probs_done = sem("probs_done")
        pT_done = sem("pT_done")
        pT_act = sem("pT_act")
        pT_dve = sem("pT_dve")
        mixed = sem("mixed")
        mix_hi = sem("mix_hi")
        mix_lo = sem("mix_lo")
        conv_turned = sem("conv_turned")
        odd_act = sem("odd_act")
        odd_dve = sem("odd_dve")
        oddT_done = sem("oddT_done")
        oddT_act = sem("oddT_act")
        oddT_dve = sem("oddT_dve")
        ret_scored = sem("ret_scored")
        dve_conv = sem("dve_conv")
        ret_decayed = sem("ret_decayed")
        ret_out = sem("ret_out")
        gn_inv = sem("gn_inv")
        gn_std = sem("gn_std")
        yr_done = sem("yr_done")
        yrT_done = sem("yrT_done")
        conv_done = sem("conv_done")
        router_hi_done = sem("router_hi_done")
        router_lo_done = sem("router_lo_done")
        logits_done = sem("logits_done")
        gap_done = sem("gap_done")
        gap_exp = sem("gap_exp")
        chosen_done = sem("chosen_done")
        counted = sem("counted")
        most_done = sem("most_done")
        pick_done = sem("pick_done")
        gathered = sem("gathered")
        gather_hi = sem("gather_hi")
        gather_lo = sem("gather_lo")
        weigh_done = sem("weigh_done")
        weighT_done = sem("weighT_done")
        weighT_out = sem("weighT_out")
        y_act = sem("y_act")
        y_dve = sem("y_dve")
        scattered = sem("scattered")
        last_act = sem("last_act")
        last_dve = sem("last_dve")
        last_scattered = sem("last_scattered")
        moe_added = sem("moe_added")
        final_x = sem("final_x")
        out_ready = sem("out_ready")
        out_stored = sem("out_stored")

        dense = FfnSignals(sem, "dense", NT, gate=(4, 5), up=(6, 7), turned=(6, 7), y=(0, 1, 2, 3))
        moe = FfnSignals(sem, "moe", 1, gate=(2,), up=(3,), turned=(4,), y=(0, 1))
        GATHER_BANKS, WEIGHT_BANK, SCATTER_BANKS = (5, 6), 7, (5, 6, 0, 1)


        def in_w(w, j, u):
            return w.rearrange("(u k p) (j n) -> u j p k n", u=2, p=P, n=IN_CHUNK)[u, j]

        def half_w(w, j, u):
            return w.rearrange("(u k p) (j n) -> u j p k n", u=2, p=P, n=HALF)[u, j]

        uq, ukv = g["even_w_uq"][0], g["even_w_ukv"][0]
        first_units = [in_w(g["even_w_in"][0], j, u) for j in range(3) for u in range(2)]
        first_units += [uq[:, 0:HALF].rearrange("(k p) n -> p k n", p=P),
                        uq[:, HALF:].rearrange("(k p) n -> p k n", p=P),
                        ukv.rearrange("(k p) n -> p k n", p=P)]
        first_units += [half_w(g["even_w_out"][0], j, u) for j in range(2) for u in range(2)]
        odd_units = [half_w(g["odd_w_in"][0], j, u) for j in range(ODD_IN_CHUNKS) for u in range(2)]
        odd_units += [half_w(g["odd_w_out"][0], j, u) for j in range(2) for u in range(2)]
        first_cols = [2 * IN_CHUNK] * (2 * U_IN) + [2 * HALF, HALF, 2 * 256, 256, PIECE, PIECE] + [PIECE] * (2 * U_OUT)
        assert len(first_units) == FFN_UNIT and len(first_cols) == 2 * FFN_UNIT

        def columns(base):
            return first_cols[base] if base < len(first_cols) else PIECE

        ffn_w = {
            "dense": [g[n] for n in ("even_w_gate", "even_w_up", "even_w_down")],
            "moe": [g[n][0] for n in ("odd_we_gate", "odd_we_up", "odd_we_down")],
        }

        def free(sp, base, laps):
            if base >= RING:
                sp.wait_ge(lo_done, laps * (2 * RING) + 2 * (base - RING) + 2)

        def load(sp, base, laps, src, wait):
            if wait:
                free(sp, base, laps)
            dst = raw[:, base % RING, 0:src.shape[-2] * src.shape[-1]].rearrange("p (k n) -> p k n", n=src.shape[-1])
            if len(src.shape) == 5:
                src = src.rearrange("e c p k n -> p (e c k) n")
            sp.dma_start(dst, src).then_inc(raw_landed[base % RING], 16)

        def gate_up_units(kind, e, c):
            out = []
            for w in ffn_w[kind][0:2]:
                v = w.rearrange("e (u k p) (c n) -> e c u p k n", u=2, p=P, n=HALF)
                out += [v[bass.ds(e, 1), bass.ds(c, 1), u] for u in range(2)]
            return out

        def down_units(kind, e, c):
            v = ffn_w[kind][2].rearrange("e (c u k p) n -> e c u p k n", c=FC, u=2, p=P)
            return [v[bass.ds(e, 1), bass.ds(c, 1), u] for u in range(2)]

        def load_all(sp, units, base, laps=0, together=False):
            if together:
                free(sp, base + len(units) - 1, laps)
            order = reversed(range(len(units))) if together else range(len(units))
            for i in order:
                load(sp, base + i, laps, units[i], not together)

        def split_hi(act, base, laps=0):
            n = columns(base)
            unit, second = base // 2, base % 2
            if not second:
                act.wait_ge(raw_landed[unit % RING], laps * 16 + 16 * (unit // RING + 1))
            if base >= RING:
                act.wait_ge(piece_used, laps * CHUNK_PIECES + base - RING + 1)
            off = columns(base - 1) if second else 0
            act.activation(w_hi[:, base % RING, 0:n], raw[:, unit % RING, off:off + n], ACT.Copy).then_inc(hi_done, 1)

        def split_lo(dve, base, laps=0):
            n = columns(base)
            unit, second = base // 2, base % 2
            off = columns(base - 1) if second else 0
            dve.wait_ge(hi_done, laps * CHUNK_PIECES + base + 1)
            dve.tensor_tensor(w_lo[:, base % RING, 0:n], raw[:, unit % RING, off:off + n],
                              w_hi[:, base % RING, 0:n].bitcast(F32), ALU.subtract).then_inc(lo_done, 1)

        def splitter(split, eng):
            at = [0]

            def until(n):
                while at[0] < n:
                    split(eng, at[0])
                    at[0] += 1

            def skip_to(n):
                at[0] = n
            return until, skip_to

        def multiplied(eng, base, laps=0):
            eng.wait_ge(piece_used, laps * CHUNK_PIECES + base + 1)

        def take(pe, base, laps=0):
            pe.wait_ge(lo_done, laps * CHUNK_PIECES + base + 1)
            return w_hi[:, base % RING, :], w_lo[:, base % RING, :]

        def product(pe, acc, a_hi, a_lo, b_hi, b_lo, start, stop):
            pe.matmul(acc, a_hi, b_hi, start=start, stop=False)
            pe.matmul(acc, a_hi, b_lo, start=False, stop=False)
            return pe.matmul(acc, a_lo, b_hi, start=False, stop=stop)

        def weight_product(pe, base, laps, banks, kts, n, left, tiles, first, last, cols=None):
            b_hi, b_lo = take(pe, base, laps)
            for t in range(tiles):
                for i, kt in enumerate(kts):
                    a_hi, a_lo = left(kt, t)
                    mm = product(pe, ps[:, banks[t], 0:n], a_hi, a_lo,
                                 b_hi[:, i * n:(i + 1) * n], b_lo[:, i * n:(i + 1) * n],
                                 start=first and i == 0, stop=last and i == len(kts) - 1)
            mm.then_inc(piece_used, 1)
            return mm

        def tokens(kt, t):
            return tok_hi[:, kt, t * P:(t + 1) * P], tok_lo[:, kt, t * P:(t + 1) * P]

        def turn(pe, bank, col, src, rows=P):
            return pe.transpose(ps[0:rows, bank, col:col + P], src, ident[:, :])

        flat_ps = ps[:, :, :].rearrange("p b n -> p (b n)")

        block = ctx.enter_context(nc.Block())

        @block.sync
        def _(sp):
            for t in range(NT):
                sp.dma_start(x[:, t, :], g["x"][0, t * P:(t + 1) * P, :]).then_inc(x_landed[t], 16)
            load_all(sp, first_units, 0)

            load_all(sp, gate_up_units("dense", 0, 0), FFN_UNIT)
            load_all(sp, gate_up_units("dense", 0, 1), FFN_UNIT + GATE_UNITS)
            load_all(sp, down_units("dense", 0, 0), FFN_UNIT + 2 * GATE_UNITS)
            loop_base = GATE_UNITS + CHUNK_UNITS
            with sp.Fori(LOOP_FIRST, FC) as c:
                load_all(sp, gate_up_units("dense", 0, c), FFN_UNIT + loop_base, c - LOOP_FIRST)
                load_all(sp, down_units("dense", 0, c - 1), FFN_UNIT + loop_base + GATE_UNITS, c - LOOP_FIRST)
            load_all(sp, down_units("dense", 0, FC - 1), FFN_UNIT + PASS_UNITS - DOWN_UNITS)

            load_all(sp, odd_units, ODD_UNIT)

            load_all(sp, gate_up_units("moe", 0, 0), MOE_UNIT)

            def passes(lo, hi):
                with sp.Fori(lo, hi) as p:
                    lap = p * FC
                    e = p if lo == 0 else p - EXPERTS
                    load_all(sp, gate_up_units("moe", e, 1), MOE_UNIT + GATE_UNITS, lap)
                    load_all(sp, down_units("moe", e, 0), MOE_UNIT + 2 * GATE_UNITS, lap, True)
                    with sp.Fori(LOOP_FIRST, FC) as c:
                        load_all(sp, gate_up_units("moe", e, c), MOE_UNIT + loop_base, lap + c - LOOP_FIRST)
                        load_all(sp, down_units("moe", e, c - 1), MOE_UNIT + loop_base + GATE_UNITS, lap + c - LOOP_FIRST)
                    load_all(sp, down_units("moe", e, FC - 1), MOE_UNIT + PASS_UNITS - DOWN_UNITS, lap)
                    nxt = (e + 1) % EXPERTS
                    load_all(sp, gate_up_units("moe", nxt, 0), MOE_UNIT + PASS_UNITS, lap)

            def quiet(n_pass):
                for i in range(RING):
                    last = max(n for n in range(MOE_UNIT + n_pass * PASS_UNITS + GATE_UNITS) if n % RING == i)
                    sp.wait_ge(raw_landed[i], 16 * (last // RING + 1))

            passes(0, EXPERTS)
            quiet(EXPERTS)
            sp.wait_ge(most_done, 1)
            full = sp.value_load(most_i[0:1, 0:1])
            with sp.If(full > SLOTS):
                passes(EXPERTS, 2 * EXPERTS)
                quiet(2 * EXPERTS)
            for t in range(NT):
                sp.wait_ge(out_ready, t + 1)
                sp.dma_start(out[0, t * P:(t + 1) * P, :], xn[:, t, :]).then_inc(out_stored, 16)
            sp.wait_ge(out_stored, 16 * NT)

        @block.gpsimd
        def _(pool):
            step = [0]

            def link(ins):
                step[0] += 1
                ins.then_inc(pool_step, 1)
                pool.wait_ge(pool_step, step[0])

            def load_gain(stage, row):
                if stage:
                    pool.wait_ge(xn_done, NT * stage)
                pool.dma_start(gain[:, :], row.partition_broadcast(P)).then_inc(gain_landed, 16)

            link(pool.memset(ident[:, :], 0.0))
            pool.affine_select(out=ident[:, :], in_=ident[:, :], compare_op=ALU.not_equal, fill=1.0, base=0,
                               pattern=[[-1, P]], channel_multiplier=1).then_inc(ident_done, 1)
            load_gain(0, g["even_norm_mix"][0])
            pool.dma_start(pos_i[:, :], g["positions"][0].rearrange("(t p) -> p t", p=P),
                           allow_slow_non_contiguous=True).then_inc(pos_landed, 16)
            pool.dma_start(lat_gain[:, 0:Q_LORA], g["even_q_norm"][0].partition_broadcast(P)).then_inc(lat_gain_landed, 16)
            pool.dma_start(lat_gain[:, Q_LORA:], g["even_kv_norm"][0].partition_broadcast(P)).then_inc(lat_gain_landed, 16)
            pool.dma_start(sinks, g["even_sinks"][0].partition_broadcast(P)).then_inc(sinks_landed, 16)
            pool.dma_start(conv_rows[:, :], g["odd_conv_w"][0].rearrange("j (k p) -> (j k) p", p=P)).then_inc(conv_landed, 16)
            pool.dma_start(router[:, :, :], g["odd_router"][0].rearrange("(k p) e -> p k e", p=P)).then_inc(router_landed, 16)
            for i in range(ROPE_HALF):
                f = float(np.float32(ROPE_THETA) ** (-np.float32(2 * i) / np.float32(B_ROPE)))
                ins = pool.memset(inv_freq[:, i:i + 1], f)
            ins.then_inc(freq_done, 1)
            link(pool.iota(dist[:, :], pattern=[[-1, SEQ]], base=P, channel_multiplier=1, allow_small_or_imprecise_dtypes=True))
            link(pool.tensor_scalar(rope_tmp[:, 0:SEQ], dist[:, :], 0.0, 2.0, ALU.max, ALU.mult))
            link(pool.tensor_tensor(dist[:, :], rope_tmp[:, 0:SEQ], dist[:, :], ALU.subtract))
            link(pool.memset(dist[0:CHUNK, SEQ - CHUNK:SEQ], MASKED))
            link(pool.memset(dist[CHUNK:P, 0:CHUNK], MASKED))
            for h in range(A_HEADS):
                slope = 2.0 ** (-8.0 * (h + 1) / A_HEADS)
                ins = pool.tensor_scalar(bias[:, (h % 2) * 4 + h // 2, :], dist[:, :], -slope / A_SCALE, None, ALU.mult)
            ins.then_inc(bias_done, 1)
            pool.wait_ge(bias_done, 1)
            link(pool.iota(dist[:, :], pattern=[[1, SEQ]], base=0, channel_multiplier=-1, allow_small_or_imprecise_dtypes=True))
            pool.affine_select(out=dist[:, :], in_=dist[:, :], compare_op=ALU.is_ge, fill=1.0e6, base=0,
                               pattern=[[1, SEQ]], channel_multiplier=-1).then_inc(dist_done, 1)
            load_gain(1, g["even_norm_ffn"][0])

            pool.wait_ge(in_act, 3)
            pool.wait_ge(in_dve, 3)
            pool.wait_ge(trig_done, 2)
            tmp = rope_tmp[:, 0:NT * ROPE_HALF].rearrange("p (t n) -> p t n", t=NT)
            k1, k2 = proj[:, :, COL_KR:COL_KR + ROPE_HALF], proj[:, :, COL_KR + ROPE_HALF:EVEN_IN]
            r1, r2 = kr_rot[:, :, 0:ROPE_HALF], kr_rot[:, :, ROPE_HALF:]
            pool.tensor_tensor(r1, k1, cos, ALU.mult)
            link(pool.tensor_tensor(tmp, k2, sin, ALU.mult))
            link(pool.tensor_tensor(r1, r1, tmp, ALU.subtract))
            pool.tensor_tensor(r2, k2, cos, ALU.mult)
            link(pool.tensor_tensor(tmp, k1, sin, ALU.mult))
            link(pool.tensor_tensor(r2, r2, tmp, ALU.add))
            for t in range(NT):
                pool.tensor_copy(k96[:, t, :, B_NOPE:], kr_rot[:, t, None, :].to_broadcast([P, B_HEADS, B_ROPE]))
            pool.wait_ge(lat_done, 2 * NT)
            pool.dma_start(gn_gain, g["odd_ret_gn"][0].partition_broadcast(P)).then_inc(gn_gain_landed, 16)
            pool.wait_ge(uq_act, 2)
            pool.wait_ge(uq_dve, 2)
            for t in range(NT):
                n = B_HEADS * ROPE_HALF
                a, b = (rope_tmp[:, i * n:(i + 1) * n].rearrange("p (h n) -> p h n", h=B_HEADS) for i in range(2))
                q1 = q96[:, t, :, B_NOPE:B_NOPE + ROPE_HALF]
                q2 = q96[:, t, :, B_NOPE + ROPE_HALF:]
                cs = cos[:, t, None, :].to_broadcast([P, B_HEADS, ROPE_HALF])
                sn = sin[:, t, None, :].to_broadcast([P, B_HEADS, ROPE_HALF])
                pool.tensor_tensor(a, q2, sn, ALU.mult)
                link(pool.tensor_tensor(b, q1, sn, ALU.mult))
                pool.tensor_tensor(q1, q1, cs, ALU.mult)
                link(pool.tensor_tensor(q2, q2, cs, ALU.mult))
                pool.tensor_tensor(q1, q1, a, ALU.subtract)
                ins = pool.tensor_tensor(q2, q2, b, ALU.add)
                if t < NT - 1:
                    link(ins)
            ins.then_inc(rope_done, 1)
            pool.wait_ge(mix_lo, 4)
            link(pool.memset(ones, 1.0))
            pool.affine_select(out=before, in_=ones, compare_op=ALU.is_gt, fill=0.0, base=0,
                               pattern=[[1, P]], channel_multiplier=-1)
            pool.iota(iota8, pattern=[[1, EXPERTS]], base=0, channel_multiplier=0, allow_small_or_imprecise_dtypes=True)
            pool.iota(iota_slot, pattern=[[1, SLOTS]], base=0, channel_multiplier=0,
                      allow_small_or_imprecise_dtypes=True).then_inc(route_consts, 1)
            load_gain(2, g["odd_norm_mix"][0])
            load_gain(3, g["odd_norm_ffn"][0])
            load_gain(4, g["final_norm"])

        @block.tensor
        def _(pe):
            pe.wait_ge(ident_done, 1)

            def norm_turns(stage):
                for t in range(NT):
                    pe.wait_ge(xn_done, NT * stage + t + 1)
                    for half in range(2):
                        for i in range(4):
                            kt = 4 * half + i
                            mm = turn(pe, 2 * t + half, i * P, xn[:, t, kt * P:(kt + 1) * P])
                        mm.then_inc(xnT_done, 1)

            norm_turns(0)
            pe.wait_ge(tok_lo_done, 4)
            in_banks = [(4, 5), (6, 7), (0, 1)]
            for j in range(3):
                for u in range(4):
                    mm = weight_product(pe, 4 * j + u, 0, in_banks[j], (2 * u, 2 * u + 1), IN_CHUNK, tokens, NT,
                                        u == 0, u == 3)

            pe.wait_ge(in_act, 3)
            pe.wait_ge(in_dve, 3)
            for t in range(NT):
                for j in range(4):
                    mm = turn(pe, 2 + t, j * P, proj[:, t, j * P:(j + 1) * P])
                mm.then_inc(qaT_done, 1)
            pe.wait_ge(ka_doubled, 1)
            for t in range(NT):
                for kv in range(A_KV):
                    mm = turn(pe, 4, kv * SEQ + t * P, ka_twice[:, t, kv * P:(kv + 1) * P])
            mm.then_inc(qaT_done, 1)
            pe.wait_ge(lat_done, 2 * NT)
            for t in range(NT):
                for j in range(3):
                    mm = turn(pe, 5 + t, j * P, proj[:, t, COL_CQ + j * P:COL_CQ + (j + 1) * P])
                mm.then_inc(latT_done, 1)
            for t in range(NT):
                for j in range(2):
                    mm = turn(pe, 7, j * SEQ + t * P, proj[:, t, COL_CKV + j * P:COL_CKV + (j + 1) * P])
            mm.then_inc(latT_done, 1)

            def scores_a(t):
                nk = P * (t + 1)
                if t:
                    pe.wait_ge(biased, 1)
                per = HALF // nk
                for h in range(A_HEADS):
                    pos = (h % 2) * 4 + h // 2
                    off = (h % 2) * A_DIM
                    mm = pe.matmul(ps[:, pos // per, (pos % per) * nk:(pos % per + 1) * nk],
                                   qaT[off:off + A_DIM, h // 2, t * P:(t + 1) * P],
                                   kaT[off:off + A_DIM, h // 4, 0:nk], start=True, stop=True)
                mm.then_inc(scored, 1)

            def scores_b(t):
                nk = P * (t + 1)
                per = HALF // nk
                for h in range(B_HEADS):
                    mm = pe.matmul(ps[:, h // per, (h % per) * nk:(h % per + 1) * nk],
                                   qbT[0:B_DIM, h, t * P:(t + 1) * P], kbT[0:B_DIM, h, 0:nk], start=True, stop=True)
                mm.then_inc(scored, 1)

            pt_bank = [0]

            def attend(kind, t, inst):
                nk = P * (t + 1)
                pe.wait_ge(probs_done, inst + 1)
                for b in range(2 * (t + 1)):
                    n = pt_bank[0]
                    if n >= 2:
                        pe.wait_ge(pT_act if n % 2 == 0 else pT_dve, n // 2)
                    for i in range(4):
                        block_no = 4 * b + i
                        mm = turn(pe, 4 + n % 2, i * P, probs_flat[:, block_no * P:(block_no + 1) * P])
                    mm.then_inc(pT_done, 1)
                    pt_bank[0] += 1
                pe.wait_ge(pT_act, pt_bank[0] // 2)
                pe.wait_ge(pT_dve, pt_bank[0] // 2)
                if inst >= 2:
                    pe.wait_ge(mix_lo, inst - 1)
                for h in range(8):
                    pos = (h % 2) * 4 + h // 2 if kind == "A" else h
                    off = (h % 2) * 64
                    for kk in range(t + 1):
                        v = (proj[:, kk, COL_V + (h // 4) * A_DIM:COL_V + (h // 4 + 1) * A_DIM] if kind == "A"
                             else v64[:, kk, h, :])
                        at = (pos * (t + 1) + kk) * P
                        mm = pe.matmul(ps[off:off + 64, 6 + t, (h // 2) * P:(h // 2 + 1) * P], v, pT_flat[:, at:at + P],
                                  start=(kk == 0), stop=(kk == t))
                mm.then_inc(mixed, 1)

            pe.wait_ge(qaT_act, 1)
            pe.wait_ge(qaT_dve, 2)
            scores_a(0)
            pe.wait_ge(latT_lo, 3)

            def latent_q(kt, t):
                return fT_hi[:, kt, t * P:(t + 1) * P], fT_lo[:, kt, t * P:(t + 1) * P]

            def latent_kv(kt, t):
                return latkv_hi[:, kt, t * P:(t + 1) * P], latkv_lo[:, kt, t * P:(t + 1) * P]

            p0 = 2 * U_IN
            weight_product(pe, p0, 0, (2, 3), (0, 1), HALF, latent_q, NT, True, False)
            weight_product(pe, p0 + 1, 0, (2, 3), (2,), HALF, latent_q, NT, False, True)
            weight_product(pe, p0 + 2, 0, (4, 5), (0, 1), 256, latent_q, NT, True, False)
            weight_product(pe, p0 + 3, 0, (4, 5), (2,), 256, latent_q, NT, False, True)
            pe.wait_ge(uq_act, 1)
            pe.wait_ge(uq_dve, 1)
            for i in range(2):
                b_hi, b_lo = take(pe, p0 + 4 + i)
                for t in range(NT):
                    a_hi, a_lo = latent_kv(i, t)
                    for half in range(2):
                        mm = product(pe, ps[:, (6, 7, 2, 3)[2 * t + half], :], a_hi, a_lo,
                                     b_hi[:, half * HALF:(half + 1) * HALF], b_lo[:, half * HALF:(half + 1) * HALF],
                                     start=(i == 0), stop=(i == 1))
                mm.then_inc(piece_used, 1)
            pe.wait_ge(uq_act, 2)
            pe.wait_ge(uq_dve, 2)
            pe.wait_ge(ukv_act, 1)
            pe.wait_ge(ukv_dve, 1)
            scores_a(1)
            attend("A", 0, 0)
            attend("A", 1, 1)
            pe.wait_ge(rope_done, 1)
            pe.wait_ge(biased, 2)
            for i in range(8):
                src = q96 if i < 4 else k96
                t, h0 = (i % 4) // 2, (i % 2) * 4
                bank = i % 4
                if i >= 4:
                    pe.wait_ge(kqT_act if i % 2 == 0 else kqT_dve, (i - 4) // 2 + 1)
                for k in range(4):
                    mm = turn(pe, bank, k * P, src[:, t, h0 + k, :], rows=B_DIM)
                mm.then_inc(kqT_done, 1)
            pe.wait_ge(kqT_act, 4)
            pe.wait_ge(kqT_dve, 4)
            for t in range(NT):
                if t:
                    pe.wait_ge(exp_done, 3)
                scores_b(t)
                attend("B", t, 2 + t)

            def output_projection(stage, base, banks):
                for j in range(2):
                    for u in range(4):
                        mm = weight_product(pe, base + 4 * j + u, 0, banks[2 * j:2 * j + 2], (2 * u, 2 * u + 1), HALF,
                                            tokens, NT, u == 0, u == 3)

            pe.wait_ge(mix_lo, 4)
            output_projection(0, 2 * (U_IN + U_UQ + U_UKV), (0, 1, 2, 3))

            def gate_up(sig, q, base, laps, which):
                tiles = sig.tiles
                banks = sig.gate_banks if which == 0 else sig.up_banks
                for u in range(4):
                    weight_product(pe, base + 4 * which + u, laps, banks, (2 * u, 2 * u + 1), HALF, tokens, tiles,
                                   u == 0, u == 3)

            def turn_hidden(sig, q):
                for t in range(sig.tiles):
                    pe.wait_ge(sig.act_done, q * sig.tiles + t + 1)
                    for i in range(4):
                        mm = turn(pe, sig.turned_banks[t], i * P, hid[:, t, i * P:(i + 1) * P])
                    mm.then_inc(sig.turned, 1)

            def down(sig, q, base, laps, first, last):
                pe.wait_ge(sig.turned_lo, (q + 1) * sig.tiles)
                for kt in range(4):
                    b_hi, b_lo = take(pe, base + kt, laps)
                    for t in range(sig.tiles):
                        a_hi, a_lo = fT_hi[:, kt, t * P:(t + 1) * P], fT_lo[:, kt, t * P:(t + 1) * P]
                        for half in range(2):
                            mm = product(pe, ps[:, sig.y_banks[2 * t + half], :], a_hi, a_lo,
                                         b_hi[:, half * HALF:(half + 1) * HALF],
                                         b_lo[:, half * HALF:(half + 1) * HALF],
                                         start=first and kt == 0, stop=last and kt == 3)
                    mm.then_inc(piece_used, 1)

            def ffn(sig, q, base, lap, between, before_last):
                gate_up(sig, q, base, lap, 0)
                gate_up(sig, q, base, lap, 1)
                between()
                turn_hidden(sig, q)
                at = base + 2 * GATE_UNITS
                gate_up(sig, q + 1, at, lap, 0)
                if sig.tiles == NT:
                    pe.wait_ge(sig.turned_lo, (q + 1) * sig.tiles)
                gate_up(sig, q + 1, at, lap, 1)
                down(sig, q, at + 2 * GATE_UNITS, lap, True, False)
                turn_hidden(sig, q + 1)
                at += CHUNK_PIECES
                with pe.Fori(LOOP_FIRST, FC) as c:
                    laps = lap + c - LOOP_FIRST
                    gate_up(sig, q + c, at, laps, 0)
                    if sig.tiles == NT:
                        pe.wait_ge(sig.turned_lo, (q + c) * sig.tiles)
                    gate_up(sig, q + c, at, laps, 1)
                    down(sig, q + c - 1, at + 2 * GATE_UNITS, laps, False, False)
                    turn_hidden(sig, q + c)
                before_last()
                down(sig, q + FC - 1, base + PASS_PIECES - 2 * DOWN_UNITS, lap, False, True)

            pe.wait_ge(x_updated, 4)
            norm_turns(1)
            pe.wait_ge(tok_lo_done, 8)
            ffn(dense, 0, 2 * FFN_UNIT, 0, lambda: None, lambda: None)

            pe.wait_ge(x_updated, 8)
            norm_turns(2)
            pe.wait_ge(conv_landed, 16)
            pe.transpose(ps[:, 4, 0:CONV_W * 4], conv_rows[:, :], ident[0:CONV_W * 4, 0:CONV_W * 4]).then_inc(conv_turned, 1)
            pe.wait_ge(tok_lo_done, 12)
            pe.wait_ge(dve_conv, 1)
            for j in range(ODD_IN_CHUNKS):
                if j >= 4:
                    pe.wait_ge(odd_act, j - 3)
                    pe.wait_ge(odd_dve, j - 3)
                for u in range(4):
                    weight_product(pe, 2 * ODD_UNIT + 4 * j + u, 0, (2 * (j % 4), 2 * (j % 4) + 1),
                                   (2 * u, 2 * u + 1), HALF, tokens, NT, u == 0, u == 3)
            for i in range(8):
                t = i % 2
                src = (qk_nat[:, 0], qk_nat[:, 1], bc_nat[:, 0], bc_nat[:, 1])[i // 2]
                if t == 0:
                    pe.wait_ge(odd_act, min(4 + i // 2, 6))
                    pe.wait_ge(odd_dve, (4, 5, 6, 7)[i // 2])
                for k in range(4):
                    mm = turn(pe, (6 + i) % 8, k * P, src[:, t, k * P:(k + 1) * P])
                mm.then_inc(oddT_done, 1)
            pe.wait_ge(oddT_act, 4)
            pe.wait_ge(oddT_dve, 4)
            for h in range(C_HEADS):
                mm = pe.matmul(ps[:, 6 + h // 2, (h % 2) * SEQ:(h % 2 + 1) * SEQ], kT[:, h, 0:P], qT[:, h, :],
                               start=True, stop=True)
                if h % 2:
                    mm.then_inc(ret_scored, 1)
            for h in range(C_HEADS):
                mm = pe.matmul(ps[:, 0, h * P:(h + 1) * P], kT[:, h, P:SEQ], qT[:, h, P:SEQ], start=True, stop=True)
            mm.then_inc(ret_scored, 1)
            for t in range(NT):
                pe.wait_ge(ret_decayed, 2 if t == 0 else 3)
                for h in range(C_HEADS):
                    for kk in range(t + 1):
                        left = sT0[:, h, t * P:(t + 1) * P] if kk == 0 else sT1[:, h, :]
                        mm = pe.matmul(ps[:, 1 + t, h * P:(h + 1) * P], left, val[:, kk, h, :],
                                       start=(kk == 0), stop=(kk == t))
                mm.then_inc(ret_out, 1)
            for t in range(NT):
                pe.wait_ge(yr_done, t + 1)
                for k in range(4):
                    mm = turn(pe, 3 + t, k * P, yr[:, t, k * P:(k + 1) * P])
                mm.then_inc(yrT_done, 1)
            pe.wait_ge(mix_lo, 7)
            output_projection(1, 2 * (ODD_UNIT + 2 * ODD_IN_CHUNKS), (5, 6, 7, 0))

            pe.wait_ge(x_updated, 12)
            norm_turns(3)
            pe.wait_ge(tok_lo_done, 16)
            pe.wait_ge(router_lo_done, 1)
            for t in range(NT):
                for kt in range(KD):
                    a_hi, a_lo = tokens(kt, t)
                    mm = product(pe, ps[:, 4, t * EXPERTS:(t + 1) * EXPERTS], a_hi, a_lo, router_hi[:, kt, :],
                                 router_lo[:, kt, :], start=(kt == 0), stop=(kt == KD - 1))
            mm.then_inc(logits_done, 1)
            pe.wait_ge(chosen_done, 1)
            pe.wait_ge(route_consts, 1)
            pe.matmul(ps[:, 5, 0:EXPERTS], before, chosen[:, 0, :], start=True, stop=True)
            pe.matmul(ps[:, 5, EXPERTS:2 * EXPERTS], ones, chosen[:, 0, :], start=True, stop=False)
            pe.matmul(ps[:, 5, EXPERTS:2 * EXPERTS], before, chosen[:, 1, :], start=False, stop=True)
            pe.matmul(ps[:, 5, 2 * EXPERTS:3 * EXPERTS], ones, chosen[:, 0, :], start=True, stop=False)
            pe.matmul(ps[:, 5, 2 * EXPERTS:3 * EXPERTS], ones, chosen[:, 1, :], start=False,
                      stop=True).then_inc(counted, 1)

            def gather(p):
                pe.wait_ge(pick_done, p + 1)
                for kt in range(KD):
                    for t in range(NT):
                        mm = pe.matmul(ps[:, GATHER_BANKS[kt // 4], (kt % 4) * SLOTS:(kt % 4 + 1) * SLOTS],
                                       xn[:, t, kt * P:(kt + 1) * P], pick[:, t, :], start=(t == 0), stop=(t == NT - 1))
                    if kt % 4 == 3:
                        mm.then_inc(gathered, 1)

            def turn_weights(p):
                pe.wait_ge(weigh_done, p + 1)
                for t in range(NT):
                    mm = turn(pe, WEIGHT_BANK, t * P, weigh[:, t, :])
                mm.then_inc(weighT_done, 1)

            def scatter(done):
                for t in range(NT):
                    for half in range(2):
                        pe.matmul(ps[:, SCATTER_BANKS[2 * t + half], :], weigh_T[:, t * P:(t + 1) * P],
                                  y_sb[:, half * HALF:(half + 1) * HALF], start=True, stop=True).then_inc(done, 1)

            def scatter_before(p):
                pe.wait_ge(weighT_out, p)
                pe.wait_ge(y_act, p)
                pe.wait_ge(y_dve, p + 1)
                scatter(scattered)

            def late(p):
                turn_weights(p)
                gather(p + 1)

            def passes(lo, hi):
                with pe.Fori(lo, hi) as p:
                    pe.wait_ge(gather_lo, 2 * p + 2)
                    ffn(moe, p * FC, 2 * MOE_UNIT, p * FC, lambda: scatter_before(p), lambda: late(p))

            gather(0)
            passes(0, EXPERTS)
            pe.wait_ge(most_done, 1)
            full = pe.value_load(most_i[0:1, 0:1])
            with pe.If(full > SLOTS):
                passes(EXPERTS, 2 * EXPERTS)
            pe.wait_ge(last_act, 1)
            pe.wait_ge(last_dve, 1)
            scatter(last_scattered)

        @block.scalar
        def _(act):
            split_until, split_skip = splitter(split_hi, act)

            def norm_start(stage):
                for t in range(NT):
                    if stage == 0:
                        act.wait_ge(x_landed[t], 16)
                    elif t == 0 and stage < 4:
                        act.wait_ge(x_updated, 4 * stage)
                    act.activation(spare[:, t * D:(t + 1) * D], x[:, t, :], ACT.Square, accum_out=sumsq[:, t:t + 1]).then_inc(sumsq_done, 1)

            def norm_root(stage):
                act.wait_ge(inv_done, stage + 1)
                act.activation(rstd, inv, ACT.Sqrt).then_inc(rstd_done, 1)

            def norm_hi(stage):
                for i in range(4):
                    t, half = i // 2, i % 2
                    act.wait_ge(xnT_done, 4 * stage + i + 1)
                    act.activation(tok_hi[:, 4 * half:4 * half + 4, t * P:(t + 1) * P],
                                   ps[:, i, :].rearrange("p (k n) -> p k n", k=4), ACT.Copy).then_inc(tok_hi_done, 1)

            norm_start(0)
            split_until(1)
            norm_root(0)
            split_until(AHEAD)
            act.wait_ge(angle_done, 1)
            act.activation(sin, angle, ACT.Sin).then_inc(trig_done, 1)
            act.activation(cos, turns, ACT.Sin).then_inc(trig_done, 1)
            norm_hi(0)
            in_banks = (4, 6, 0)
            for j in range(3):
                multiplied(act, 4 * j + 3)
                act.activation(proj[:, 0, j * IN_CHUNK:(j + 1) * IN_CHUNK], ps[:, in_banks[j], 0:IN_CHUNK],
                               ACT.Copy).then_inc(in_act, 1)
                split_until(4 * (j + 1) + AHEAD)
            act.wait_ge(in_dve, 3)
            act.wait_ge(in_act, 3)
            for t in range(NT):
                for i, (at, n) in enumerate(((COL_CQ, Q_LORA), (COL_CKV, KV_LORA))):
                    scratch = spare[:, t * D + i * HALF:t * D + i * HALF + n]
                    ins = act.activation(scratch, proj[:, t, at:at + n], ACT.Square,
                                         accum_out=lat_sumsq[:, t, i:i + 1])
            ins.then_inc(lat_sq, 1)
            act.wait_ge(lat_inv, 1)
            act.activation(lat_rstd, lat_rstd, ACT.Sqrt).then_inc(lat_std, 1)
            act.wait_ge(qaT_done, 1)
            act.activation(qaT[:, :, 0:P], ps[:, 2, :].rearrange("p (k n) -> p k n", k=4), ACT.Copy).then_inc(qaT_act, 1)
            for t in range(NT):
                act.wait_ge(latT_done, t + 1)
                act.activation(fT_hi[:, 0:3, t * P:(t + 1) * P], ps[:, 5 + t, 0:3 * P].rearrange("p (k n) -> p k n", k=3),
                               ACT.Copy).then_inc(latT_hi, 1)
            act.wait_ge(latT_done, 3)
            act.activation(latkv_hi, ps[:, 7, :].rearrange("p (k n) -> p k n", k=2), ACT.Copy).then_inc(latT_hi, 1)

            def exps(kind, t, inst):
                nk = P * (t + 1)
                act.wait_ge(max_done, inst + 1)
                scale = A_SCALE if kind == "A" else B_SCALE
                for pos in range(8):
                    src = probs_flat if kind == "A" else flat_ps
                    ins = act.activation(probs_flat[:, pos * nk:(pos + 1) * nk], src[:, pos * nk:(pos + 1) * nk], ACT.Exp,
                                         bias=neg_max[:, pos:pos + 1], scale=scale, accum_out=den[:, pos:pos + 1])
                if kind == "A":
                    act.wait_ge(sink_arg, inst + 1)
                    ins = act.activation(sink_e, sink_e, ACT.Exp)
                ins.then_inc(exp_done, 1)

            pt_bank = [0]

            def probs_out(t):
                for b in range(2 * (t + 1)):
                    if pt_bank[0] % 2 == 0:
                        act.wait_ge(pT_done, pt_bank[0] + 1)
                        act.activation(pT_flat[:, b * HALF:(b + 1) * HALF], ps[:, 4, :], ACT.Copy).then_inc(pT_act, 1)
                    pt_bank[0] += 1

            def mix_out(kind, t, inst):
                act.wait_ge(mixed, inst + 1)
                k0 = 0 if kind == "A" else 4
                act.activation(tok_hi[:, k0:k0 + 4, t * P:(t + 1) * P], ps[:, 6 + t, :].rearrange("p (k n) -> p k n", k=4),
                               ACT.Copy).then_inc(mix_hi, 1)

            exps("A", 0, 0)
            multiplied(act, 2 * U_IN + 1)
            q_flat = q96[:, 0, :, :].rearrange("p h n -> p (h n)")
            act.activation(q_flat[:, 0:HALF], ps[:, 2, :], ACT.Copy).then_inc(uq_act, 1)
            multiplied(act, 2 * U_IN + 3)
            act.activation(q_flat[:, HALF:], ps[:, 4, 0:256], ACT.Copy).then_inc(uq_act, 1)
            split_until(2 * U_IN + 4 + AHEAD)
            multiplied(act, 2 * (U_IN + U_UQ + U_UKV) - 1)
            for half in range(2):
                kv = ps[:, 6 + half, :].rearrange("p (h n) -> p h n", h=4)
                act.activation(k96[:, 0, 4 * half:4 * half + 4, 0:B_NOPE], kv[:, :, 0:B_NOPE], ACT.Copy)
                ins = act.activation(v64[:, 0, 4 * half:4 * half + 4, :], kv[:, :, B_NOPE:], ACT.Copy)
            ins.then_inc(ukv_act, 1)
            split_until(2 * (U_IN + U_UQ + U_UKV) + AHEAD)
            probs_out(0)
            mix_out("A", 0, 0)
            exps("A", 1, 1)
            probs_out(1)
            mix_out("A", 1, 1)
            for i in range(0, 8, 2):
                act.wait_ge(kqT_done, i + 1)
                dst = qbT if i < 4 else kbT
                t = (i % 4) // 2
                act.activation(dst[0:B_DIM, 0:4, t * P:(t + 1) * P],
                               ps[0:B_DIM, i % 4, :].rearrange("p (k n) -> p k n", k=4), ACT.Copy).then_inc(kqT_act, 1)
            for t in range(NT):
                exps("B", t, 2 + t)
                probs_out(t)
                mix_out("B", t, 2 + t)
            split_until(2 * FFN_UNIT + AHEAD)

            act.wait_ge(mix_lo, 4)
            act.wait_ge(dist_done, 1)
            for h in range(C_HEADS):
                log_gamma = math.log(1.0 - 2.0 ** (-5.0 - h))
                ins = act.activation(decay[:, h, :], dist[:, :], ACT.Exp, scale=log_gamma)
            ins.then_inc(decay_exp, 1)

            def chunk(sig, q, base, laps, with_down, before_turn=None):
                n = CHUNK_PIECES if with_down else 2 * GATE_UNITS
                for j in range(n):
                    if j == 3:
                        multiplied(act, base + 3, laps)
                        for t in range(sig.tiles):
                            act.activation(hid[:, t, :], ps[:, sig.gate_banks[t], :], ACT.Silu).then_inc(sig.silu_done, 1)
                    if j == n - 1:
                        if before_turn is not None:
                            before_turn()
                        for t in range(sig.tiles):
                            act.wait_ge(sig.turned, q * sig.tiles + t + 1)
                            act.activation(fT_hi[:, :, t * P:(t + 1) * P],
                                           ps[:, sig.turned_banks[t], :].rearrange("p (k n) -> p k n", k=4),
                                           ACT.Copy).then_inc(sig.turned_hi, 1)
                    split_hi(act, base + j + AHEAD, laps)

            def ffn(sig, q, base, lap, between, before_last):
                chunk(sig, q, base, lap, False, between)
                at = base + 2 * GATE_UNITS
                chunk(sig, q + 1, at, lap, True)
                at += CHUNK_PIECES
                with act.Fori(LOOP_FIRST, FC) as c:
                    chunk(sig, q + c, at, lap + c - LOOP_FIRST, True)
                if before_last is not None:
                    before_last()
                for j in range(2 * DOWN_UNITS):
                    split_hi(act, base + PASS_PIECES - 2 * DOWN_UNITS + j + AHEAD, lap)

            norm_start(1)
            norm_root(1)
            norm_hi(1)
            ffn(dense, 0, 2 * FFN_UNIT, 0, None, None)
            split_skip(2 * ODD_UNIT + AHEAD)

            norm_start(2)
            norm_root(2)
            norm_hi(2)
            for j in range(ODD_IN_CHUNKS):
                multiplied(act, 2 * ODD_UNIT + 4 * j + 3)
                src = ps[:, 2 * (j % 4), :]
                if j < 2:
                    act.activation(qk_nat[:, j, 0, :], src, ACT.Copy).then_inc(odd_act, 1)
                elif j == 2:
                    act.activation(val[:, 0, :, :], src.rearrange("p (h n) -> p h n", h=C_HEADS), ACT.Copy).then_inc(odd_act, 1)
                elif j == 3:
                    act.activation(gate[:, 0, :], src, ACT.Silu)
                    act.activation(gate[:, 1, :], ps[:, 7, :], ACT.Silu).then_inc(odd_act, 1)
                elif j < 6:
                    act.activation(bc_nat[:, j - 4, 0, :], src, ACT.Copy).then_inc(odd_act, 1)
                split_until(2 * ODD_UNIT + 4 * (j + 1) + AHEAD)
            for i in range(0, 8, 2):
                act.wait_ge(oddT_done, i + 1)
                dst = (qT, kT, bT, uT)[i // 2]
                act.activation(dst[:, :, 0:P], ps[:, (6 + i) % 8, :].rearrange("p (k n) -> p k n", k=4),
                               ACT.Copy).then_inc(oddT_act, 1)
            act.wait_ge(gn_inv, 1)
            act.activation(gn_rstd, gn_rstd, ACT.Sqrt).then_inc(gn_std, 1)
            act.wait_ge(conv_done, 1)
            act.activation(tok_hi[:, 4:8, :], conv, ACT.Copy).then_inc(mix_hi, 1)
            for t in range(NT):
                act.wait_ge(yrT_done, t + 1)
                act.activation(tok_hi[:, 0:4, t * P:(t + 1) * P], ps[:, 3 + t, :].rearrange("p (k n) -> p k n", k=4),
                               ACT.Copy).then_inc(mix_hi, 1)
            act.wait_ge(router_landed, 16)
            act.activation(router_hi[:, :, :], router[:, :, :], ACT.Copy).then_inc(router_hi_done, 1)
            split_until(2 * MOE_UNIT + AHEAD)

            norm_start(3)
            norm_root(3)
            norm_hi(3)
            act.wait_ge(gap_done, 1)
            act.activation(gate1, gap, ACT.Exp).then_inc(gap_exp, 1)

            def gather_out(p):
                for i in range(2):
                    act.wait_ge(gathered, 2 * p + i + 1)
                    act.activation(tok_hi[:, 4 * i:4 * i + 4, 0:SLOTS],
                                   ps[:, GATHER_BANKS[i], :].rearrange("p (k n) -> p k n", k=4),
                                   ACT.Copy).then_inc(gather_hi, 1)

            def weights_out(p):
                act.wait_ge(weighT_done, p + 1)
                act.activation(weigh_T, ps[:, WEIGHT_BANK, 0:SEQ], ACT.Copy).then_inc(weighT_out, 1)

            def late(p):
                weights_out(p)
                gather_out(p + 1)

            def passes(lo, hi):
                with act.Fori(lo, hi) as p:
                    ffn(moe, p * FC, 2 * MOE_UNIT, p * FC, None, lambda: late(p))
                    multiplied(act, 2 * MOE_UNIT + PASS_PIECES - 1, p * FC)
                    act.activation(y_sb[:, 0:HALF], ps[:, moe.y_banks[0], :], ACT.Copy).then_inc(y_act, 1)

            gather_out(0)
            passes(0, EXPERTS)
            act.wait_ge(most_done, 1)
            full = act.value_load(most_i[0:1, 0:1])
            with act.If(full > SLOTS):
                passes(EXPERTS, 2 * EXPERTS)
            act.drain().then_inc(last_act, 1)
            act.wait_ge(final_x, 1)
            norm_start(4)
            norm_root(4)

        @block.vector
        def _(dve):
            split_until, split_skip = splitter(split_lo, dve)
            step = [0]

            def link(ins):
                step[0] += 1
                ins.then_inc(dve_step, 1)
                dve.wait_ge(dve_step, step[0])

            def norm_mean(stage):
                dve.wait_ge(sumsq_done, NT * (stage + 1))
                link(dve.tensor_scalar(inv, sumsq, 1.0 / D, EPS, ALU.mult, ALU.add))
                dve.reciprocal(inv, inv).then_inc(inv_done, 1)

            def norm_apply(stage):
                dve.wait_ge(rstd_done, stage + 1)
                dve.wait_ge(gain_landed, 16 * (stage + 1))
                for t in range(NT):
                    dve.scalar_tensor_tensor(out=xn[:, t, :], in0=x[:, t, :], scalar=rstd[:, t:t + 1],
                                             in1=gain[:, :], op0=ALU.mult, op1=ALU.mult)\
                       .then_inc(xn_done if stage < 4 else out_ready, 1)

            def norm_lo(stage):
                for i in range(4):
                    t, half = i // 2, i % 2
                    dst = (slice(None), slice(4 * half, 4 * half + 4), slice(t * P, (t + 1) * P))
                    dve.wait_ge(tok_hi_done, 4 * stage + i + 1)
                    dve.tensor_tensor(tok_lo[dst], ps[:, i, :].rearrange("p (k n) -> p k n", k=4),
                                      tok_hi[dst].bitcast(F32), ALU.subtract).then_inc(tok_lo_done, 1)

            norm_mean(0)
            split_until(1)
            norm_apply(0)
            dve.wait_ge(pos_landed, 16)
            dve.wait_ge(freq_done, 1)
            link(dve.tensor_copy(pos_f, pos_i[:, :]))
            for t in range(NT):
                ins = dve.tensor_scalar(angle[:, t, :], inv_freq, pos_f[:, t:t + 1], None, ALU.mult)
            link(ins)
            link(dve.tensor_scalar(turns, angle, 1.0 / (2.0 * math.pi), None, ALU.mult))
            whole = 1.5 * 2.0 ** 23
            link(dve.tensor_scalar(turns, turns, whole, whole, ALU.add, ALU.subtract))
            two_pi = 2.0 * math.pi
            c1 = 6.28125
            c2 = float(np.float32(np.round((two_pi - c1) * 2.0 ** 21) / 2.0 ** 21))
            c3 = two_pi - c1 - c2
            for c in (c1, c2, c3):
                link(dve.scalar_tensor_tensor(out=angle, in0=turns, scalar=-c, in1=angle, op0=ALU.mult, op1=ALU.add))
            link(dve.tensor_scalar(angle, angle, math.pi, -math.pi, ALU.min, ALU.max))
            link(dve.scalar_tensor_tensor(out=turns, in0=angle, scalar=-1.0, in1=angle, op0=ALU.mult, op1=ALU.max))
            dve.tensor_scalar(turns, turns, -1.0, math.pi / 2.0, ALU.mult, ALU.add).then_inc(angle_done, 1)
            split_until(AHEAD)
            norm_lo(0)
            in_banks = (5, 7, 1)
            for j in range(3):
                multiplied(dve, 4 * j + 3)
                dve.tensor_copy(proj[:, 1, j * IN_CHUNK:(j + 1) * IN_CHUNK], ps[:, in_banks[j], 0:IN_CHUNK])\
                   .then_inc(in_dve, 1)
                split_until(4 * (j + 1) + AHEAD)
            dve.wait_ge(in_act, 3)
            dve.wait_ge(in_dve, 3)
            dve.wait_ge(sumsq_done, 2)
            for t in range(NT):
                dst = ka_twice[:, t, :].rearrange("p (g a n) -> p g a n", g=A_KV, a=2)
                src = proj[:, t, COL_K:COL_V].rearrange("p (g n) -> p g n", g=A_KV)
                for a in range(2):
                    ins = dve.tensor_copy(dst[:, :, a, :], src)
            ins.then_inc(ka_doubled, 1)
            dve.wait_ge(lat_sq, 1)
            for i, n in enumerate((Q_LORA, KV_LORA)):
                ins = dve.tensor_scalar(lat_rstd[:, :, i], lat_sumsq[:, :, i], 1.0 / n, EPS, ALU.mult, ALU.add)
            link(ins)
            dve.reciprocal(lat_rstd, lat_rstd).then_inc(lat_inv, 1)
            dve.wait_ge(lat_std, 1)
            dve.wait_ge(lat_gain_landed, 32)
            for t in range(NT):
                for i, (at, n, go) in enumerate(((COL_CQ, Q_LORA, 0), (COL_CKV, KV_LORA, Q_LORA))):
                    dve.scalar_tensor_tensor(out=proj[:, t, at:at + n], in0=proj[:, t, at:at + n],
                                             scalar=lat_rstd[:, t, i:i + 1], in1=lat_gain[:, go:go + n],
                                             op0=ALU.mult, op1=ALU.mult).then_inc(lat_done, 1)
            dve.wait_ge(qaT_done, 2)
            dve.tensor_copy(qaT[:, :, P:SEQ], ps[:, 3, :].rearrange("p (k n) -> p k n", k=4)).then_inc(qaT_dve, 1)
            dve.wait_ge(qaT_done, 3)
            dve.tensor_copy(kaT, ps[:, 4, :].rearrange("p (k n) -> p k n", k=2)).then_inc(qaT_dve, 1)
            for t in range(NT):
                dve.wait_ge(latT_hi, t + 1)
                dve.tensor_tensor(fT_lo[:, 0:3, t * P:(t + 1) * P], ps[:, 5 + t, 0:3 * P].rearrange("p (k n) -> p k n", k=3),
                                  fT_hi[:, 0:3, t * P:(t + 1) * P].bitcast(F32), ALU.subtract).then_inc(latT_lo, 1)
            dve.wait_ge(latT_hi, 3)
            dve.tensor_tensor(latkv_lo, ps[:, 7, :].rearrange("p (k n) -> p k n", k=2), latkv_hi.bitcast(F32),
                              ALU.subtract).then_inc(latT_lo, 1)
            dve.wait_ge(sinks_landed, 16)
            sinks_pos = sinks.rearrange("p (j a) -> p a j", a=2)
            by_pos = lambda v: v.rearrange("p (a j) -> p a j", a=2)

            def softmax_start(kind, t, inst):
                nk = P * (t + 1)
                dve.wait_ge(scored, inst + 1)
                if kind == "A":
                    if inst == 0:
                        dve.wait_ge(bias_done, 1)
                    else:
                        dve.wait_ge(pT_done, 2)
                    for b in range(2 * (t + 1)):
                        if t == 0:
                            tab = bias[:, 4 * b:4 * b + 4, P:SEQ]
                            s = ps[:, b, :].rearrange("p (h n) -> p h n", h=4)
                            o = probs_flat[:, b * HALF:(b + 1) * HALF].rearrange("p (h n) -> p h n", h=4)
                        else:
                            tab = bias[:, 2 * b:2 * b + 2, :]
                            s = ps[:, b, :].rearrange("p (h n) -> p h n", h=2)
                            o = probs_flat[:, b * HALF:(b + 1) * HALF].rearrange("p (h n) -> p h n", h=2)
                        ins = dve.tensor_tensor(o, s, tab, ALU.add)
                    ins.then_inc(biased, 1)
                    dve.wait_ge(biased, inst + 1)
                    link(dve.tensor_reduce(row_max, probs_flat[:, 0:8 * nk].rearrange("p (h n) -> p h n", h=8), AX.X, ALU.max))
                    link(dve.scalar_tensor_tensor(out=by_pos(row_max), in0=sinks_pos, scalar=1.0 / A_SCALE,
                                                  in1=by_pos(row_max), op0=ALU.mult, op1=ALU.max))
                    dve.tensor_scalar(neg_max, row_max, -A_SCALE, None, ALU.mult).then_inc(max_done, 1)
                    dve.wait_ge(max_done, inst + 1)
                    dve.tensor_tensor(by_pos(sink_e), sinks_pos, by_pos(neg_max), ALU.add).then_inc(sink_arg, 1)
                else:
                    s = flat_ps[:, 0:8 * nk].rearrange("p (h n) -> p h n", h=8)
                    link(dve.memset(s[0:CHUNK, :, nk - CHUNK:nk], -1.0e30))
                    link(dve.tensor_reduce(row_max, s, AX.X, ALU.max))
                    dve.tensor_scalar(neg_max, row_max, -B_SCALE, None, ALU.mult).then_inc(max_done, 1)

            def softmax_end(kind, t, inst):
                nk = P * (t + 1)
                dve.wait_ge(exp_done, inst + 1)
                if kind == "A":
                    link(dve.tensor_tensor(den, den, sink_e, ALU.add))
                link(dve.reciprocal(den, den))
                pr = probs_flat[:, 0:8 * nk].rearrange("p (h n) -> p h n", h=8)
                dve.tensor_tensor(pr, pr, den[:, :, None].to_broadcast([P, 8, nk]), ALU.mult).then_inc(probs_done, 1)

            pt_bank = [0]

            def probs_out(t):
                for b in range(2 * (t + 1)):
                    if pt_bank[0] % 2:
                        dve.wait_ge(pT_done, pt_bank[0] + 1)
                        dve.tensor_copy(pT_flat[:, b * HALF:(b + 1) * HALF], ps[:, 5, :]).then_inc(pT_dve, 1)
                    pt_bank[0] += 1

            def mix_out(kind, t, inst):
                dve.wait_ge(mix_hi, inst + 1)
                k0 = 0 if kind == "A" else 4
                dst = (slice(None), slice(k0, k0 + 4), slice(t * P, (t + 1) * P))
                dve.tensor_tensor(tok_lo[dst], ps[:, 6 + t, :].rearrange("p (k n) -> p k n", k=4),
                                  tok_hi[dst].bitcast(F32), ALU.subtract).then_inc(mix_lo, 1)

            softmax_start("A", 0, 0)
            multiplied(dve, 2 * U_IN + 1)
            q_flat = q96[:, 1, :, :].rearrange("p h n -> p (h n)")
            dve.tensor_copy(q_flat[:, 0:HALF], ps[:, 3, :]).then_inc(uq_dve, 1)
            multiplied(dve, 2 * U_IN + 3)
            dve.tensor_copy(q_flat[:, HALF:], ps[:, 5, 0:256]).then_inc(uq_dve, 1)
            split_until(2 * U_IN + 4 + AHEAD)
            softmax_end("A", 0, 0)
            multiplied(dve, 2 * (U_IN + U_UQ + U_UKV) - 1)
            for half in range(2):
                kv = ps[:, 2 + half, :].rearrange("p (h n) -> p h n", h=4)
                dve.tensor_copy(k96[:, 1, 4 * half:4 * half + 4, 0:B_NOPE], kv[:, :, 0:B_NOPE])
                ins = dve.tensor_copy(v64[:, 1, 4 * half:4 * half + 4, :], kv[:, :, B_NOPE:])
            ins.then_inc(ukv_dve, 1)
            split_until(2 * (U_IN + U_UQ + U_UKV) + AHEAD)
            probs_out(0)
            mix_out("A", 0, 0)
            softmax_start("A", 1, 1)
            softmax_end("A", 1, 1)
            probs_out(1)
            mix_out("A", 1, 1)
            for i in range(1, 8, 2):
                dve.wait_ge(kqT_done, i + 1)
                dst = qbT if i < 4 else kbT
                t = (i % 4) // 2
                dve.tensor_copy(dst[0:B_DIM, 4:8, t * P:(t + 1) * P],
                                ps[0:B_DIM, i % 4, :].rearrange("p (k n) -> p k n", k=4)).then_inc(kqT_dve, 1)
            for t in range(NT):
                softmax_start("B", t, 2 + t)
                softmax_end("B", t, 2 + t)
                probs_out(t)
                mix_out("B", t, 2 + t)

            def residual(base, banks):
                for i in range(4):
                    half, t = i // 2, i % 2
                    multiplied(dve, base + 4 * half + 3)
                    xs = x[:, t, half * HALF:(half + 1) * HALF]
                    dve.tensor_tensor(xs, xs, ps[:, banks[i], :], ALU.add).then_inc(x_updated, 1)
                    if i == 1:
                        split_until(base + 4 + AHEAD)

            base = 2 * (U_IN + U_UQ + U_UKV)
            residual(base, (0, 1, 2, 3))
            split_until(2 * FFN_UNIT + AHEAD)

            def chunk(sig, q, base, laps, with_down, before_turn=None):
                n = CHUNK_PIECES if with_down else 2 * GATE_UNITS
                for j in range(n):
                    if j == 7:
                        multiplied(dve, base + 7, laps)
                        for t in range(sig.tiles):
                            dve.wait_ge(sig.silu_done, q * sig.tiles + t + 1)
                            dve.tensor_tensor(hid[:, t, :], hid[:, t, :], ps[:, sig.up_banks[t], :], ALU.mult)\
                               .then_inc(sig.act_done, 1)
                    if j == n - 1:
                        if before_turn is not None:
                            before_turn()
                        for t in range(sig.tiles):
                            dve.wait_ge(sig.turned_hi, q * sig.tiles + t + 1)
                            dve.tensor_tensor(fT_lo[:, :, t * P:(t + 1) * P],
                                              ps[:, sig.turned_banks[t], :].rearrange("p (k n) -> p k n", k=4),
                                              fT_hi[:, :, t * P:(t + 1) * P].bitcast(F32), ALU.subtract)\
                               .then_inc(sig.turned_lo, 1)
                    split_lo(dve, base + j + AHEAD, laps)

            def ffn(sig, q, base, lap, between, before_last):
                chunk(sig, q, base, lap, False, between)
                at = base + 2 * GATE_UNITS
                chunk(sig, q + 1, at, lap, True)
                at += CHUNK_PIECES
                with dve.Fori(LOOP_FIRST, FC) as c:
                    chunk(sig, q + c, at, lap + c - LOOP_FIRST, True)
                if before_last is not None:
                    before_last()
                for j in range(2 * DOWN_UNITS):
                    split_lo(dve, base + PASS_PIECES - 2 * DOWN_UNITS + j + AHEAD, lap)

            norm_mean(1)
            norm_apply(1)
            norm_lo(1)
            dve.wait_ge(decay_exp, 1)
            dve.tensor_scalar(decay, decay, float(C_DIM) ** -0.5, None, ALU.mult)
            ffn(dense, 0, 2 * FFN_UNIT, 0, None, None)
            multiplied(dve, 2 * ODD_UNIT - 1)
            for i in range(4):
                t, half = i // 2, i % 2
                xs = x[:, t, half * HALF:(half + 1) * HALF]
                dve.tensor_tensor(xs, xs, ps[:, dense.y_banks[i], :], ALU.add).then_inc(x_updated, 1)
            split_skip(2 * ODD_UNIT + AHEAD)

            norm_mean(2)
            norm_apply(2)
            norm_lo(2)
            dve.wait_ge(conv_turned, 1)
            dve.tensor_copy(conv_w, ps[:, 4, 0:CONV_W * 4].rearrange("p (j k) -> p j k", j=CONV_W)).then_inc(dve_conv, 1)
            for j in range(ODD_IN_CHUNKS):
                multiplied(dve, 2 * ODD_UNIT + 4 * j + 3)
                src = ps[:, 2 * (j % 4) + 1, :]
                if j < 2:
                    dve.tensor_copy(qk_nat[:, j, 1, :], src).then_inc(odd_dve, 1)
                elif j == 2:
                    dve.tensor_copy(val[:, 1, :, :], src.rearrange("p (h n) -> p h n", h=C_HEADS)).then_inc(odd_dve, 1)
                elif j == 3:
                    dve.wait_ge(odd_act, 4)
                    dve.wait_ge(gn_gain_landed, 16)
                    dve.tensor_tensor(gate, gate, gn_gain[:, None, :].to_broadcast([P, NT, HALF]), ALU.mult)\
                       .then_inc(odd_dve, 1)
                elif j < 6:
                    dve.tensor_copy(bc_nat[:, j - 4, 1, :], src).then_inc(odd_dve, 1)
                else:
                    dve.wait_ge(odd_act, 6)
                    dve.wait_ge(odd_dve, 6)
                    for t in range(NT):
                        ins = dve.tensor_tensor(bc_nat[:, 1, t, :], bc_nat[:, 1, t, :], ps[:, 4 + t, :], ALU.mult)
                    ins.then_inc(odd_dve, 1)
                split_until(2 * ODD_UNIT + 4 * (j + 1) + AHEAD)
            for i in range(1, 8, 2):
                dve.wait_ge(oddT_done, i + 1)
                dst = (qT, kT, bT, uT)[i // 2]
                dve.tensor_copy(dst[:, :, P:SEQ], ps[:, (6 + i) % 8, :].rearrange("p (k n) -> p k n", k=4))\
                   .then_inc(oddT_dve, 1)
            for i in range(3):
                dve.wait_ge(ret_scored, i + 1)
                if i < 2:
                    dve.tensor_tensor(sT0[:, 2 * i:2 * i + 2, :], ps[:, 6 + i, :].rearrange("p (h n) -> p h n", h=2),
                                      decay[:, 2 * i:2 * i + 2, :], ALU.mult).then_inc(ret_decayed, 1)
                else:
                    dve.tensor_tensor(sT1, ps[:, 0, :].rearrange("p (h n) -> p h n", h=C_HEADS), decay[:, :, 0:P],
                                      ALU.mult).then_inc(ret_decayed, 1)
            dve.wait_ge(oddT_act, 4)
            dve.wait_ge(oddT_dve, 4)
            dve.wait_ge(dve_conv, 1)
            for shift in range(CONV_W):
                for k in range(4):
                    w = conv_w[:, CONV_W - 1 - shift, k:k + 1]
                    if shift == 0:
                        ins = dve.tensor_scalar(conv[:, k, :], uT[:, k, :], w, None, ALU.mult)
                    else:
                        ins = dve.scalar_tensor_tensor(out=conv[:, k, shift:], in0=uT[:, k, 0:SEQ - shift], scalar=w,
                                                       in1=conv[:, k, shift:], op0=ALU.mult, op1=ALU.add)
                link(ins)
            dve.tensor_tensor(conv, conv, bT, ALU.mult).then_inc(conv_done, 1)
            for t in range(NT):
                dve.wait_ge(ret_out, t + 1)
                for h in range(C_HEADS):
                    ins = dve.bn_stats(bn[:, t * C_HEADS + h, :], ps[:, 1 + t, h * P:(h + 1) * P])
            link(ins)
            for i in range(NT * C_HEADS):
                ins = dve.bn_aggr(mv[:, i, :], bn[:, i, :])
            link(ins)
            link(dve.tensor_scalar(gn_rstd, mv[:, :, 1], EPS, None, ALU.add))
            dve.reciprocal(gn_rstd, gn_rstd).then_inc(gn_inv, 1)
            dve.wait_ge(mix_hi, 5)
            dve.wait_ge(conv_done, 1)
            dve.tensor_tensor(tok_lo[:, 4:8, :], conv, tok_hi[:, 4:8, :].bitcast(F32), ALU.subtract).then_inc(mix_lo, 1)
            dve.wait_ge(gn_std, 1)
            dve.wait_ge(odd_dve, 7)
            for t in range(NT):
                for h in range(C_HEADS):
                    i = t * C_HEADS + h
                    ins = dve.tensor_scalar(yr[:, t, h * P:(h + 1) * P], ps[:, 1 + t, h * P:(h + 1) * P], mv[:, i, 0:1],
                                            gn_rstd[:, i:i + 1], ALU.subtract, ALU.mult)
                link(ins)
                dve.tensor_tensor(yr[:, t, :], yr[:, t, :], gate[:, t, :], ALU.mult).then_inc(yr_done, 1)
            for t in range(NT):
                dve.wait_ge(mix_hi, 6 + t)
                dst = (slice(None), slice(0, 4), slice(t * P, (t + 1) * P))
                dve.tensor_tensor(tok_lo[dst], ps[:, 3 + t, :].rearrange("p (k n) -> p k n", k=4),
                                  tok_hi[dst].bitcast(F32), ALU.subtract).then_inc(mix_lo, 1)
            dve.wait_ge(router_hi_done, 1)
            dve.tensor_tensor(router_lo[:, :, :], router[:, :, :], router_hi[:, :, :].bitcast(F32), ALU.subtract)\
               .then_inc(router_lo_done, 1)
            base = 2 * (ODD_UNIT + 2 * ODD_IN_CHUNKS)
            residual(base, (5, 6, 7, 0))
            split_until(2 * MOE_UNIT + AHEAD)

            norm_mean(3)
            norm_apply(3)
            norm_lo(3)
            dve.wait_ge(logits_done, 1)
            dve.wait_ge(route_consts, 1)
            link(dve.tensor_copy(logits, ps[:, 4, 0:NT * EXPERTS].rearrange("p (t e) -> p t e", t=NT)))
            for t in range(NT):
                ins = dve.max(top[:, t, :], logits[:, t, :])
            link(ins)
            for t in range(NT):
                ins = dve.max_index(idx_u[:, t, :], top[:, t, :], logits[:, t, :])
            link(ins)
            dve.tensor_tensor(gap, top[:, :, 1], top[:, :, 0], ALU.subtract).then_inc(gap_done, 1)
            link(dve.tensor_copy(idx_f, idx_u[:, :, 0:2]))
            for t in range(NT):
                dve.tensor_scalar(pick1[:, t, :], iota8, idx_f[:, t, 0:1], None, ALU.is_equal)
                ins = dve.tensor_scalar(pick2[:, t, :], iota8, idx_f[:, t, 1:2], None, ALU.is_equal)
            link(ins)
            dve.tensor_tensor(chosen, pick1, pick2, ALU.add).then_inc(chosen_done, 1)
            dve.wait_ge(gap_exp, 1)
            link(dve.tensor_scalar(gate2, gate1, 1.0, None, ALU.add))
            link(dve.reciprocal(gate2, gate2))
            link(dve.tensor_tensor(gate1, gate1, gate2, ALU.mult))
            for t in range(NT):
                link(dve.tensor_scalar(pick1[:, t, :], pick1[:, t, :], gate2[:, t:t + 1], None, ALU.mult))
                ins = dve.scalar_tensor_tensor(out=share[:, t, 0:EXPERTS], in0=pick2[:, t, :], scalar=gate1[:, t:t + 1],
                                               in1=pick1[:, t, :], op0=ALU.mult, op1=ALU.add)
            link(ins)
            dve.memset(share[:, :, 2 * EXPERTS:], 0.0)
            dve.memset(place[:, :, 2 * EXPERTS:], -1.0)
            link(dve.tensor_copy(share[:, :, EXPERTS:2 * EXPERTS], share[:, :, 0:EXPERTS]))
            dve.wait_ge(counted, 1)
            dve.wait_ge(chosen_done, 1)
            link(dve.scalar_tensor_tensor(out=place1, in0=ps[:, 5, 0:NT * EXPERTS].rearrange("p (t e) -> p t e", t=NT),
                                          scalar=1.0, in1=chosen, op0=ALU.add, op1=ALU.mult))
            for b in range(2):
                dve.tensor_scalar(place[:, :, b * EXPERTS:(b + 1) * EXPERTS], place1, -1.0 - b * SLOTS, None, ALU.add)
            link(dve.tensor_reduce(most, ps[:, 5, NT * EXPERTS:3 * EXPERTS], AX.X, ALU.max))
            dve.tensor_copy(most_i[:, :], most).then_inc(most_done, 1)
            dve.wait_ge(most_done, 1)

            def make_pick(p):
                for t in range(NT):
                    ins = dve.tensor_scalar(pick[:, t, :], iota_slot, place[:, t, bass.ds(p, 1)], None, ALU.is_equal)
                ins.then_inc(pick_done, 1)

            def make_weigh(p):
                for t in range(NT):
                    ins = dve.tensor_scalar(weigh[:, t, :], iota_slot, place[:, t, bass.ds(p, 1)],
                                            share[:, t, bass.ds(p, 1)], ALU.is_equal, ALU.mult)
                ins.then_inc(weigh_done, 1)

            def gather_out(p):
                for i in range(2):
                    dst = (slice(None), slice(4 * i, 4 * i + 4), slice(0, SLOTS))
                    dve.wait_ge(gather_hi, 2 * p + i + 1)
                    dve.tensor_tensor(tok_lo[dst], ps[:, GATHER_BANKS[i], :].rearrange("p (k n) -> p k n", k=4),
                                      tok_hi[dst].bitcast(F32), ALU.subtract).then_inc(gather_lo, 1)

            def add_scattered(done, first):
                for i in range(4):
                    t, half = i // 2, i % 2
                    xs = x[:, t, half * HALF:(half + 1) * HALF]
                    dve.wait_ge(done, first + i + 1)
                    dve.tensor_tensor(xs, xs, ps[:, SCATTER_BANKS[i], :], ALU.add).then_inc(moe_added, 1)

            def passes(lo, hi):
                with dve.Fori(lo, hi) as p:
                    make_weigh(p)
                    make_pick(p + 1)
                    ffn(moe, p * FC, 2 * MOE_UNIT, p * FC, lambda: add_scattered(scattered, 4 * p),
                        lambda: gather_out(p + 1))
                    multiplied(dve, 2 * MOE_UNIT + PASS_PIECES - 1, p * FC)
                    dve.tensor_copy(y_sb[:, HALF:D], ps[:, moe.y_banks[1], :]).then_inc(y_dve, 1)

            make_pick(0)
            dve.memset(weigh_T, 0.0)
            dve.memset(y_sb, 0.0).then_inc(y_dve, 1)
            gather_out(0)
            passes(0, EXPERTS)
            full = dve.value_load(most_i[0:1, 0:1])
            with dve.If(full > SLOTS):
                passes(EXPERTS, 2 * EXPERTS)
            dve.drain().then_inc(last_dve, 1)
            add_scattered(last_scattered, 0)
            dve.drain().then_inc(final_x, 1)
            dve.wait_ge(final_x, 1)
            norm_mean(4)
            norm_apply(4)


_NAMES = ["x", "positions", "even_norm_mix", "even_w_in", "even_sinks", "even_q_norm", "even_w_uq", "even_kv_norm",
          "even_w_ukv", "even_w_out", "even_norm_ffn", "even_w_gate", "even_w_up", "even_w_down", "odd_norm_mix",
          "odd_w_in", "odd_ret_gn", "odd_conv_w", "odd_w_out", "odd_norm_ffn", "odd_router", "odd_we_gate", "odd_we_up",
          "odd_we_down", "final_norm"]


def kernel(**inputs):
    import concourse.bacc as bacc
    from concourse.bass_utils import run_bass_kernel_spmd

    nc = bacc.Bacc("TRN2", target_bir_lowering=False, num_devices=1)
    arrays, aps = {}, {}
    for name in _NAMES:
        a = np.ascontiguousarray(inputs[name])
        arrays[f"in_{name}"] = a
        aps[name] = nc.dram_tensor(f"in_{name}", a.shape, mybir.dt.from_np(a.dtype), kind="ExternalInput").ap()
    out = nc.dram_tensor("out_y", (1, SEQ, D), F32, kind="ExternalOutput").ap()
    build_trunk(nc, aps, out)
    r = run_bass_kernel_spmd(nc, [arrays], core_ids=[0])
    return r.results[0]["out_y"]
```

```python
import math
from contextlib import ExitStack

import numpy as np

import concourse.bass as bass
from concourse import mybir

F32 = mybir.dt.float32
F32R = mybir.dt.float32r
I32 = mybir.dt.int32
U32 = mybir.dt.uint32
ALU = mybir.AluOpType
ACT = mybir.ActivationFunctionType
AX = mybir.AxisListType

P = 128
SEQ = 256
NT = SEQ // P
D = 1024
KD = D // P
CHUNK = 64
EPS = 1e-6
HALF = 512
A_HEADS, A_KV, A_DIM = 8, 2, 64
B_HEADS, B_NOPE, B_ROPE, B_V = 8, 64, 32, 64
B_DIM = B_NOPE + B_ROPE
Q_LORA, KV_LORA = 384, 256
ROPE_HALF = B_ROPE // 2
ROPE_THETA = 10000.0
EVEN_IN = A_HEADS * A_DIM + 2 * A_KV * A_DIM + Q_LORA + KV_LORA + B_ROPE
COL_K = A_HEADS * A_DIM
COL_V = COL_K + A_KV * A_DIM
COL_CQ = COL_V + A_KV * A_DIM
COL_CKV = COL_CQ + Q_LORA
COL_KR = COL_CKV + KV_LORA
IN_CHUNK = EVEN_IN // 3
A_SCALE = float(A_DIM) ** -0.5
B_SCALE = float(B_DIM) ** -0.5
MASKED = 1.0e32
C_HEADS, C_DIM = 4, 128
CONV_W = 3
D_FF = 3584
FC = D_FF // HALF
EXPERTS = 8
SLOTS = 128

RING = 6
AHEAD = 6
UNIT = 2048
PIECE = 1024
GATE_UNITS, DOWN_UNITS = 4, 2
CHUNK_UNITS = GATE_UNITS + DOWN_UNITS
CHUNK_PIECES = 2 * CHUNK_UNITS
PASS_UNITS = FC * CHUNK_UNITS
PASS_PIECES = 2 * PASS_UNITS
U_IN, U_UQ, U_UKV, U_OUT = 6, 2, 1, 4
FFN_UNIT = U_IN + U_UQ + U_UKV + U_OUT
ODD_UNIT = FFN_UNIT + PASS_UNITS
ODD_IN_CHUNKS = 7
MOE_UNIT = ODD_UNIT + 2 * ODD_IN_CHUNKS + U_OUT
assert CHUNK_UNITS == RING and EVEN_IN % 3 == 0
LOOP_FIRST = 2


class FfnSignals:

    def __init__(self, sem, name, tiles, gate, up, turned, y):
        self.tiles = tiles
        self.gate_banks, self.up_banks, self.turned_banks, self.y_banks = gate, up, turned, y
        self.silu_done = sem(f"{name}_silu_done")
        self.act_done = sem(f"{name}_act_done")
        self.turned = sem(f"{name}_turned")
        self.turned_hi = sem(f"{name}_turned_hi")
        self.turned_lo = sem(f"{name}_turned_lo")


def build_trunk(nc, ins, out):
    g = ins
    with ExitStack() as ctx:
        def sb(name, shape, dt=F32):
            return ctx.enter_context(nc.sbuf_tensor(name, shape, dt))

        def sem(name):
            return ctx.enter_context(nc.semaphore(name))

        raw = sb("raw", [P, RING, UNIT])
        w_hi = sb("w_hi", [P, RING, PIECE], F32R)
        w_lo = sb("w_lo", [P, RING, PIECE], F32R)
        x = sb("x", [P, NT, D])
        tok_hi = sb("tok_hi", [P, KD, SEQ], F32R)
        tok_lo = sb("tok_lo", [P, KD, SEQ], F32R)
        fT_hi = sb("fT_hi", [P, 4, SEQ], F32R)
        fT_lo = sb("fT_lo", [P, 4, SEQ], F32R)
        gain = sb("gain", [P, D])
        lat_gain = sb("lat_gain", [P, Q_LORA + KV_LORA])
        gn_gain = lat_gain[:, 0:C_HEADS * C_DIM]
        ident = sb("ident", [P, P])
        xn = sb("xn", [P, NT, D])
        spare = sb("spare", [P, 2 * D])
        hid = spare[:, 0:D].rearrange("p (t n) -> p t n", t=NT)
        y_sb = spare[:, D:2 * D]
        arena = sb("arena", [P, 11648])

        taken = [0]

        def part(shape):
            n = int(np.prod(shape))
            at = taken[0]
            taken[0] += n
            assert taken[0] <= 11648, taken[0]
            v = arena[:, at:at + n]
            if len(shape) == 2:
                v = v.rearrange("p (a b) -> p a b", a=shape[0])
            if len(shape) == 3:
                v = v.rearrange("p (a b c) -> p a b c", a=shape[0], b=shape[1])
            return v

        proj = part([NT, EVEN_IN])
        q96 = part([NT, B_HEADS, B_DIM])
        k96 = part([NT, B_HEADS, B_DIM])
        qaT = part([4, SEQ])
        kaT = part([A_KV, SEQ])
        bias = part([A_HEADS, SEQ])
        kbT = bias
        qbT = part([B_HEADS, SEQ])
        v64 = proj[:, :, 0:B_HEADS * B_V].rearrange("p t (h d) -> p t h d", h=B_HEADS)
        latkv_hi, latkv_lo = tok_hi[:, 4:6, :], tok_lo[:, 4:6, :]
        ka_twice = q96[:, :, :, :].rearrange("p t h n -> p t (h n)")[:, :, 0:2 * A_KV * A_DIM]
        pT_flat = spare[:, :]
        probs_flat = xn[:, :, :].rearrange("p t d -> p (t d)")
        taken[0] = 0
        val = part([NT, C_HEADS, C_DIM])
        gate = part([NT, HALF])
        qT = part([C_HEADS, SEQ])
        kT = part([C_HEADS, SEQ])
        bT = part([4, SEQ])
        uT = part([4, SEQ])
        decay = part([C_HEADS, SEQ])
        sT0 = part([C_HEADS, SEQ])
        sT1 = part([C_HEADS, P])
        conv = part([4, SEQ])
        yr = part([NT, HALF])
        qk_nat = xn[:, :, :].rearrange("p a (t n) -> p a t n", t=NT)
        bc_nat = spare[:, :].rearrange("p (a t n) -> p a t n", a=2, t=NT)
        before = part([P])
        ones = part([P])
        iota_slot = part([SLOTS])
        taken[0] = 0
        pick = part([NT, SLOTS])
        weigh = part([NT, SLOTS])
        weigh_T = part([SEQ])
        logits_T = part([SEQ])[0:EXPERTS, :]
        final_scratch = part([NT, 2, HALF])

        small = sb("small", [P, 704])
        used = [0]

        def bit(shape):
            n = int(np.prod(shape))
            at = used[0]
            used[0] += n
            assert used[0] <= 704, used[0]
            v = small[:, at:at + n]
            if len(shape) == 2:
                v = v.rearrange("p (a b) -> p a b", a=shape[0])
            if len(shape) == 3:
                v = v.rearrange("p (a b c) -> p a b c", a=shape[0], b=shape[1])
            return v

        sumsq = bit([NT, 2])
        inv = bit([NT])
        rstd = bit([NT])
        lat_sumsq = bit([NT, 2])
        lat_rstd = bit([NT, 2])
        angle = bit([NT, ROPE_HALF])
        turns = bit([NT, ROPE_HALF])
        cos = bit([NT, ROPE_HALF])
        sin = bit([NT, ROPE_HALF])
        inv_freq = bit([ROPE_HALF])
        pos_f = bit([NT])
        sinks = bit([A_HEADS])
        row_max = bit([A_HEADS])
        neg_max = bit([A_HEADS])
        den = bit([A_HEADS])
        sink_e = bit([A_HEADS])
        kr_rot = bit([NT, B_ROPE])
        conv_rows = sb("conv_rows", [CONV_W * 4, P])
        conv_w = bit([CONV_W, 4])
        bn = bit([NT * C_HEADS, 6])
        mv = bit([NT * C_HEADS, 2])
        gn_rstd = bit([NT * C_HEADS])
        logits = bit([NT, EXPERTS])
        top = bit([NT, 8])
        idx_f = bit([NT, 2])
        gap = bit([NT])
        gate1 = bit([NT])
        gate2 = bit([NT])
        pick1 = bit([NT, EXPERTS])
        pick2 = bit([NT, EXPERTS])
        chosen = bit([NT, EXPERTS])
        iota8 = bit([EXPERTS])
        place1 = bit([NT, EXPERTS])
        most = bit([1])
        N_PASS = 2 * EXPERTS + 1
        place = bit([NT, N_PASS])
        share = bit([NT, N_PASS])
        pos_i = sb("pos_i", [P, NT], I32)
        idx_u = sb("idx_u", [P, NT, 8], U32)
        most_i = sb("most_i", [P, 1], I32)
        router = sb("router", [P, KD, EXPERTS])
        router_hi = sb("router_hi", [P, KD, EXPERTS], F32R)
        router_lo = sb("router_lo", [P, KD, EXPERTS], F32R)
        dist = sb("dist", [P, SEQ])
        rope_tmp = sb("rope_tmp", [P, SEQ])

        ps = ctx.enter_context(nc.psum_tensor("ps", [P, 8, HALF], F32))

        raw_landed = [sem(f"raw_landed{i}") for i in range(RING)]
        hi_done = sem("hi_done")
        lo_done = sem("lo_done")
        piece_used = sem("piece_used")
        x_landed = [sem(f"x_landed{t}") for t in range(NT)]
        first_gain_landed = sem("first_gain_landed")
        gain_landed = sem("gain_landed")
        lat_gain_landed = sem("lat_gain_landed")
        gn_gain_landed = sem("gn_gain_landed")
        pos_landed = sem("pos_landed")
        sinks_landed = sem("sinks_landed")
        conv_landed = sem("conv_landed")
        router_landed = sem("router_landed")
        pool_step = sem("pool_step")
        dve_step = sem("dve_step")
        act_step = sem("act_step")
        ident_done = sem("ident_done")
        bias_done = sem("bias_done")
        route_consts = sem("route_consts")
        dist_done = sem("dist_done")
        decay_exp = sem("decay_exp")
        freq_done = sem("freq_done")
        angle_done = sem("angle_done")
        trig_done = sem("trig_done")
        tile0_done = sem("tile0_done")
        sumsq_done = sem("sumsq_done")
        inv_done = sem("inv_done")
        rstd_done = sem("rstd_done")
        xn_done = sem("xn_done")
        xnT_done = sem("xnT_done")
        tok_hi_done = sem("tok_hi_done")
        tok_lo_done = sem("tok_lo_done")
        x_updated = sem("x_updated")
        in_act = sem("in_act")
        in_dve = sem("in_dve")
        lat_sq = sem("lat_sq")
        lat_inv = sem("lat_inv")
        lat_std = sem("lat_std")
        lat_done = sem("lat_done")
        latT_done = sem("latT_done")
        latT_hi = sem("latT_hi")
        latT_lo = sem("latT_lo")
        qaT_done = sem("qaT_done")
        qaT_act = sem("qaT_act")
        qaT_dve = sem("qaT_dve")
        ka_doubled = sem("ka_doubled")
        uq_act = sem("uq_act")
        uq_dve = sem("uq_dve")
        ukv_act = sem("ukv_act")
        ukv_dve = sem("ukv_dve")
        kr_done = sem("kr_done")
        rope_done = sem("rope_done")
        kqT_done = sem("kqT_done")
        kqT_act = sem("kqT_act")
        kqT_dve = sem("kqT_dve")
        scored = sem("scored")
        biased = sem("biased")
        max_done = sem("max_done")
        sink_arg = sem("sink_arg")
        exp_done = sem("exp_done")
        probs_done = sem("probs_done")
        pT_done = sem("pT_done")
        pT_act = sem("pT_act")
        pT_dve = sem("pT_dve")
        mixed = sem("mixed")
        mix_hi = sem("mix_hi")
        mix_lo = sem("mix_lo")
        conv_turned = sem("conv_turned")
        odd_act = sem("odd_act")
        odd_dve = sem("odd_dve")
        oddT_done = sem("oddT_done")
        oddT_act = sem("oddT_act")
        oddT_dve = sem("oddT_dve")
        ret_scored = sem("ret_scored")
        dve_conv = sem("dve_conv")
        ret_decayed = sem("ret_decayed")
        ret_out = sem("ret_out")
        gn_inv = sem("gn_inv")
        gn_std = sem("gn_std")
        yr_done = sem("yr_done")
        yrT_done = sem("yrT_done")
        conv_done = sem("conv_done")
        router_hi_done = sem("router_hi_done")
        router_lo_done = sem("router_lo_done")
        logitsT_done = sem("logitsT_done")
        logitsT_out = sem("logitsT_out")
        logits_done = sem("logits_done")
        gap_done = sem("gap_done")
        gap_exp = sem("gap_exp")
        chosen_done = sem("chosen_done")
        counted = sem("counted")
        most_done = sem("most_done")
        pick_done = sem("pick_done")
        gathered = sem("gathered")
        gather_hi = sem("gather_hi")
        gather_lo = sem("gather_lo")
        weigh_done = sem("weigh_done")
        weighT_done = sem("weighT_done")
        weighT_out = sem("weighT_out")
        y_act = sem("y_act")
        y_dve = sem("y_dve")
        scattered = sem("scattered")
        last_act = sem("last_act")
        last_dve = sem("last_dve")
        last_scattered = sem("last_scattered")
        moe_added = sem("moe_added")
        out_ready = sem("out_ready")
        out_stored = sem("out_stored")

        dense = FfnSignals(sem, "dense", NT, gate=(4, 5), up=(6, 7), turned=(6, 7), y=(0, 1, 2, 3))
        moe = FfnSignals(sem, "moe", 1, gate=(2,), up=(3,), turned=(4,), y=(0, 1))
        GATHER_BANKS, WEIGHT_BANK, SCATTER_BANKS = (5, 6), 7, (5, 6, 0, 1)


        def in_w(w, j, u):
            return w.rearrange("(u k p) (j n) -> u j p k n", u=2, p=P, n=IN_CHUNK)[u, j]

        def half_w(w, j, u):
            return w.rearrange("(u k p) (j n) -> u j p k n", u=2, p=P, n=HALF)[u, j]

        uq, ukv = g["even_w_uq"][0], g["even_w_ukv"][0]
        first_units = [in_w(g["even_w_in"][0], j, u) for j in range(3) for u in range(2)]
        first_units += [uq[:, 0:HALF].rearrange("(k p) n -> p k n", p=P),
                        uq[:, HALF:].rearrange("(k p) n -> p k n", p=P),
                        ukv.rearrange("(k p) n -> p k n", p=P)]
        first_units += [half_w(g["even_w_out"][0], j, u) for j in range(2) for u in range(2)]
        odd_units = [half_w(g["odd_w_in"][0], j, u) for j in range(ODD_IN_CHUNKS) for u in range(2)]
        odd_units += [half_w(g["odd_w_out"][0], j, u) for j in range(2) for u in range(2)]
        first_cols = [2 * IN_CHUNK] * (2 * U_IN) + [2 * HALF, HALF, 2 * 256, 256, PIECE, PIECE] + [PIECE] * (2 * U_OUT)
        assert len(first_units) == FFN_UNIT and len(first_cols) == 2 * FFN_UNIT

        def columns(base):
            return first_cols[base] if base < len(first_cols) else PIECE

        ffn_w = {
            "dense": [g[n] for n in ("even_w_gate", "even_w_up", "even_w_down")],
            "moe": [g[n][0] for n in ("odd_we_gate", "odd_we_up", "odd_we_down")],
        }

        def free(sp, base, laps):
            if base >= RING:
                sp.wait_ge(lo_done, laps * (2 * RING) + 2 * (base - RING) + 2)

        def load(sp, base, laps, src, wait):
            if wait:
                free(sp, base, laps)
            dst = raw[:, base % RING, 0:src.shape[-2] * src.shape[-1]].rearrange("p (k n) -> p k n", n=src.shape[-1])
            if len(src.shape) == 5:
                src = src.rearrange("e c p k n -> p (e c k) n")
            sp.dma_start(dst, src).then_inc(raw_landed[base % RING], 16)

        def gate_up_units(kind, e, c):
            out = []
            for w in ffn_w[kind][0:2]:
                v = w.rearrange("e (u k p) (c n) -> e c u p k n", u=2, p=P, n=HALF)
                out += [v[bass.ds(e, 1), bass.ds(c, 1), u] for u in range(2)]
            return out

        def down_units(kind, e, c):
            v = ffn_w[kind][2].rearrange("e (c u k p) n -> e c u p k n", c=FC, u=2, p=P)
            return [v[bass.ds(e, 1), bass.ds(c, 1), u] for u in range(2)]

        def load_all(sp, units, base, laps=0, together=False):
            if together:
                free(sp, base + len(units) - 1, laps)
            order = reversed(range(len(units))) if together else range(len(units))
            for i in order:
                load(sp, base + i, laps, units[i], not together)

        def split_hi(act, base, laps=0):
            n = columns(base)
            unit, second = base // 2, base % 2
            if not second:
                act.wait_ge(raw_landed[unit % RING], laps * 16 + 16 * (unit // RING + 1))
            if base >= RING:
                act.wait_ge(piece_used, laps * CHUNK_PIECES + base - RING + 1)
            off = columns(base - 1) if second else 0
            act.activation(w_hi[:, base % RING, 0:n], raw[:, unit % RING, off:off + n], ACT.Copy).then_inc(hi_done, 1)

        def split_lo(dve, base, laps=0):
            n = columns(base)
            unit, second = base // 2, base % 2
            off = columns(base - 1) if second else 0
            dve.wait_ge(hi_done, laps * CHUNK_PIECES + base + 1)
            dve.tensor_tensor(w_lo[:, base % RING, 0:n], raw[:, unit % RING, off:off + n],
                              w_hi[:, base % RING, 0:n].bitcast(F32), ALU.subtract).then_inc(lo_done, 1)

        def splitter(split, eng):
            at = [0]

            def until(n):
                while at[0] < n:
                    split(eng, at[0])
                    at[0] += 1

            def skip_to(n):
                at[0] = n
            return until, skip_to

        def multiplied(eng, base, laps=0):
            eng.wait_ge(piece_used, laps * CHUNK_PIECES + base + 1)

        def take(pe, base, laps=0):
            pe.wait_ge(lo_done, laps * CHUNK_PIECES + base + 1)
            return w_hi[:, base % RING, :], w_lo[:, base % RING, :]

        def product(pe, acc, a_hi, a_lo, b_hi, b_lo, start, stop):
            pe.matmul(acc, a_hi, b_hi, start=start, stop=False)
            pe.matmul(acc, a_hi, b_lo, start=False, stop=False)
            return pe.matmul(acc, a_lo, b_hi, start=False, stop=stop)

        def weight_product(pe, base, laps, banks, kts, n, left, tiles, first, last, cols=None):
            b_hi, b_lo = take(pe, base, laps)
            for t in range(tiles):
                for i, kt in enumerate(kts):
                    a_hi, a_lo = left(kt, t)
                    mm = product(pe, ps[:, banks[t], 0:n], a_hi, a_lo,
                                 b_hi[:, i * n:(i + 1) * n], b_lo[:, i * n:(i + 1) * n],
                                 start=first and i == 0, stop=last and i == len(kts) - 1)
            mm.then_inc(piece_used, 1)
            return mm

        def tokens(kt, t):
            return tok_hi[:, kt, t * P:(t + 1) * P], tok_lo[:, kt, t * P:(t + 1) * P]

        def turn(pe, bank, col, src, rows=P):
            return pe.transpose(ps[0:rows, bank, col:col + P], src, ident[:, :])

        def norm_order(stage):
            return [(0, 0), (1, 0), (0, 1), (1, 1)] if stage in (1, 3) else [(0, 0), (0, 1), (1, 0), (1, 1)]

        flat_ps = ps[:, :, :].rearrange("p b n -> p (b n)")

        block = ctx.enter_context(nc.Block())

        @block.sync
        def _(sp):
            for t in range(NT):
                sp.dma_start(x[:, t, :], g["x"][0, t * P:(t + 1) * P, :]).then_inc(x_landed[t], 16)
            sp.dma_start(gain[:, :], g["even_norm_mix"][0].partition_broadcast(P)).then_inc(first_gain_landed, 16)
            load_all(sp, first_units, 0)

            load_all(sp, gate_up_units("dense", 0, 0), FFN_UNIT)
            load_all(sp, gate_up_units("dense", 0, 1), FFN_UNIT + GATE_UNITS)
            load_all(sp, down_units("dense", 0, 0), FFN_UNIT + 2 * GATE_UNITS)
            loop_base = GATE_UNITS + CHUNK_UNITS
            with sp.Fori(LOOP_FIRST, FC) as c:
                load_all(sp, gate_up_units("dense", 0, c), FFN_UNIT + loop_base, c - LOOP_FIRST)
                load_all(sp, down_units("dense", 0, c - 1), FFN_UNIT + loop_base + GATE_UNITS, c - LOOP_FIRST)
            load_all(sp, down_units("dense", 0, FC - 1), FFN_UNIT + PASS_UNITS - DOWN_UNITS)

            load_all(sp, odd_units, ODD_UNIT)

            load_all(sp, gate_up_units("moe", 0, 0), MOE_UNIT)

            def passes(lo, hi):
                with sp.Fori(lo, hi) as p:
                    lap = p * FC
                    e = p if lo == 0 else p - EXPERTS
                    load_all(sp, gate_up_units("moe", e, 1), MOE_UNIT + GATE_UNITS, lap)
                    load_all(sp, down_units("moe", e, 0), MOE_UNIT + 2 * GATE_UNITS, lap, True)
                    with sp.Fori(LOOP_FIRST, FC) as c:
                        load_all(sp, gate_up_units("moe", e, c), MOE_UNIT + loop_base, lap + c - LOOP_FIRST)
                        load_all(sp, down_units("moe", e, c - 1), MOE_UNIT + loop_base + GATE_UNITS, lap + c - LOOP_FIRST)
                    load_all(sp, down_units("moe", e, FC - 1), MOE_UNIT + PASS_UNITS - DOWN_UNITS, lap)
                    nxt = (e + 1) % EXPERTS
                    load_all(sp, gate_up_units("moe", nxt, 0), MOE_UNIT + PASS_UNITS, lap)

            def quiet(n_pass):
                for i in range(RING):
                    last = max(n for n in range(MOE_UNIT + n_pass * PASS_UNITS + GATE_UNITS) if n % RING == i)
                    sp.wait_ge(raw_landed[i], 16 * (last // RING + 1))

            passes(0, EXPERTS)
            quiet(EXPERTS)
            sp.wait_ge(most_done, 1)
            full = sp.value_load(most_i[0:1, 0:1])
            with sp.If(full > SLOTS):
                passes(EXPERTS, 2 * EXPERTS)
                quiet(2 * EXPERTS)
            for t in range(NT):
                sp.wait_ge(out_ready, t + 1)
                sp.dma_start(out[0, t * P:(t + 1) * P, :], xn[:, t, :]).then_inc(out_stored, 16)
            sp.wait_ge(out_stored, 16 * NT)

        @block.gpsimd
        def _(pool):
            step = [0]

            def link(ins):
                step[0] += 1
                ins.then_inc(pool_step, 1)
                pool.wait_ge(pool_step, step[0])

            def load_gain(stage, row):
                pool.wait_ge(xn_done, NT * stage)
                pool.dma_start(gain[:, :], row.partition_broadcast(P)).then_inc(gain_landed, 16)

            link(pool.memset(ident[:, :], 0.0))
            pool.affine_select(out=ident[:, :], in_=ident[:, :], compare_op=ALU.not_equal, fill=1.0, base=0,
                               pattern=[[-1, P]], channel_multiplier=1).then_inc(ident_done, 1)
            pool.dma_start(pos_i[:, :], g["positions"][0].rearrange("(t p) -> p t", p=P),
                           allow_slow_non_contiguous=True).then_inc(pos_landed, 16)
            pool.dma_start(lat_gain[:, 0:Q_LORA], g["even_q_norm"][0].partition_broadcast(P)).then_inc(lat_gain_landed, 16)
            pool.dma_start(lat_gain[:, Q_LORA:], g["even_kv_norm"][0].partition_broadcast(P)).then_inc(lat_gain_landed, 16)
            pool.dma_start(sinks, g["even_sinks"][0].partition_broadcast(P)).then_inc(sinks_landed, 16)
            pool.dma_start(conv_rows[:, :], g["odd_conv_w"][0].rearrange("j (k p) -> (j k) p", p=P)).then_inc(conv_landed, 16)
            pool.dma_start(router[:, :, :], g["odd_router"][0].rearrange("(k p) e -> p k e", p=P)).then_inc(router_landed, 16)
            for i in range(ROPE_HALF):
                f = float(np.float32(ROPE_THETA) ** (-np.float32(2 * i) / np.float32(B_ROPE)))
                ins = pool.memset(inv_freq[:, i:i + 1], f)
            ins.then_inc(freq_done, 1)
            link(pool.iota(dist[:, :], pattern=[[-1, SEQ]], base=P, channel_multiplier=1, allow_small_or_imprecise_dtypes=True))
            link(pool.tensor_scalar(rope_tmp[:, 0:SEQ], dist[:, :], 0.0, 2.0, ALU.max, ALU.mult))
            link(pool.tensor_tensor(dist[:, :], rope_tmp[:, 0:SEQ], dist[:, :], ALU.subtract))
            link(pool.memset(dist[0:CHUNK, SEQ - CHUNK:SEQ], MASKED))
            link(pool.memset(dist[CHUNK:P, 0:CHUNK], MASKED))
            for h in range(A_HEADS):
                slope = 2.0 ** (-8.0 * (h + 1) / A_HEADS)
                ins = pool.tensor_scalar(bias[:, (h % 2) * 4 + h // 2, :], dist[:, :], -slope / A_SCALE, None, ALU.mult)
            ins.then_inc(bias_done, 1)
            pool.wait_ge(bias_done, 1)
            link(pool.iota(dist[:, :], pattern=[[1, SEQ]], base=0, channel_multiplier=-1, allow_small_or_imprecise_dtypes=True))
            pool.affine_select(out=dist[:, :], in_=dist[:, :], compare_op=ALU.is_ge, fill=1.0e6, base=0,
                               pattern=[[1, SEQ]], channel_multiplier=-1).then_inc(dist_done, 1)
            load_gain(1, g["even_norm_ffn"][0])

            pool.wait_ge(in_act, 3)
            pool.wait_ge(in_dve, 3)
            pool.wait_ge(trig_done, 2)
            tmp = rope_tmp[:, 0:NT * ROPE_HALF].rearrange("p (t n) -> p t n", t=NT)
            k1, k2 = proj[:, :, COL_KR:COL_KR + ROPE_HALF], proj[:, :, COL_KR + ROPE_HALF:EVEN_IN]
            r1, r2 = kr_rot[:, :, 0:ROPE_HALF], kr_rot[:, :, ROPE_HALF:]
            pool.tensor_tensor(r1, k1, cos, ALU.mult)
            link(pool.tensor_tensor(tmp, k2, sin, ALU.mult))
            link(pool.tensor_tensor(r1, r1, tmp, ALU.subtract))
            pool.tensor_tensor(r2, k2, cos, ALU.mult)
            link(pool.tensor_tensor(tmp, k1, sin, ALU.mult))
            link(pool.tensor_tensor(r2, r2, tmp, ALU.add))
            for t in range(NT):
                pool.tensor_copy(k96[:, t, :, B_NOPE:], kr_rot[:, t, None, :].to_broadcast([P, B_HEADS, B_ROPE]))
            pool.wait_ge(lat_done, 2 * NT)
            pool.dma_start(gn_gain, g["odd_ret_gn"][0].partition_broadcast(P)).then_inc(gn_gain_landed, 16)
            pool.wait_ge(uq_act, 2)
            pool.wait_ge(uq_dve, 2)
            for t in range(NT):
                n = B_HEADS * ROPE_HALF
                a, b = (rope_tmp[:, i * n:(i + 1) * n].rearrange("p (h n) -> p h n", h=B_HEADS) for i in range(2))
                q1 = q96[:, t, :, B_NOPE:B_NOPE + ROPE_HALF]
                q2 = q96[:, t, :, B_NOPE + ROPE_HALF:]
                cs = cos[:, t, None, :].to_broadcast([P, B_HEADS, ROPE_HALF])
                sn = sin[:, t, None, :].to_broadcast([P, B_HEADS, ROPE_HALF])
                pool.tensor_tensor(a, q2, sn, ALU.mult)
                link(pool.tensor_tensor(b, q1, sn, ALU.mult))
                pool.tensor_tensor(q1, q1, cs, ALU.mult)
                link(pool.tensor_tensor(q2, q2, cs, ALU.mult))
                pool.tensor_tensor(q1, q1, a, ALU.subtract)
                ins = pool.tensor_tensor(q2, q2, b, ALU.add)
                if t < NT - 1:
                    link(ins)
            ins.then_inc(rope_done, 1)
            pool.wait_ge(mix_lo, 4)
            link(pool.memset(ones, 1.0))
            pool.affine_select(out=before, in_=ones, compare_op=ALU.is_gt, fill=0.0, base=0,
                               pattern=[[1, P]], channel_multiplier=-1)
            pool.iota(iota8, pattern=[[1, EXPERTS]], base=0, channel_multiplier=0, allow_small_or_imprecise_dtypes=True)
            pool.iota(iota_slot, pattern=[[1, SLOTS]], base=0, channel_multiplier=0,
                      allow_small_or_imprecise_dtypes=True).then_inc(route_consts, 1)
            load_gain(2, g["odd_norm_mix"][0])
            load_gain(3, g["odd_norm_ffn"][0])
            load_gain(4, g["final_norm"])

        @block.tensor
        def _(pe):
            pe.wait_ge(ident_done, 1)

            def norm_turn(stage, t):
                pe.wait_ge(xn_done, NT * stage + t + 1)
                for half in range(2):
                    for i in range(4):
                        kt = 4 * half + i
                        mm = turn(pe, 2 * t + half, i * P, xn[:, t, kt * P:(kt + 1) * P])
                    mm.then_inc(xnT_done, 1)

            def first_product(stage, base, banks, n):
                norm_turn(stage, 0)
                for t in range(NT):
                    for u in range(4):
                        if t == 0 and u == (2 if stage else 0):
                            norm_turn(stage, 1)
                        b_hi, b_lo = take(pe, base + u)
                        if u % 2 == 0:
                            pe.wait_ge(tok_lo_done, 4 * stage + 2 * t + u // 2 + 1)
                        for i in range(2):
                            a_hi, a_lo = tokens(2 * u + i, t)
                            mm = product(pe, ps[:, banks[t], 0:n], a_hi, a_lo, b_hi[:, i * n:(i + 1) * n],
                                         b_lo[:, i * n:(i + 1) * n], start=(u == 0 and i == 0), stop=(u == 3 and i == 1))
                        if t == NT - 1:
                            mm.then_inc(piece_used, 1)

            in_banks = [(4, 5), (6, 7), (0, 1)]
            first_product(0, 0, in_banks[0], IN_CHUNK)
            for j in range(1, 3):
                for u in range(4):
                    mm = weight_product(pe, 4 * j + u, 0, in_banks[j], (2 * u, 2 * u + 1), IN_CHUNK, tokens, NT,
                                        u == 0, u == 3)

            pe.wait_ge(in_act, 3)
            pe.wait_ge(in_dve, 3)
            for t in range(NT):
                for j in range(4):
                    mm = turn(pe, 2 + t, j * P, proj[:, t, j * P:(j + 1) * P])
                mm.then_inc(qaT_done, 1)
            pe.wait_ge(ka_doubled, 1)
            for t in range(NT):
                for kv in range(A_KV):
                    mm = turn(pe, 4, kv * SEQ + t * P, ka_twice[:, t, kv * P:(kv + 1) * P])
            mm.then_inc(qaT_done, 1)
            pe.wait_ge(lat_done, 2 * NT)
            for t in range(NT):
                for j in range(3):
                    mm = turn(pe, 5 + t, j * P, proj[:, t, COL_CQ + j * P:COL_CQ + (j + 1) * P])
                mm.then_inc(latT_done, 1)
            for t in range(NT):
                for j in range(2):
                    mm = turn(pe, 7, j * SEQ + t * P, proj[:, t, COL_CKV + j * P:COL_CKV + (j + 1) * P])
            mm.then_inc(latT_done, 1)

            def scores_a(t):
                nk = P * (t + 1)
                if t:
                    pe.wait_ge(biased, 1)
                per = HALF // nk
                for h in range(A_HEADS):
                    pos = (h % 2) * 4 + h // 2
                    off = (h % 2) * A_DIM
                    mm = pe.matmul(ps[:, pos // per, (pos % per) * nk:(pos % per + 1) * nk],
                                   qaT[off:off + A_DIM, h // 2, t * P:(t + 1) * P],
                                   kaT[off:off + A_DIM, h // 4, 0:nk], start=True, stop=True)
                mm.then_inc(scored, 1)

            def scores_b(t):
                nk = P * (t + 1)
                per = HALF // nk
                for h in range(B_HEADS):
                    mm = pe.matmul(ps[:, h // per, (h % per) * nk:(h % per + 1) * nk],
                                   qbT[0:B_DIM, h, t * P:(t + 1) * P], kbT[0:B_DIM, h, 0:nk], start=True, stop=True)
                mm.then_inc(scored, 1)

            pt_bank = [0]

            def attend(kind, t, inst):
                nk = P * (t + 1)
                pe.wait_ge(probs_done, inst + 1)
                for b in range(2 * (t + 1)):
                    n = pt_bank[0]
                    if n >= 2:
                        pe.wait_ge(pT_act if n % 2 == 0 else pT_dve, n // 2)
                    for i in range(4):
                        block_no = 4 * b + i
                        mm = turn(pe, 4 + n % 2, i * P, probs_flat[:, block_no * P:(block_no + 1) * P])
                    mm.then_inc(pT_done, 1)
                    pt_bank[0] += 1
                pe.wait_ge(pT_act, pt_bank[0] // 2)
                pe.wait_ge(pT_dve, pt_bank[0] // 2)
                if inst >= 2:
                    pe.wait_ge(mix_lo, inst - 1)
                for h in range(8):
                    pos = (h % 2) * 4 + h // 2 if kind == "A" else h
                    off = (h % 2) * 64
                    for kk in range(t + 1):
                        v = (proj[:, kk, COL_V + (h // 4) * A_DIM:COL_V + (h // 4 + 1) * A_DIM] if kind == "A"
                             else v64[:, kk, h, :])
                        at = (pos * (t + 1) + kk) * P
                        mm = pe.matmul(ps[off:off + 64, 6 + t, (h // 2) * P:(h // 2 + 1) * P], v, pT_flat[:, at:at + P],
                                  start=(kk == 0), stop=(kk == t))
                mm.then_inc(mixed, 1)

            pe.wait_ge(qaT_act, 1)
            pe.wait_ge(qaT_dve, 2)
            scores_a(0)
            pe.wait_ge(latT_lo, 3)

            def latent_q(kt, t):
                return fT_hi[:, kt, t * P:(t + 1) * P], fT_lo[:, kt, t * P:(t + 1) * P]

            def latent_kv(kt, t):
                return latkv_hi[:, kt, t * P:(t + 1) * P], latkv_lo[:, kt, t * P:(t + 1) * P]

            p0 = 2 * U_IN
            weight_product(pe, p0, 0, (2, 3), (0, 1), HALF, latent_q, NT, True, False)
            weight_product(pe, p0 + 1, 0, (2, 3), (2,), HALF, latent_q, NT, False, True)
            weight_product(pe, p0 + 2, 0, (4, 5), (0, 1), 256, latent_q, NT, True, False)
            weight_product(pe, p0 + 3, 0, (4, 5), (2,), 256, latent_q, NT, False, True)
            pe.wait_ge(uq_act, 1)
            pe.wait_ge(uq_dve, 1)
            for i in range(2):
                b_hi, b_lo = take(pe, p0 + 4 + i)
                for t in range(NT):
                    a_hi, a_lo = latent_kv(i, t)
                    for half in range(2):
                        mm = product(pe, ps[:, (6, 7, 2, 3)[2 * t + half], :], a_hi, a_lo,
                                     b_hi[:, half * HALF:(half + 1) * HALF], b_lo[:, half * HALF:(half + 1) * HALF],
                                     start=(i == 0), stop=(i == 1))
                mm.then_inc(piece_used, 1)
            pe.wait_ge(uq_act, 2)
            pe.wait_ge(uq_dve, 2)
            pe.wait_ge(ukv_act, 1)
            pe.wait_ge(ukv_dve, 1)
            scores_a(1)
            attend("A", 0, 0)
            attend("A", 1, 1)
            pe.wait_ge(rope_done, 1)
            pe.wait_ge(biased, 2)
            for i in range(8):
                src = q96 if i < 4 else k96
                t, h0 = (i % 4) // 2, (i % 2) * 4
                bank = i % 4
                if i >= 4:
                    pe.wait_ge(kqT_act if i % 2 == 0 else kqT_dve, (i - 4) // 2 + 1)
                for k in range(4):
                    mm = turn(pe, bank, k * P, src[:, t, h0 + k, :], rows=B_DIM)
                mm.then_inc(kqT_done, 1)
            pe.wait_ge(kqT_act, 4)
            pe.wait_ge(kqT_dve, 4)
            for t in range(NT):
                if t:
                    pe.wait_ge(exp_done, 3)
                scores_b(t)
                attend("B", t, 2 + t)

            def output_projection(base, banks):
                for u in range(4):
                    weight_product(pe, base + u, 0, banks[0:2], (2 * u, 2 * u + 1), HALF, tokens, NT, u == 0, u == 3)
                for t in range(NT):
                    for u in range(4):
                        b_hi, b_lo = take(pe, base + 4 + u)
                        for i in range(2):
                            a_hi, a_lo = tokens(2 * u + i, t)
                            mm = product(pe, ps[:, banks[2 + t], :], a_hi, a_lo, b_hi[:, i * HALF:(i + 1) * HALF],
                                         b_lo[:, i * HALF:(i + 1) * HALF], start=(u == 0 and i == 0),
                                         stop=(u == 3 and i == 1))
                        if t == NT - 1:
                            mm.then_inc(piece_used, 1)
                    if t == 0:
                        mm.then_inc(tile0_done, 1)

            pe.wait_ge(mix_lo, 4)
            output_projection(2 * (U_IN + U_UQ + U_UKV), (0, 1, 2, 3))

            def gate_up(sig, q, base, laps, which):
                tiles = sig.tiles
                banks = sig.gate_banks if which == 0 else sig.up_banks
                for u in range(4):
                    weight_product(pe, base + 4 * which + u, laps, banks, (2 * u, 2 * u + 1), HALF, tokens, tiles,
                                   u == 0, u == 3)

            def turn_hidden(sig, q):
                for t in range(sig.tiles):
                    pe.wait_ge(sig.act_done, q * sig.tiles + t + 1)
                    for i in range(4):
                        mm = turn(pe, sig.turned_banks[t], i * P, hid[:, t, i * P:(i + 1) * P])
                    mm.then_inc(sig.turned, 1)

            def down(sig, q, base, laps, first, last):
                pe.wait_ge(sig.turned_lo, (q + 1) * sig.tiles)
                for kt in range(4):
                    b_hi, b_lo = take(pe, base + kt, laps)
                    for t in range(sig.tiles):
                        a_hi, a_lo = fT_hi[:, kt, t * P:(t + 1) * P], fT_lo[:, kt, t * P:(t + 1) * P]
                        for half in range(2):
                            mm = product(pe, ps[:, sig.y_banks[2 * t + half], :], a_hi, a_lo,
                                         b_hi[:, half * HALF:(half + 1) * HALF],
                                         b_lo[:, half * HALF:(half + 1) * HALF],
                                         start=first and kt == 0, stop=last and kt == 3)
                    mm.then_inc(piece_used, 1)

            def ffn(sig, q, base, lap, between, before_last):
                if sig.tiles == 1:
                    gate_up(sig, q, base, lap, 0)
                gate_up(sig, q, base, lap, 1)
                between()
                turn_hidden(sig, q)
                at = base + 2 * GATE_UNITS
                gate_up(sig, q + 1, at, lap, 0)
                if sig.tiles == NT:
                    pe.wait_ge(sig.turned_lo, (q + 1) * sig.tiles)
                gate_up(sig, q + 1, at, lap, 1)
                down(sig, q, at + 2 * GATE_UNITS, lap, True, False)
                turn_hidden(sig, q + 1)
                at += CHUNK_PIECES
                with pe.Fori(LOOP_FIRST, FC) as c:
                    laps = lap + c - LOOP_FIRST
                    gate_up(sig, q + c, at, laps, 0)
                    if sig.tiles == NT:
                        pe.wait_ge(sig.turned_lo, (q + c) * sig.tiles)
                    gate_up(sig, q + c, at, laps, 1)
                    down(sig, q + c - 1, at + 2 * GATE_UNITS, laps, False, False)
                    turn_hidden(sig, q + c)
                before_last()
                at = base + PASS_PIECES - 2 * DOWN_UNITS
                if sig.tiles == 1:
                    down(sig, q + FC - 1, at, lap, False, True)
                    return
                pe.wait_ge(sig.turned_lo, (q + FC) * NT)
                for t in range(NT):
                    for kt in range(4):
                        b_hi, b_lo = take(pe, at + kt, lap)
                        a_hi, a_lo = fT_hi[:, kt, t * P:(t + 1) * P], fT_lo[:, kt, t * P:(t + 1) * P]
                        for half in range(2):
                            mm = product(pe, ps[:, sig.y_banks[2 * t + half], :], a_hi, a_lo,
                                         b_hi[:, half * HALF:(half + 1) * HALF],
                                         b_lo[:, half * HALF:(half + 1) * HALF], start=False, stop=kt == 3)
                        if t == NT - 1:
                            mm.then_inc(piece_used, 1)
                    if t == 0:
                        mm.then_inc(tile0_done, 1)

            first_product(1, 2 * FFN_UNIT, dense.gate_banks, HALF)
            ffn(dense, 0, 2 * FFN_UNIT, 0, lambda: None, lambda: None)

            odd_banks = [(4, 5), (6, 7), (0, 1), (2, 3), (4, 5), (6, 7), (0, 1)]
            first_product(2, 2 * ODD_UNIT, odd_banks[0], HALF)
            pe.wait_ge(conv_landed, 16)
            pe.transpose(ps[:, 6, 0:CONV_W * 4], conv_rows[:, :], ident[0:CONV_W * 4, 0:CONV_W * 4]).then_inc(conv_turned, 1)
            pe.wait_ge(dve_conv, 1)
            for j in range(1, ODD_IN_CHUNKS):
                if j >= 4:
                    pe.wait_ge(odd_act, j - 3)
                    pe.wait_ge(odd_dve, j - 3)
                for u in range(4):
                    weight_product(pe, 2 * ODD_UNIT + 4 * j + u, 0, odd_banks[j],
                                   (2 * u, 2 * u + 1), HALF, tokens, NT, u == 0, u == 3)
            for i in range(8):
                t = i % 2
                src = (qk_nat[:, 0], qk_nat[:, 1], bc_nat[:, 0], bc_nat[:, 1])[i // 2]
                if t == 0:
                    pe.wait_ge(odd_act, min(4 + i // 2, 6))
                    pe.wait_ge(odd_dve, (4, 5, 6, 7)[i // 2])
                for k in range(4):
                    mm = turn(pe, (2 + i) % 8, k * P, src[:, t, k * P:(k + 1) * P])
                mm.then_inc(oddT_done, 1)
            pe.wait_ge(oddT_act, 4)
            pe.wait_ge(oddT_dve, 4)
            for h in range(C_HEADS):
                mm = pe.matmul(ps[:, 2 + h // 2, (h % 2) * SEQ:(h % 2 + 1) * SEQ], kT[:, h, 0:P], qT[:, h, :],
                               start=True, stop=True)
                if h % 2:
                    mm.then_inc(ret_scored, 1)
            for h in range(C_HEADS):
                mm = pe.matmul(ps[:, 4, h * P:(h + 1) * P], kT[:, h, P:SEQ], qT[:, h, P:SEQ], start=True, stop=True)
            mm.then_inc(ret_scored, 1)
            for t in range(NT):
                pe.wait_ge(ret_decayed, 2 if t == 0 else 3)
                for h in range(C_HEADS):
                    for kk in range(t + 1):
                        left = sT0[:, h, t * P:(t + 1) * P] if kk == 0 else sT1[:, h, :]
                        mm = pe.matmul(ps[:, 5 + t, h * P:(h + 1) * P], left, val[:, kk, h, :],
                                       start=(kk == 0), stop=(kk == t))
                mm.then_inc(ret_out, 1)
            for t in range(NT):
                pe.wait_ge(yr_done, t + 1)
                for k in range(4):
                    mm = turn(pe, (7, 0)[t], k * P, yr[:, t, k * P:(k + 1) * P])
                mm.then_inc(yrT_done, 1)
            pe.wait_ge(mix_lo, 7)
            output_projection(2 * (ODD_UNIT + 2 * ODD_IN_CHUNKS), (1, 2, 3, 6))

            for t in range(NT):
                norm_turn(3, t)
            pe.wait_ge(router_lo_done, 1)
            for kt in range(KD):
                if kt % 4 == 0:
                    pe.wait_ge(tok_lo_done, 12 + 3 + kt // 4)
                mm = product(pe, ps[0:EXPERTS, 4, 0:SEQ], router_hi[:, kt, :], router_lo[:, kt, :], tok_hi[:, kt, :],
                             tok_lo[:, kt, :], start=(kt == 0), stop=(kt == KD - 1))
            mm.then_inc(logitsT_done, 1)
            pe.wait_ge(logitsT_out, 1)
            for t in range(NT):
                mm = pe.transpose(ps[:, 5, t * EXPERTS:(t + 1) * EXPERTS], logits_T[:, t * P:(t + 1) * P],
                                  ident[0:EXPERTS, 0:EXPERTS])
            mm.then_inc(logits_done, 1)
            pe.wait_ge(chosen_done, 1)
            pe.wait_ge(route_consts, 1)
            pe.matmul(ps[:, 7, 0:EXPERTS], before, chosen[:, 0, :], start=True, stop=True)
            pe.matmul(ps[:, 7, EXPERTS:2 * EXPERTS], ones, chosen[:, 0, :], start=True, stop=False)
            pe.matmul(ps[:, 7, EXPERTS:2 * EXPERTS], before, chosen[:, 1, :], start=False, stop=True)
            pe.matmul(ps[:, 7, 2 * EXPERTS:3 * EXPERTS], ones, chosen[:, 0, :], start=True, stop=False)
            pe.matmul(ps[:, 7, 2 * EXPERTS:3 * EXPERTS], ones, chosen[:, 1, :], start=False,
                      stop=True).then_inc(counted, 1)

            def gather(p):
                pe.wait_ge(pick_done, p + 1)
                for kt in range(KD):
                    for t in range(NT):
                        mm = pe.matmul(ps[:, GATHER_BANKS[kt // 4], (kt % 4) * SLOTS:(kt % 4 + 1) * SLOTS],
                                       xn[:, t, kt * P:(kt + 1) * P], pick[:, t, :], start=(t == 0), stop=(t == NT - 1))
                    if kt % 4 == 3:
                        mm.then_inc(gathered, 1)

            def turn_weights(p):
                pe.wait_ge(weigh_done, p + 1)
                for t in range(NT):
                    mm = turn(pe, WEIGHT_BANK, t * P, weigh[:, t, :])
                mm.then_inc(weighT_done, 1)

            def scatter(done):
                for t in range(NT):
                    for half in range(2):
                        pe.matmul(ps[:, SCATTER_BANKS[2 * t + half], :], weigh_T[:, t * P:(t + 1) * P],
                                  y_sb[:, half * HALF:(half + 1) * HALF], start=True, stop=True).then_inc(done, 1)

            def scatter_before(p):
                pe.wait_ge(weighT_out, p + 1)
                pe.wait_ge(y_act, p + 1)
                pe.wait_ge(y_dve, p + 1)
                scatter(scattered)

            def late(p):
                turn_weights(p)
                gather(p + 1)

            def passes(lo, hi):
                with pe.Fori(lo, hi) as p:
                    pe.wait_ge(gather_lo, 2 * p + 2)
                    ffn(moe, p * FC, 2 * MOE_UNIT, p * FC, lambda: scatter_before(p), lambda: late(p))

            gather(0)
            passes(0, EXPERTS)
            pe.wait_ge(most_done, 1)
            full = pe.value_load(most_i[0:1, 0:1])
            with pe.If(full > SLOTS):
                passes(EXPERTS, 2 * EXPERTS)
            pe.wait_ge(last_act, 1)
            pe.wait_ge(last_dve, 1)
            scatter(last_scattered)

        @block.scalar
        def _(act):
            split_until, split_skip = splitter(split_hi, act)

            def square(stage, t, half):
                if stage == 0:
                    act.wait_ge(x_landed[t], 16)
                else:
                    act.wait_ge(x_updated, 4 * (stage - 1) + norm_order(stage).index((t, half)) + 1)
                at = (2 * t + half) * HALF
                scratch = spare[:, at:at + HALF] if stage < 4 else final_scratch[:, t, half, :]
                act.activation(scratch, x[:, t, half * HALF:(half + 1) * HALF], ACT.Square,
                               accum_out=sumsq[:, t, half:half + 1]).then_inc(sumsq_done, 1)

            def norm_root(stage, t):
                act.wait_ge(inv_done, NT * stage + t + 1)
                act.activation(rstd[:, t:t + 1], inv[:, t:t + 1], ACT.Sqrt, scale=float(D)).then_inc(rstd_done, 1)

            def norm_hi(stage, t):
                for half in range(2):
                    act.wait_ge(xnT_done, 4 * stage + 2 * t + half + 1)
                    act.activation(tok_hi[:, 4 * half:4 * half + 4, t * P:(t + 1) * P],
                                   ps[:, 2 * t + half, :].rearrange("p (k n) -> p k n", k=4), ACT.Copy).then_inc(tok_hi_done, 1)

            def norm(stage, base):
                squares = norm_order(stage)
                first = squares.index((0, 1)) + 1
                for t, half in squares[0:first]:
                    square(stage, t, half)
                norm_root(stage, 0)
                split_until(base + 4)
                norm_hi(stage, 0)
                for t, half in squares[first:]:
                    square(stage, t, half)
                norm_root(stage, 1)
                split_until(base + 5)
                norm_hi(stage, 1)
                split_until(base + AHEAD)

            for t in range(NT):
                square(0, t, 0)
                square(0, t, 1)
                norm_root(0, t)
            for t in range(NT):
                split_until(1 + t)
                norm_hi(0, t)
            split_until(AHEAD)
            act.wait_ge(angle_done, 1)
            act.activation(sin, angle, ACT.Sin).then_inc(trig_done, 1)
            act.activation(cos, turns, ACT.Sin).then_inc(trig_done, 1)
            in_banks = (4, 6, 0)
            for j in range(3):
                multiplied(act, 4 * j + 3)
                act.activation(proj[:, 0, j * IN_CHUNK:(j + 1) * IN_CHUNK], ps[:, in_banks[j], 0:IN_CHUNK],
                               ACT.Copy).then_inc(in_act, 1)
                split_until(4 * (j + 1) + AHEAD)
            act.wait_ge(in_dve, 3)
            act.wait_ge(in_act, 3)
            for t in range(NT):
                for i, (at, n) in enumerate(((COL_CQ, Q_LORA), (COL_CKV, KV_LORA))):
                    scratch = spare[:, t * D + i * HALF:t * D + i * HALF + n]
                    ins = act.activation(scratch, proj[:, t, at:at + n], ACT.Square,
                                         accum_out=lat_sumsq[:, t, i:i + 1])
            ins.then_inc(lat_sq, 1)
            act.wait_ge(lat_inv, 1)
            act.activation(lat_rstd, lat_rstd, ACT.Sqrt).then_inc(lat_std, 1)
            act.wait_ge(qaT_done, 1)
            act.activation(qaT[:, :, 0:P], ps[:, 2, :].rearrange("p (k n) -> p k n", k=4), ACT.Copy).then_inc(qaT_act, 1)
            for t in range(NT):
                act.wait_ge(latT_done, t + 1)
                act.activation(fT_hi[:, 0:3, t * P:(t + 1) * P], ps[:, 5 + t, 0:3 * P].rearrange("p (k n) -> p k n", k=3),
                               ACT.Copy).then_inc(latT_hi, 1)
            act.wait_ge(latT_done, 3)
            act.activation(latkv_hi, ps[:, 7, :].rearrange("p (k n) -> p k n", k=2), ACT.Copy).then_inc(latT_hi, 1)

            def exps(kind, t, inst):
                nk = P * (t + 1)
                act.wait_ge(max_done, inst + 1)
                scale = A_SCALE if kind == "A" else B_SCALE
                for pos in range(8):
                    src = probs_flat if kind == "A" else flat_ps
                    ins = act.activation(probs_flat[:, pos * nk:(pos + 1) * nk], src[:, pos * nk:(pos + 1) * nk], ACT.Exp,
                                         bias=neg_max[:, pos:pos + 1], scale=scale, accum_out=den[:, pos:pos + 1])
                if kind == "A":
                    act.wait_ge(sink_arg, inst + 1)
                    ins = act.activation(sink_e, sink_e, ACT.Exp)
                ins.then_inc(exp_done, 1)

            pt_bank = [0]

            def probs_out(t):
                for b in range(2 * (t + 1)):
                    if pt_bank[0] % 2 == 0:
                        act.wait_ge(pT_done, pt_bank[0] + 1)
                        act.activation(pT_flat[:, b * HALF:(b + 1) * HALF], ps[:, 4, :], ACT.Copy).then_inc(pT_act, 1)
                    pt_bank[0] += 1

            def mix_out(kind, t, inst):
                act.wait_ge(mixed, inst + 1)
                k0 = 0 if kind == "A" else 4
                act.activation(tok_hi[:, k0:k0 + 4, t * P:(t + 1) * P], ps[:, 6 + t, :].rearrange("p (k n) -> p k n", k=4),
                               ACT.Copy).then_inc(mix_hi, 1)

            exps("A", 0, 0)
            multiplied(act, 2 * U_IN + 1)
            q_flat = q96[:, 0, :, :].rearrange("p h n -> p (h n)")
            act.activation(q_flat[:, 0:HALF], ps[:, 2, :], ACT.Copy).then_inc(uq_act, 1)
            multiplied(act, 2 * U_IN + 3)
            act.activation(q_flat[:, HALF:], ps[:, 4, 0:256], ACT.Copy).then_inc(uq_act, 1)
            split_until(2 * U_IN + 4 + AHEAD)
            multiplied(act, 2 * (U_IN + U_UQ + U_UKV) - 1)
            for half in range(2):
                kv = ps[:, 6 + half, :].rearrange("p (h n) -> p h n", h=4)
                act.activation(k96[:, 0, 4 * half:4 * half + 4, 0:B_NOPE], kv[:, :, 0:B_NOPE], ACT.Copy)
                ins = act.activation(v64[:, 0, 4 * half:4 * half + 4, :], kv[:, :, B_NOPE:], ACT.Copy)
            ins.then_inc(ukv_act, 1)
            split_until(2 * (U_IN + U_UQ + U_UKV) + AHEAD)
            probs_out(0)
            mix_out("A", 0, 0)
            exps("A", 1, 1)
            probs_out(1)
            mix_out("A", 1, 1)
            for i in range(0, 8, 2):
                act.wait_ge(kqT_done, i + 1)
                dst = qbT if i < 4 else kbT
                t = (i % 4) // 2
                act.activation(dst[0:B_DIM, 0:4, t * P:(t + 1) * P],
                               ps[0:B_DIM, i % 4, :].rearrange("p (k n) -> p k n", k=4), ACT.Copy).then_inc(kqT_act, 1)
            for t in range(NT):
                exps("B", t, 2 + t)
                probs_out(t)
                mix_out("B", t, 2 + t)
            act.wait_ge(mix_lo, 4)
            act.wait_ge(dist_done, 1)
            for h in range(C_HEADS):
                log_gamma = math.log(1.0 - 2.0 ** (-5.0 - h))
                ins = act.activation(decay[:, h, :], dist[:, :], ACT.Exp, scale=log_gamma)
            ins.then_inc(decay_exp, 1)
            split_until(2 * (U_IN + U_UQ + U_UKV) + 4 + AHEAD)

            def chunk(sig, q, base, laps, with_down, before_turn=None):
                n = CHUNK_PIECES if with_down else 2 * GATE_UNITS
                for j in range(n):
                    if j == 3:
                        multiplied(act, base + 3, laps)
                        for t in range(sig.tiles):
                            act.activation(hid[:, t, :], ps[:, sig.gate_banks[t], :], ACT.Silu).then_inc(sig.silu_done, 1)
                    if j == n - 1:
                        if before_turn is not None:
                            before_turn()
                        for t in range(sig.tiles):
                            act.wait_ge(sig.turned, q * sig.tiles + t + 1)
                            act.activation(fT_hi[:, :, t * P:(t + 1) * P],
                                           ps[:, sig.turned_banks[t], :].rearrange("p (k n) -> p k n", k=4),
                                           ACT.Copy).then_inc(sig.turned_hi, 1)
                    split_hi(act, base + j + AHEAD, laps)

            def ffn(sig, q, base, lap, between, before_last):
                chunk(sig, q, base, lap, False, between)
                at = base + 2 * GATE_UNITS
                chunk(sig, q + 1, at, lap, True)
                at += CHUNK_PIECES
                with act.Fori(LOOP_FIRST, FC) as c:
                    chunk(sig, q + c, at, lap + c - LOOP_FIRST, True)
                if sig.tiles == NT:
                    return
                before_last()
                for j in range(2 * DOWN_UNITS):
                    split_hi(act, base + PASS_PIECES - 2 * DOWN_UNITS + j + AHEAD, lap)

            norm(1, 2 * FFN_UNIT)
            ffn(dense, 0, 2 * FFN_UNIT, 0, None, None)
            split_skip(2 * ODD_UNIT + 2)

            norm(2, 2 * ODD_UNIT)
            for j in range(ODD_IN_CHUNKS):
                multiplied(act, 2 * ODD_UNIT + 4 * j + 3)
                src = ps[:, (4 + 2 * j) % 8, :]
                if j < 2:
                    act.activation(qk_nat[:, j, 0, :], src, ACT.Copy).then_inc(odd_act, 1)
                elif j == 2:
                    act.activation(val[:, 0, :, :], src.rearrange("p (h n) -> p h n", h=C_HEADS), ACT.Copy).then_inc(odd_act, 1)
                elif j == 3:
                    act.activation(gate[:, 0, :], src, ACT.Silu)
                    act.activation(gate[:, 1, :], ps[:, 3, :], ACT.Silu).then_inc(odd_act, 1)
                elif j < 6:
                    act.activation(bc_nat[:, j - 4, 0, :], src, ACT.Copy).then_inc(odd_act, 1)
                split_until(2 * ODD_UNIT + 4 * (j + 1) + AHEAD)
            for i in range(0, 8, 2):
                act.wait_ge(oddT_done, i + 1)
                dst = (qT, kT, bT, uT)[i // 2]
                act.activation(dst[:, :, 0:P], ps[:, (2 + i) % 8, :].rearrange("p (k n) -> p k n", k=4),
                               ACT.Copy).then_inc(oddT_act, 1)
            act.wait_ge(gn_inv, 1)
            act.activation(gn_rstd, gn_rstd, ACT.Sqrt).then_inc(gn_std, 1)
            act.wait_ge(conv_done, 1)
            act.activation(tok_hi[:, 4:8, :], conv, ACT.Copy).then_inc(mix_hi, 1)
            for t in range(NT):
                act.wait_ge(yrT_done, t + 1)
                act.activation(tok_hi[:, 0:4, t * P:(t + 1) * P], ps[:, (7, 0)[t], :].rearrange("p (k n) -> p k n", k=4),
                               ACT.Copy).then_inc(mix_hi, 1)
            act.wait_ge(router_landed, 16)
            act.activation(router_hi[:, :, :], router[:, :, :], ACT.Copy).then_inc(router_hi_done, 1)
            split_until(2 * (ODD_UNIT + 2 * ODD_IN_CHUNKS) + 4 + AHEAD)

            norm(3, 2 * MOE_UNIT)
            act.wait_ge(logitsT_done, 1)
            act.activation(logits_T, ps[0:EXPERTS, 4, 0:SEQ], ACT.Copy).then_inc(logitsT_out, 1)
            act.wait_ge(gap_done, 1)
            act.activation(gate1, gap, ACT.Exp).then_inc(gap_exp, 1)

            def gather_out(p):
                for i in range(2):
                    act.wait_ge(gathered, 2 * p + i + 1)
                    act.activation(tok_hi[:, 4 * i:4 * i + 4, 0:SLOTS],
                                   ps[:, GATHER_BANKS[i], :].rearrange("p (k n) -> p k n", k=4),
                                   ACT.Copy).then_inc(gather_hi, 1)

            def weights_out(p):
                act.wait_ge(weighT_done, p + 1)
                act.activation(weigh_T, ps[:, WEIGHT_BANK, 0:SEQ], ACT.Copy).then_inc(weighT_out, 1)

            def late(p):
                weights_out(p)
                gather_out(p + 1)

            def passes(lo, hi):
                with act.Fori(lo, hi) as p:
                    ffn(moe, p * FC, 2 * MOE_UNIT, p * FC, None, lambda: late(p))
                    multiplied(act, 2 * MOE_UNIT + PASS_PIECES - 1, p * FC)
                    act.activation(y_sb[:, 0:HALF], ps[:, moe.y_banks[0], :], ACT.Copy).then_inc(y_act, 1)

            act.wait_ge(y_dve, 1)
            act.activation(weigh_T, y_sb[:, HALF:HALF + SEQ], ACT.Copy).then_inc(weighT_out, 1)
            act.activation(y_sb[:, 0:HALF], y_sb[:, HALF:D], ACT.Copy).then_inc(y_act, 1)
            gather_out(0)
            passes(0, EXPERTS)
            act.wait_ge(most_done, 1)
            full = act.value_load(most_i[0:1, 0:1])
            with act.If(full > SLOTS):
                passes(EXPERTS, 2 * EXPERTS)
            act.drain().then_inc(last_act, 1)
            for t in range(NT):
                square(4, t, 0)
                square(4, t, 1)
                norm_root(4, t)

        @block.vector
        def _(dve):
            split_until, split_skip = splitter(split_lo, dve)
            step = [0]

            def link(ins):
                step[0] += 1
                ins.then_inc(dve_step, 1)
                dve.wait_ge(dve_step, step[0])

            def norm_mean(stage, t):
                done = 4 if t else norm_order(stage).index((0, 1)) + 1
                dve.wait_ge(sumsq_done, 4 * stage + done)
                link(dve.scalar_tensor_tensor(out=inv[:, t:t + 1], in0=sumsq[:, t, 0:1], scalar=EPS * D,
                                              in1=sumsq[:, t, 1:2], op0=ALU.add, op1=ALU.add))
                dve.reciprocal(inv[:, t:t + 1], inv[:, t:t + 1]).then_inc(inv_done, 1)

            def norm_apply(stage, t):
                dve.wait_ge(rstd_done, NT * stage + t + 1)
                if stage == 0:
                    dve.wait_ge(first_gain_landed, 16)
                else:
                    dve.wait_ge(gain_landed, 16 * stage)
                dve.scalar_tensor_tensor(out=xn[:, t, :], in0=x[:, t, :], scalar=rstd[:, t:t + 1],
                                         in1=gain[:, :], op0=ALU.mult, op1=ALU.mult)\
                   .then_inc(xn_done if stage < 4 else out_ready, 1)

            def norm_lo(stage, t):
                for half in range(2):
                    dst = (slice(None), slice(4 * half, 4 * half + 4), slice(t * P, (t + 1) * P))
                    dve.wait_ge(tok_hi_done, 4 * stage + 2 * t + half + 1)
                    dve.tensor_tensor(tok_lo[dst], ps[:, 2 * t + half, :].rearrange("p (k n) -> p k n", k=4),
                                      tok_hi[dst].bitcast(F32), ALU.subtract).then_inc(tok_lo_done, 1)

            def residual_norm(stage, base, banks, n_before):
                order = norm_order(stage)
                first = order.index((0, 1)) + 1

                def add(i):
                    t, half = order[i]
                    xs = x[:, t, half * HALF:(half + 1) * HALF]
                    dve.tensor_tensor(xs, xs, ps[:, banks[i], :], ALU.add).then_inc(x_updated, 1)

                if first == 3:
                    multiplied(dve, base - 5)
                    add(0)
                    add(1)
                    split_until(base + 2)
                dve.wait_ge(tile0_done, n_before)
                for i in range(2 if first == 3 else 0, first):
                    add(i)
                norm_mean(stage, 0)
                norm_apply(stage, 0)
                split_until(base + 3)
                multiplied(dve, base - 1)
                for i in range(first, 4):
                    add(i)
                norm_lo(stage, 0)
                norm_mean(stage, 1)
                split_until(base + 4)
                norm_apply(stage, 1)
                split_until(base + 5)
                norm_lo(stage, 1)
                split_until(base + AHEAD)

            for t in range(NT):
                norm_mean(0, t)
                norm_apply(0, t)
            for t in range(NT):
                split_until(1 + t)
                norm_lo(0, t)
            split_until(AHEAD)
            dve.wait_ge(pos_landed, 16)
            dve.wait_ge(freq_done, 1)
            link(dve.tensor_copy(pos_f, pos_i[:, :]))
            for t in range(NT):
                ins = dve.tensor_scalar(angle[:, t, :], inv_freq, pos_f[:, t:t + 1], None, ALU.mult)
            link(ins)
            link(dve.tensor_scalar(turns, angle, 1.0 / (2.0 * math.pi), None, ALU.mult))
            whole = 1.5 * 2.0 ** 23
            link(dve.tensor_scalar(turns, turns, whole, whole, ALU.add, ALU.subtract))
            two_pi = 2.0 * math.pi
            c1 = 6.28125
            c2 = float(np.float32(np.round((two_pi - c1) * 2.0 ** 21) / 2.0 ** 21))
            c3 = two_pi - c1 - c2
            for c in (c1, c2, c3):
                link(dve.scalar_tensor_tensor(out=angle, in0=turns, scalar=-c, in1=angle, op0=ALU.mult, op1=ALU.add))
            link(dve.tensor_scalar(angle, angle, math.pi, -math.pi, ALU.min, ALU.max))
            link(dve.scalar_tensor_tensor(out=turns, in0=angle, scalar=-1.0, in1=angle, op0=ALU.mult, op1=ALU.max))
            dve.tensor_scalar(turns, turns, -1.0, math.pi / 2.0, ALU.mult, ALU.add).then_inc(angle_done, 1)
            in_banks = (5, 7, 1)
            for j in range(3):
                multiplied(dve, 4 * j + 3)
                dve.tensor_copy(proj[:, 1, j * IN_CHUNK:(j + 1) * IN_CHUNK], ps[:, in_banks[j], 0:IN_CHUNK])\
                   .then_inc(in_dve, 1)
                split_until(4 * (j + 1) + AHEAD)
            dve.wait_ge(in_act, 3)
            dve.wait_ge(in_dve, 3)
            dve.wait_ge(sumsq_done, 2)
            for t in range(NT):
                dst = ka_twice[:, t, :].rearrange("p (g a n) -> p g a n", g=A_KV, a=2)
                src = proj[:, t, COL_K:COL_V].rearrange("p (g n) -> p g n", g=A_KV)
                for a in range(2):
                    ins = dve.tensor_copy(dst[:, :, a, :], src)
            ins.then_inc(ka_doubled, 1)
            dve.wait_ge(lat_sq, 1)
            for i, n in enumerate((Q_LORA, KV_LORA)):
                ins = dve.tensor_scalar(lat_rstd[:, :, i], lat_sumsq[:, :, i], 1.0 / n, EPS, ALU.mult, ALU.add)
            link(ins)
            dve.reciprocal(lat_rstd, lat_rstd).then_inc(lat_inv, 1)
            dve.wait_ge(lat_std, 1)
            dve.wait_ge(lat_gain_landed, 32)
            for t in range(NT):
                for i, (at, n, go) in enumerate(((COL_CQ, Q_LORA, 0), (COL_CKV, KV_LORA, Q_LORA))):
                    dve.scalar_tensor_tensor(out=proj[:, t, at:at + n], in0=proj[:, t, at:at + n],
                                             scalar=lat_rstd[:, t, i:i + 1], in1=lat_gain[:, go:go + n],
                                             op0=ALU.mult, op1=ALU.mult).then_inc(lat_done, 1)
            dve.wait_ge(qaT_done, 2)
            dve.tensor_copy(qaT[:, :, P:SEQ], ps[:, 3, :].rearrange("p (k n) -> p k n", k=4)).then_inc(qaT_dve, 1)
            dve.wait_ge(qaT_done, 3)
            dve.tensor_copy(kaT, ps[:, 4, :].rearrange("p (k n) -> p k n", k=2)).then_inc(qaT_dve, 1)
            for t in range(NT):
                dve.wait_ge(latT_hi, t + 1)
                dve.tensor_tensor(fT_lo[:, 0:3, t * P:(t + 1) * P], ps[:, 5 + t, 0:3 * P].rearrange("p (k n) -> p k n", k=3),
                                  fT_hi[:, 0:3, t * P:(t + 1) * P].bitcast(F32), ALU.subtract).then_inc(latT_lo, 1)
            dve.wait_ge(latT_hi, 3)
            dve.tensor_tensor(latkv_lo, ps[:, 7, :].rearrange("p (k n) -> p k n", k=2), latkv_hi.bitcast(F32),
                              ALU.subtract).then_inc(latT_lo, 1)
            dve.wait_ge(sinks_landed, 16)
            sinks_pos = sinks.rearrange("p (j a) -> p a j", a=2)
            by_pos = lambda v: v.rearrange("p (a j) -> p a j", a=2)

            def softmax_start(kind, t, inst):
                nk = P * (t + 1)
                dve.wait_ge(scored, inst + 1)
                if kind == "A":
                    if inst == 0:
                        dve.wait_ge(bias_done, 1)
                    else:
                        dve.wait_ge(pT_done, 2)
                    for b in range(2 * (t + 1)):
                        if t == 0:
                            tab = bias[:, 4 * b:4 * b + 4, P:SEQ]
                            s = ps[:, b, :].rearrange("p (h n) -> p h n", h=4)
                            o = probs_flat[:, b * HALF:(b + 1) * HALF].rearrange("p (h n) -> p h n", h=4)
                        else:
                            tab = bias[:, 2 * b:2 * b + 2, :]
                            s = ps[:, b, :].rearrange("p (h n) -> p h n", h=2)
                            o = probs_flat[:, b * HALF:(b + 1) * HALF].rearrange("p (h n) -> p h n", h=2)
                        ins = dve.tensor_tensor(o, s, tab, ALU.add)
                    ins.then_inc(biased, 1)
                    dve.wait_ge(biased, inst + 1)
                    link(dve.tensor_reduce(row_max, probs_flat[:, 0:8 * nk].rearrange("p (h n) -> p h n", h=8), AX.X, ALU.max))
                    link(dve.scalar_tensor_tensor(out=by_pos(row_max), in0=sinks_pos, scalar=1.0 / A_SCALE,
                                                  in1=by_pos(row_max), op0=ALU.mult, op1=ALU.max))
                    dve.tensor_scalar(neg_max, row_max, -A_SCALE, None, ALU.mult).then_inc(max_done, 1)
                    dve.wait_ge(max_done, inst + 1)
                    dve.tensor_tensor(by_pos(sink_e), sinks_pos, by_pos(neg_max), ALU.add).then_inc(sink_arg, 1)
                else:
                    s = flat_ps[:, 0:8 * nk].rearrange("p (h n) -> p h n", h=8)
                    link(dve.memset(s[0:CHUNK, :, nk - CHUNK:nk], -1.0e30))
                    link(dve.tensor_reduce(row_max, s, AX.X, ALU.max))
                    dve.tensor_scalar(neg_max, row_max, -B_SCALE, None, ALU.mult).then_inc(max_done, 1)

            def softmax_end(kind, t, inst):
                nk = P * (t + 1)
                dve.wait_ge(exp_done, inst + 1)
                if kind == "A":
                    link(dve.tensor_tensor(den, den, sink_e, ALU.add))
                link(dve.reciprocal(den, den))
                pr = probs_flat[:, 0:8 * nk].rearrange("p (h n) -> p h n", h=8)
                dve.tensor_tensor(pr, pr, den[:, :, None].to_broadcast([P, 8, nk]), ALU.mult).then_inc(probs_done, 1)

            pt_bank = [0]

            def probs_out(t):
                for b in range(2 * (t + 1)):
                    if pt_bank[0] % 2:
                        dve.wait_ge(pT_done, pt_bank[0] + 1)
                        dve.tensor_copy(pT_flat[:, b * HALF:(b + 1) * HALF], ps[:, 5, :]).then_inc(pT_dve, 1)
                    pt_bank[0] += 1

            def mix_out(kind, t, inst):
                dve.wait_ge(mix_hi, inst + 1)
                k0 = 0 if kind == "A" else 4
                dst = (slice(None), slice(k0, k0 + 4), slice(t * P, (t + 1) * P))
                dve.tensor_tensor(tok_lo[dst], ps[:, 6 + t, :].rearrange("p (k n) -> p k n", k=4),
                                  tok_hi[dst].bitcast(F32), ALU.subtract).then_inc(mix_lo, 1)

            softmax_start("A", 0, 0)
            multiplied(dve, 2 * U_IN + 1)
            q_flat = q96[:, 1, :, :].rearrange("p h n -> p (h n)")
            dve.tensor_copy(q_flat[:, 0:HALF], ps[:, 3, :]).then_inc(uq_dve, 1)
            multiplied(dve, 2 * U_IN + 3)
            dve.tensor_copy(q_flat[:, HALF:], ps[:, 5, 0:256]).then_inc(uq_dve, 1)
            split_until(2 * U_IN + 4 + AHEAD)
            softmax_end("A", 0, 0)
            multiplied(dve, 2 * (U_IN + U_UQ + U_UKV) - 1)
            for half in range(2):
                kv = ps[:, 2 + half, :].rearrange("p (h n) -> p h n", h=4)
                dve.tensor_copy(k96[:, 1, 4 * half:4 * half + 4, 0:B_NOPE], kv[:, :, 0:B_NOPE])
                ins = dve.tensor_copy(v64[:, 1, 4 * half:4 * half + 4, :], kv[:, :, B_NOPE:])
            ins.then_inc(ukv_dve, 1)
            split_until(2 * (U_IN + U_UQ + U_UKV) + AHEAD)
            probs_out(0)
            mix_out("A", 0, 0)
            softmax_start("A", 1, 1)
            softmax_end("A", 1, 1)
            probs_out(1)
            mix_out("A", 1, 1)
            for i in range(1, 8, 2):
                dve.wait_ge(kqT_done, i + 1)
                dst = qbT if i < 4 else kbT
                t = (i % 4) // 2
                dve.tensor_copy(dst[0:B_DIM, 4:8, t * P:(t + 1) * P],
                                ps[0:B_DIM, i % 4, :].rearrange("p (k n) -> p k n", k=4)).then_inc(kqT_dve, 1)
            for t in range(NT):
                softmax_start("B", t, 2 + t)
                softmax_end("B", t, 2 + t)
                probs_out(t)
                mix_out("B", t, 2 + t)

            def chunk(sig, q, base, laps, with_down, before_turn=None):
                n = CHUNK_PIECES if with_down else 2 * GATE_UNITS
                for j in range(n):
                    if j == 7:
                        multiplied(dve, base + 7, laps)
                        for t in range(sig.tiles):
                            dve.wait_ge(sig.silu_done, q * sig.tiles + t + 1)
                            dve.tensor_tensor(hid[:, t, :], hid[:, t, :], ps[:, sig.up_banks[t], :], ALU.mult)\
                               .then_inc(sig.act_done, 1)
                    if j == n - 1:
                        if before_turn is not None:
                            before_turn()
                        for t in range(sig.tiles):
                            dve.wait_ge(sig.turned_hi, q * sig.tiles + t + 1)
                            dve.tensor_tensor(fT_lo[:, :, t * P:(t + 1) * P],
                                              ps[:, sig.turned_banks[t], :].rearrange("p (k n) -> p k n", k=4),
                                              fT_hi[:, :, t * P:(t + 1) * P].bitcast(F32), ALU.subtract)\
                               .then_inc(sig.turned_lo, 1)
                    split_lo(dve, base + j + AHEAD, laps)

            def ffn(sig, q, base, lap, between, before_last):
                chunk(sig, q, base, lap, False, between)
                at = base + 2 * GATE_UNITS
                chunk(sig, q + 1, at, lap, True)
                at += CHUNK_PIECES
                with dve.Fori(LOOP_FIRST, FC) as c:
                    chunk(sig, q + c, at, lap + c - LOOP_FIRST, True)
                if sig.tiles == NT:
                    return
                before_last()
                for j in range(2 * DOWN_UNITS):
                    split_lo(dve, base + PASS_PIECES - 2 * DOWN_UNITS + j + AHEAD, lap)

            residual_norm(1, 2 * FFN_UNIT, (0, 1, 2, 3), 1)
            dve.wait_ge(decay_exp, 1)
            dve.tensor_scalar(decay, decay, float(C_DIM) ** -0.5, None, ALU.mult)
            ffn(dense, 0, 2 * FFN_UNIT, 0, None, None)
            split_skip(2 * ODD_UNIT + 2)

            residual_norm(2, 2 * ODD_UNIT, dense.y_banks, 2)
            dve.wait_ge(conv_turned, 1)
            dve.tensor_copy(conv_w, ps[:, 6, 0:CONV_W * 4].rearrange("p (j k) -> p j k", j=CONV_W)).then_inc(dve_conv, 1)
            for j in range(ODD_IN_CHUNKS):
                multiplied(dve, 2 * ODD_UNIT + 4 * j + 3)
                src = ps[:, (4 + 2 * j) % 8 + 1, :]
                if j < 2:
                    dve.tensor_copy(qk_nat[:, j, 1, :], src).then_inc(odd_dve, 1)
                elif j == 2:
                    dve.tensor_copy(val[:, 1, :, :], src.rearrange("p (h n) -> p h n", h=C_HEADS)).then_inc(odd_dve, 1)
                elif j == 3:
                    dve.wait_ge(odd_act, 4)
                    dve.wait_ge(gn_gain_landed, 16)
                    dve.tensor_tensor(gate, gate, gn_gain[:, None, :].to_broadcast([P, NT, HALF]), ALU.mult)\
                       .then_inc(odd_dve, 1)
                elif j < 6:
                    dve.tensor_copy(bc_nat[:, j - 4, 1, :], src).then_inc(odd_dve, 1)
                else:
                    dve.wait_ge(odd_act, 6)
                    dve.wait_ge(odd_dve, 6)
                    for t in range(NT):
                        ins = dve.tensor_tensor(bc_nat[:, 1, t, :], bc_nat[:, 1, t, :], ps[:, t, :], ALU.mult)
                    ins.then_inc(odd_dve, 1)
                split_until(2 * ODD_UNIT + 4 * (j + 1) + AHEAD)
            for i in range(1, 8, 2):
                dve.wait_ge(oddT_done, i + 1)
                dst = (qT, kT, bT, uT)[i // 2]
                dve.tensor_copy(dst[:, :, P:SEQ], ps[:, (2 + i) % 8, :].rearrange("p (k n) -> p k n", k=4))\
                   .then_inc(oddT_dve, 1)
            for i in range(3):
                dve.wait_ge(ret_scored, i + 1)
                if i < 2:
                    dve.tensor_tensor(sT0[:, 2 * i:2 * i + 2, :], ps[:, 2 + i, :].rearrange("p (h n) -> p h n", h=2),
                                      decay[:, 2 * i:2 * i + 2, :], ALU.mult).then_inc(ret_decayed, 1)
                else:
                    dve.tensor_tensor(sT1, ps[:, 4, :].rearrange("p (h n) -> p h n", h=C_HEADS), decay[:, :, 0:P],
                                      ALU.mult).then_inc(ret_decayed, 1)
            dve.wait_ge(oddT_act, 4)
            dve.wait_ge(oddT_dve, 4)
            dve.wait_ge(dve_conv, 1)
            for shift in range(CONV_W):
                for k in range(4):
                    w = conv_w[:, CONV_W - 1 - shift, k:k + 1]
                    if shift == 0:
                        ins = dve.tensor_scalar(conv[:, k, :], uT[:, k, :], w, None, ALU.mult)
                    else:
                        ins = dve.scalar_tensor_tensor(out=conv[:, k, shift:], in0=uT[:, k, 0:SEQ - shift], scalar=w,
                                                       in1=conv[:, k, shift:], op0=ALU.mult, op1=ALU.add)
                link(ins)
            dve.tensor_tensor(conv, conv, bT, ALU.mult).then_inc(conv_done, 1)
            for t in range(NT):
                dve.wait_ge(ret_out, t + 1)
                for h in range(C_HEADS):
                    ins = dve.bn_stats(bn[:, t * C_HEADS + h, :], ps[:, 5 + t, h * P:(h + 1) * P])
            link(ins)
            for i in range(NT * C_HEADS):
                ins = dve.bn_aggr(mv[:, i, :], bn[:, i, :])
            link(ins)
            link(dve.tensor_scalar(gn_rstd, mv[:, :, 1], EPS, None, ALU.add))
            dve.reciprocal(gn_rstd, gn_rstd).then_inc(gn_inv, 1)
            dve.wait_ge(mix_hi, 5)
            dve.wait_ge(conv_done, 1)
            dve.tensor_tensor(tok_lo[:, 4:8, :], conv, tok_hi[:, 4:8, :].bitcast(F32), ALU.subtract).then_inc(mix_lo, 1)
            dve.wait_ge(gn_std, 1)
            dve.wait_ge(odd_dve, 7)
            for t in range(NT):
                for h in range(C_HEADS):
                    i = t * C_HEADS + h
                    ins = dve.tensor_scalar(yr[:, t, h * P:(h + 1) * P], ps[:, 5 + t, h * P:(h + 1) * P], mv[:, i, 0:1],
                                            gn_rstd[:, i:i + 1], ALU.subtract, ALU.mult)
                link(ins)
                dve.tensor_tensor(yr[:, t, :], yr[:, t, :], gate[:, t, :], ALU.mult).then_inc(yr_done, 1)
            for t in range(NT):
                dve.wait_ge(mix_hi, 6 + t)
                dst = (slice(None), slice(0, 4), slice(t * P, (t + 1) * P))
                dve.tensor_tensor(tok_lo[dst], ps[:, (7, 0)[t], :].rearrange("p (k n) -> p k n", k=4),
                                  tok_hi[dst].bitcast(F32), ALU.subtract).then_inc(mix_lo, 1)
            dve.wait_ge(router_hi_done, 1)
            dve.tensor_tensor(router_lo[:, :, :], router[:, :, :], router_hi[:, :, :].bitcast(F32), ALU.subtract)\
               .then_inc(router_lo_done, 1)
            residual_norm(3, 2 * MOE_UNIT, (1, 2, 3, 6), 3)
            dve.wait_ge(logits_done, 1)
            dve.wait_ge(route_consts, 1)
            link(dve.tensor_copy(logits, ps[:, 5, 0:NT * EXPERTS].rearrange("p (t e) -> p t e", t=NT)))
            for t in range(NT):
                ins = dve.max(top[:, t, :], logits[:, t, :])
            link(ins)
            for t in range(NT):
                ins = dve.max_index(idx_u[:, t, :], top[:, t, :], logits[:, t, :])
            link(ins)
            dve.tensor_tensor(gap, top[:, :, 1], top[:, :, 0], ALU.subtract).then_inc(gap_done, 1)
            link(dve.tensor_copy(idx_f, idx_u[:, :, 0:2]))
            for t in range(NT):
                dve.tensor_scalar(pick1[:, t, :], iota8, idx_f[:, t, 0:1], None, ALU.is_equal)
                ins = dve.tensor_scalar(pick2[:, t, :], iota8, idx_f[:, t, 1:2], None, ALU.is_equal)
            link(ins)
            dve.tensor_tensor(chosen, pick1, pick2, ALU.add).then_inc(chosen_done, 1)
            dve.wait_ge(gap_exp, 1)
            link(dve.tensor_scalar(gate2, gate1, 1.0, None, ALU.add))
            link(dve.reciprocal(gate2, gate2))
            link(dve.tensor_tensor(gate1, gate1, gate2, ALU.mult))
            for t in range(NT):
                link(dve.tensor_scalar(pick1[:, t, :], pick1[:, t, :], gate2[:, t:t + 1], None, ALU.mult))
                ins = dve.scalar_tensor_tensor(out=share[:, t, 0:EXPERTS], in0=pick2[:, t, :], scalar=gate1[:, t:t + 1],
                                               in1=pick1[:, t, :], op0=ALU.mult, op1=ALU.add)
            link(ins)
            dve.memset(share[:, :, 2 * EXPERTS:], 0.0)
            dve.memset(place[:, :, 2 * EXPERTS:], -1.0)
            link(dve.tensor_copy(share[:, :, EXPERTS:2 * EXPERTS], share[:, :, 0:EXPERTS]))
            dve.wait_ge(counted, 1)
            dve.wait_ge(chosen_done, 1)
            link(dve.scalar_tensor_tensor(out=place1, in0=ps[:, 7, 0:NT * EXPERTS].rearrange("p (t e) -> p t e", t=NT),
                                          scalar=1.0, in1=chosen, op0=ALU.add, op1=ALU.mult))
            for b in range(2):
                dve.tensor_scalar(place[:, :, b * EXPERTS:(b + 1) * EXPERTS], place1, -1.0 - b * SLOTS, None, ALU.add)
            link(dve.tensor_reduce(most, ps[:, 7, NT * EXPERTS:3 * EXPERTS], AX.X, ALU.max))
            dve.tensor_copy(most_i[:, :], most).then_inc(most_done, 1)
            dve.wait_ge(most_done, 1)

            def make_pick(p):
                for t in range(NT):
                    ins = dve.tensor_scalar(pick[:, t, :], iota_slot, place[:, t, bass.ds(p, 1)], None, ALU.is_equal)
                ins.then_inc(pick_done, 1)

            def make_weigh(p):
                for t in range(NT):
                    ins = dve.tensor_scalar(weigh[:, t, :], iota_slot, place[:, t, bass.ds(p, 1)],
                                            share[:, t, bass.ds(p, 1)], ALU.is_equal, ALU.mult)
                ins.then_inc(weigh_done, 1)

            def gather_out(p):
                for i in range(2):
                    dst = (slice(None), slice(4 * i, 4 * i + 4), slice(0, SLOTS))
                    dve.wait_ge(gather_hi, 2 * p + i + 1)
                    dve.tensor_tensor(tok_lo[dst], ps[:, GATHER_BANKS[i], :].rearrange("p (k n) -> p k n", k=4),
                                      tok_hi[dst].bitcast(F32), ALU.subtract).then_inc(gather_lo, 1)

            def add_scattered(done, first, halves, signal):
                for i in halves:
                    t, half = i // 2, i % 2
                    xs = x[:, t, half * HALF:(half + 1) * HALF]
                    dve.wait_ge(done, first + i + 1)
                    dve.tensor_tensor(xs, xs, ps[:, SCATTER_BANKS[i], :], ALU.add).then_inc(signal, 1)

            def passes(lo, hi):
                with dve.Fori(lo, hi) as p:
                    make_weigh(p)
                    make_pick(p + 1)
                    ffn(moe, p * FC, 2 * MOE_UNIT, p * FC, lambda: add_scattered(scattered, 4 * p, range(4), moe_added),
                        lambda: gather_out(p + 1))
                    multiplied(dve, 2 * MOE_UNIT + PASS_PIECES - 1, p * FC)
                    dve.tensor_copy(y_sb[:, HALF:D], ps[:, moe.y_banks[1], :]).then_inc(y_dve, 1)

            make_pick(0)
            dve.memset(y_sb[:, HALF:D], 0.0).then_inc(y_dve, 1)
            gather_out(0)
            passes(0, EXPERTS)
            full = dve.value_load(most_i[0:1, 0:1])
            with dve.If(full > SLOTS):
                passes(EXPERTS, 2 * EXPERTS)
            dve.drain().then_inc(last_dve, 1)
            dve.wait_ge(last_dve, 1)
            for t in range(NT):
                add_scattered(last_scattered, 0, (2 * t, 2 * t + 1), x_updated)
                norm_mean(4, t)
                norm_apply(4, t)


_NAMES = ["x", "positions", "even_norm_mix", "even_w_in", "even_sinks", "even_q_norm", "even_w_uq", "even_kv_norm",
          "even_w_ukv", "even_w_out", "even_norm_ffn", "even_w_gate", "even_w_up", "even_w_down", "odd_norm_mix",
          "odd_w_in", "odd_ret_gn", "odd_conv_w", "odd_w_out", "odd_norm_ffn", "odd_router", "odd_we_gate", "odd_we_up",
          "odd_we_down", "final_norm"]


def kernel(**inputs):
    import concourse.bacc as bacc
    from concourse.bass_utils import run_bass_kernel_spmd

    nc = bacc.Bacc("TRN2", target_bir_lowering=False, num_devices=1)
    arrays, aps = {}, {}
    for name in _NAMES:
        a = np.ascontiguousarray(inputs[name])
        arrays[f"in_{name}"] = a
        aps[name] = nc.dram_tensor(f"in_{name}", a.shape, mybir.dt.from_np(a.dtype), kind="ExternalInput").ap()
    out = nc.dram_tensor("out_y", (1, SEQ, D), F32, kind="ExternalOutput").ap()
    build_trunk(nc, aps, out)
    r = run_bass_kernel_spmd(nc, [arrays], core_ids=[0])
    return r.results[0]["out_y"]
```

```python
import math
from contextlib import ExitStack

import numpy as np

import concourse.bass as bass
from concourse import mybir

F32 = mybir.dt.float32
F32R = mybir.dt.float32r
I32 = mybir.dt.int32
U32 = mybir.dt.uint32
ALU = mybir.AluOpType
ACT = mybir.ActivationFunctionType
AX = mybir.AxisListType

P = 128
SEQ = 256
NT = SEQ // P
D = 1024
KD = D // P
CHUNK = 64
EPS = 1e-6
HALF = 512
A_HEADS, A_KV, A_DIM = 8, 2, 64
B_HEADS, B_NOPE, B_ROPE, B_V = 8, 64, 32, 64
B_DIM = B_NOPE + B_ROPE
Q_LORA, KV_LORA = 384, 256
ROPE_HALF = B_ROPE // 2
ROPE_THETA = 10000.0
EVEN_IN = A_HEADS * A_DIM + 2 * A_KV * A_DIM + Q_LORA + KV_LORA + B_ROPE
COL_K = A_HEADS * A_DIM
COL_V = COL_K + A_KV * A_DIM
COL_CQ = COL_V + A_KV * A_DIM
COL_CKV = COL_CQ + Q_LORA
COL_KR = COL_CKV + KV_LORA
IN_CHUNK = EVEN_IN // 3
A_SCALE = float(A_DIM) ** -0.5
B_SCALE = float(B_DIM) ** -0.5
MASKED = 1.0e32
C_HEADS, C_DIM = 4, 128
CONV_W = 3
D_FF = 3584
FC = D_FF // HALF
EXPERTS = 8
SLOTS = 128

RING = 6
AHEAD = 6
UNIT = 2048
PIECE = 1024
GATE_UNITS, DOWN_UNITS = 4, 2
CHUNK_UNITS = GATE_UNITS + DOWN_UNITS
CHUNK_PIECES = 2 * CHUNK_UNITS
PASS_UNITS = FC * CHUNK_UNITS
PASS_PIECES = 2 * PASS_UNITS
U_IN, U_UQ, U_UKV, U_OUT = 6, 2, 1, 4
FFN_UNIT = U_IN + U_UQ + U_UKV + U_OUT
ODD_UNIT = FFN_UNIT + PASS_UNITS
ODD_IN_CHUNKS = 7
ODD_CHUNKS = (4, 5, 6, 0, 1, 2, 3)
MOE_UNIT = ODD_UNIT + 2 * ODD_IN_CHUNKS + U_OUT
assert CHUNK_UNITS == RING and EVEN_IN % 3 == 0
LOOP_FIRST = 2


class FfnSignals:

    def __init__(self, sem, name, tiles, gate, up, turned, y):
        self.tiles = tiles
        self.gate_banks, self.up_banks, self.turned_banks, self.y_banks = gate, up, turned, y
        self.silu_done = sem(f"{name}_silu_done")
        self.act_done = sem(f"{name}_act_done")
        self.turned = sem(f"{name}_turned")
        self.turned_hi = sem(f"{name}_turned_hi")
        self.turned_lo = sem(f"{name}_turned_lo")


def build_trunk(nc, ins, out):
    g = ins
    with ExitStack() as ctx:
        def sb(name, shape, dt=F32):
            return ctx.enter_context(nc.sbuf_tensor(name, shape, dt))

        def sem(name):
            return ctx.enter_context(nc.semaphore(name))

        raw = sb("raw", [P, RING, UNIT])
        w_hi = sb("w_hi", [P, RING, PIECE], F32R)
        w_lo = sb("w_lo", [P, RING, PIECE], F32R)
        x = sb("x", [P, NT, D])
        tok_hi = sb("tok_hi", [P, KD, SEQ], F32R)
        tok_lo = sb("tok_lo", [P, KD, SEQ], F32R)
        fT_hi = sb("fT_hi", [P, 4, SEQ], F32R)
        fT_lo = sb("fT_lo", [P, 4, SEQ], F32R)
        gain = sb("gain", [P, D])
        lat_gain = sb("lat_gain", [P, Q_LORA + KV_LORA])
        gn_gain = lat_gain[:, 0:C_HEADS * C_DIM]
        ident = sb("ident", [P, P])
        xn = sb("xn", [P, NT, D])
        spare = sb("spare", [P, 2 * D])
        hid = spare[:, 0:D].rearrange("p (t n) -> p t n", t=NT)
        y_sb = spare[:, D:2 * D]
        arena = sb("arena", [P, 11648])

        taken = [0]

        def part(shape):
            n = int(np.prod(shape))
            at = taken[0]
            taken[0] += n
            assert taken[0] <= 11648, taken[0]
            v = arena[:, at:at + n]
            if len(shape) == 2:
                v = v.rearrange("p (a b) -> p a b", a=shape[0])
            if len(shape) == 3:
                v = v.rearrange("p (a b c) -> p a b c", a=shape[0], b=shape[1])
            return v

        proj = part([NT, EVEN_IN])
        q96 = part([NT, B_HEADS, B_DIM])
        k96 = part([NT, B_HEADS, B_DIM])
        qaT = part([4, SEQ])
        kaT = part([A_KV, SEQ])
        bias = part([A_HEADS, SEQ])
        kbT = bias
        qbT = part([B_HEADS, SEQ])
        v64 = proj[:, :, 0:B_HEADS * B_V].rearrange("p t (h d) -> p t h d", h=B_HEADS)
        latkv_hi, latkv_lo = tok_hi[:, 4:6, :], tok_lo[:, 4:6, :]
        ka_twice = q96[:, :, :, :].rearrange("p t h n -> p t (h n)")[:, :, 0:2 * A_KV * A_DIM]
        xn_flat = xn[:, :, :].rearrange("p t d -> p (t d)")
        probs_of = (spare[:, 0:D], xn_flat, qaT.rearrange("p a n -> p (a n)"), xn_flat)
        after_latents = [proj[:, t, COL_CQ:COL_CQ + HALF] for t in range(NT)]
        in_spare = [spare[:, b * HALF:(b + 1) * HALF] for b in range(4)]
        probsT_of = (after_latents, in_spare, after_latents, in_spare)
        SCORE_BANK = (0, 2, 4, 0)
        PROBS_BANKS = ((6, 7), (6, 7, 4, 5), (4, 5), (0, 1, 3, 5))
        MIXED_BANK = (0, 1, 4, 2)
        EVEN_OUT_BANKS = (6, 7, 3, 5)
        taken[0] = 0
        val = part([NT, C_HEADS, C_DIM])
        gate = part([NT, HALF])
        qT = part([C_HEADS, SEQ])
        kT = part([C_HEADS, SEQ])
        bT = part([4, SEQ])
        uT = part([4, SEQ])
        decay = part([C_HEADS, SEQ])
        sT0 = part([C_HEADS, SEQ])
        sT1 = part([C_HEADS, P])
        conv = part([4, SEQ])
        yr = part([NT, HALF])
        qk_nat = xn[:, :, :].rearrange("p a (t n) -> p a t n", t=NT)
        bc_nat = spare[:, :].rearrange("p (a t n) -> p a t n", a=2, t=NT)
        before = part([P])
        ones = part([P])
        iota_slot = part([SLOTS])
        taken[0] = 0
        pick = part([NT, SLOTS])
        weigh = part([NT, SLOTS])
        weigh_T = part([SEQ])
        logits_T = part([SEQ])[0:EXPERTS, :]
        final_scratch = part([NT, 2, HALF])

        small = sb("small", [P, 704])
        used = [0]

        def bit(shape):
            n = int(np.prod(shape))
            at = used[0]
            used[0] += n
            assert used[0] <= 704, used[0]
            v = small[:, at:at + n]
            if len(shape) == 2:
                v = v.rearrange("p (a b) -> p a b", a=shape[0])
            if len(shape) == 3:
                v = v.rearrange("p (a b c) -> p a b c", a=shape[0], b=shape[1])
            return v

        sumsq = bit([NT, 2])
        inv = bit([NT])
        rstd = bit([NT])
        lat_sumsq = bit([NT, 2])
        lat_rstd = bit([NT, 2])
        angle = bit([NT, ROPE_HALF])
        turns = bit([NT, ROPE_HALF])
        cos = bit([NT, ROPE_HALF])
        sin = bit([NT, ROPE_HALF])
        inv_freq = bit([ROPE_HALF])
        pos_f = bit([NT])
        warm = bit([1])
        sinks = bit([A_HEADS])
        row_maxes, neg_maxes, dens, sink_es = (bit([2, A_HEADS]) for _ in range(4))
        kr_rot = bit([NT, B_ROPE])
        conv_rows = sb("conv_rows", [CONV_W * 4, P])
        conv_w = bit([CONV_W, 4])
        bn = bit([NT * C_HEADS, 6])
        mv = bit([NT * C_HEADS, 2])
        gn_rstd = bit([NT * C_HEADS])
        top = bit([NT, 8])
        idx_f = bit([NT, 2])
        gap = bit([NT])
        gate1 = bit([NT])
        gate2 = bit([NT])
        pick1 = bit([NT, EXPERTS])
        pick2 = bit([NT, EXPERTS])
        chosen = bit([NT, EXPERTS])
        iota8 = bit([EXPERTS])
        place1 = bit([NT, EXPERTS])
        most = bit([1])
        N_PASS = 2 * EXPERTS + 1
        place = bit([NT, N_PASS])
        share = bit([NT, N_PASS])
        pos_i = sb("pos_i", [P, NT], I32)
        idx_u = sb("idx_u", [P, NT, 8], U32)
        most_i = sb("most_i", [P, 1], I32)
        router = sb("router", [P, KD, EXPERTS])
        router_hi = sb("router_hi", [P, KD, EXPERTS], F32R)
        router_lo = sb("router_lo", [P, KD, EXPERTS], F32R)
        dist = sb("dist", [P, SEQ])
        rope_tmp = sb("rope_tmp", [P, SEQ])

        ps = ctx.enter_context(nc.psum_tensor("ps", [P, 8, HALF], F32))

        raw_landed = [sem(f"raw_landed{i}") for i in range(RING)]
        hi_done = sem("hi_done")
        lo_done = sem("lo_done")
        piece_used = sem("piece_used")
        x_landed = [sem(f"x_landed{t}") for t in range(NT)]
        first_gain_landed = sem("first_gain_landed")
        gain_landed = sem("gain_landed")
        lat_gain_landed = sem("lat_gain_landed")
        gn_gain_landed = sem("gn_gain_landed")
        pos_landed = sem("pos_landed")
        sinks_landed = sem("sinks_landed")
        conv_landed = sem("conv_landed")
        router_landed = sem("router_landed")
        pool_step = sem("pool_step")
        dve_step = sem("dve_step")
        ident_done = sem("ident_done")
        bias_done = sem("bias_done")
        route_consts = sem("route_consts")
        dist_done = sem("dist_done")
        decay_exp = sem("decay_exp")
        freq_done = sem("freq_done")
        angle_done = sem("angle_done")
        trig_done = sem("trig_done")
        tile0_done = sem("tile0_done")
        sumsq_done = sem("sumsq_done")
        inv_done = sem("inv_done")
        rstd_done = sem("rstd_done")
        xn_done = sem("xn_done")
        xnT_done = sem("xnT_done")
        tok_hi_done = sem("tok_hi_done")
        tok_lo_done = sem("tok_lo_done")
        x_updated = sem("x_updated")
        in_act = sem("in_act")
        in_dve = sem("in_dve")
        lat_sq = sem("lat_sq")
        lat_inv = sem("lat_inv")
        lat_std = sem("lat_std")
        lat_done = sem("lat_done")
        latT_done = sem("latT_done")
        latT_hi = sem("latT_hi")
        latT_lo = sem("latT_lo")
        qaT_done = sem("qaT_done")
        qaT_act = sem("qaT_act")
        qaT_dve = sem("qaT_dve")
        ka_doubled = sem("ka_doubled")
        uq_act = sem("uq_act")
        uq_dve = sem("uq_dve")
        ukv_act = sem("ukv_act")
        ukv_dve = sem("ukv_dve")
        rope_done = sem("rope_done")
        kqT_done = sem("kqT_done")
        kqT_act = sem("kqT_act")
        kqT_dve = sem("kqT_dve")
        scored = sem("scored")
        biased = sem("biased")
        max_done = sem("max_done")
        sink_arg = sem("sink_arg")
        exp_done = sem("exp_done")
        probs_done = sem("probs_done")
        pT_done = sem("pT_done")
        pT_act = sem("pT_act")
        pT_dve = sem("pT_dve")
        mixed = sem("mixed")
        mix_hi = sem("mix_hi")
        mix_lo = sem("mix_lo")
        conv_turned = sem("conv_turned")
        odd_act = sem("odd_act")
        odd_dve = sem("odd_dve")
        oddT_done = sem("oddT_done")
        oddT_act = sem("oddT_act")
        oddT_dve = sem("oddT_dve")
        ret_scored = sem("ret_scored")
        dve_conv = sem("dve_conv")
        ret_decayed = sem("ret_decayed")
        ret_out = sem("ret_out")
        gn_inv = sem("gn_inv")
        gn_std = sem("gn_std")
        yr_done = sem("yr_done")
        yrT_done = sem("yrT_done")
        conv_done = sem("conv_done")
        router_hi_done = sem("router_hi_done")
        router_lo_done = sem("router_lo_done")
        logitsT_done = sem("logitsT_done")
        logitsT_out = sem("logitsT_out")
        logits_done = sem("logits_done")
        gap_done = sem("gap_done")
        gap_exp = sem("gap_exp")
        chosen_done = sem("chosen_done")
        counted = sem("counted")
        all_counted = sem("all_counted")
        most_done = sem("most_done")
        pick_done = sem("pick_done")
        gathered = sem("gathered")
        gather_hi = sem("gather_hi")
        gather_lo = sem("gather_lo")
        weigh_done = sem("weigh_done")
        weighT_done = sem("weighT_done")
        weighT_out = sem("weighT_out")
        y_act = sem("y_act")
        y_dve = sem("y_dve")
        scattered = sem("scattered")
        last_act = sem("last_act")
        last_dve = sem("last_dve")
        last_scattered = sem("last_scattered")
        moe_added = sem("moe_added")
        out_ready = sem("out_ready")
        out_stored = sem("out_stored")

        dense = FfnSignals(sem, "dense", NT, gate=(4, 5), up=(6, 7), turned=(6, 7), y=(0, 1, 2, 3))
        moe = FfnSignals(sem, "moe", 1, gate=(2,), up=(3,), turned=(4,), y=(0, 1))
        RET_BANKS, ODD_OUT_BANKS = (3, 6), (1, 2, 3, 6)
        GATHER_BANKS, WEIGHT_BANK, SCATTER_BANKS = (5, 6), 7, (5, 6, 0, 1)


        def in_w(w, j, u):
            return w.rearrange("(u k p) (j n) -> u j p k n", u=2, p=P, n=IN_CHUNK)[u, j]

        def half_w(w, j, u):
            return w.rearrange("(u k p) (j n) -> u j p k n", u=2, p=P, n=HALF)[u, j]

        uq, ukv = g["even_w_uq"][0], g["even_w_ukv"][0]
        first_units = [in_w(g["even_w_in"][0], j, u) for j in range(3) for u in range(2)]
        first_units += [uq[:, 0:HALF].rearrange("(k p) n -> p k n", p=P),
                        uq[:, HALF:].rearrange("(k p) n -> p k n", p=P),
                        ukv.rearrange("(k p) n -> p k n", p=P)]
        first_units += [half_w(g["even_w_out"][0], j, u) for j in range(2) for u in range(2)]
        odd_units = [half_w(g["odd_w_in"][0], j, u) for j in ODD_CHUNKS for u in range(2)]
        odd_units += [half_w(g["odd_w_out"][0], j, u) for j in range(2) for u in (1, 0)]
        first_cols = [2 * IN_CHUNK] * (2 * U_IN) + [2 * HALF, HALF, 2 * 256, 256, PIECE, PIECE] + [PIECE] * (2 * U_OUT)
        assert len(first_units) == FFN_UNIT and len(first_cols) == 2 * FFN_UNIT

        def columns(base):
            return first_cols[base] if base < len(first_cols) else PIECE

        ffn_w = {
            "dense": [g[n] for n in ("even_w_gate", "even_w_up", "even_w_down")],
            "moe": [g[n][0] for n in ("odd_we_gate", "odd_we_up", "odd_we_down")],
        }

        def free(sp, base, laps):
            if base >= RING:
                sp.wait_ge(lo_done, laps * (2 * RING) + 2 * (base - RING) + 2)

        def load(sp, base, laps, src, wait):
            if wait:
                free(sp, base, laps)
            dst = raw[:, base % RING, 0:src.shape[-2] * src.shape[-1]].rearrange("p (k n) -> p k n", n=src.shape[-1])
            if len(src.shape) == 5:
                src = src.rearrange("e c p k n -> p (e c k) n")
            sp.dma_start(dst, src).then_inc(raw_landed[base % RING], 16)

        def gate_up_units(kind, e, c):
            out = []
            for w in ffn_w[kind][0:2]:
                v = w.rearrange("e (u k p) (c n) -> e c u p k n", u=2, p=P, n=HALF)
                out += [v[bass.ds(e, 1), bass.ds(c, 1), u] for u in range(2)]
            return out

        def down_units(kind, e, c):
            v = ffn_w[kind][2].rearrange("e (c u k p) n -> e c u p k n", c=FC, u=2, p=P)
            return [v[bass.ds(e, 1), bass.ds(c, 1), u] for u in range(2)]

        def load_all(sp, units, base, laps=0, together=False):
            if together:
                free(sp, base + len(units) - 1, laps)
            order = reversed(range(len(units))) if together else range(len(units))
            for i in order:
                load(sp, base + i, laps, units[i], not together)

        def split_hi(act, base, laps=0):
            n = columns(base)
            unit, second = base // 2, base % 2
            if not second:
                act.wait_ge(raw_landed[unit % RING], laps * 16 + 16 * (unit // RING + 1))
            if base >= RING:
                act.wait_ge(piece_used, laps * CHUNK_PIECES + base - RING + 1)
            off = columns(base - 1) if second else 0
            act.activation(w_hi[:, base % RING, 0:n], raw[:, unit % RING, off:off + n], ACT.Copy).then_inc(hi_done, 1)

        def split_lo(dve, base, laps=0):
            n = columns(base)
            unit, second = base // 2, base % 2
            off = columns(base - 1) if second else 0
            dve.wait_ge(hi_done, laps * CHUNK_PIECES + base + 1)
            dve.tensor_tensor(w_lo[:, base % RING, 0:n], raw[:, unit % RING, off:off + n],
                              w_hi[:, base % RING, 0:n].bitcast(F32), ALU.subtract).then_inc(lo_done, 1)

        def splitter(split, eng):
            at = [0]

            def until(n):
                while at[0] < n:
                    split(eng, at[0])
                    at[0] += 1

            def skip_to(n):
                at[0] = n
            return until, skip_to

        def multiplied(eng, base, laps=0):
            eng.wait_ge(piece_used, laps * CHUNK_PIECES + base + 1)

        def take(pe, base, laps=0):
            pe.wait_ge(lo_done, laps * CHUNK_PIECES + base + 1)
            return w_hi[:, base % RING, :], w_lo[:, base % RING, :]

        def product(pe, acc, a_hi, a_lo, b_hi, b_lo, start, stop):
            pe.matmul(acc, a_hi, b_hi, start=start, stop=False)
            pe.matmul(acc, a_hi, b_lo, start=False, stop=False)
            return pe.matmul(acc, a_lo, b_hi, start=False, stop=stop)

        def weight_product(pe, base, laps, banks, kts, n, left, tiles, first, last):
            b_hi, b_lo = take(pe, base, laps)
            for t in range(tiles):
                for i, kt in enumerate(kts):
                    a_hi, a_lo = left(kt, t)
                    mm = product(pe, ps[:, banks[t], 0:n], a_hi, a_lo,
                                 b_hi[:, i * n:(i + 1) * n], b_lo[:, i * n:(i + 1) * n],
                                 start=first and i == 0, stop=last and i == len(kts) - 1)
            mm.then_inc(piece_used, 1)
            return mm

        def tokens(kt, t):
            return tok_hi[:, kt, t * P:(t + 1) * P], tok_lo[:, kt, t * P:(t + 1) * P]

        def turn(pe, bank, col, src, rows=P):
            return pe.transpose(ps[0:rows, bank, col:col + P], src, ident[:, :])

        def norm_order(stage):
            return [(0, 0), (1, 0), (0, 1), (1, 1)] if stage in (1, 3) else [(0, 0), (0, 1), (1, 0), (1, 1)]

        PROBS_ORDER = [(i, b) for i in range(4) for b in range(2 * (i % 2 + 1))]

        def copied_by_act(inst, b):
            return inst == 0 or (inst != 2 and b % 2 == 0)

        def copies(inst, b):
            same = [copied_by_act(*ib) == copied_by_act(inst, b) for ib in PROBS_ORDER]
            return sum(same[0:PROBS_ORDER.index((inst, b)) + 1])

        flat_ps = ps[:, :, :].rearrange("p b n -> p (b n)")

        block = ctx.enter_context(nc.Block())

        @block.sync
        def _(sp):
            for t in range(NT):
                sp.dma_start(x[:, t, :], g["x"][0, t * P:(t + 1) * P, :]).then_inc(x_landed[t], 16)
            sp.dma_start(gain[:, :], g["even_norm_mix"][0].partition_broadcast(P)).then_inc(first_gain_landed, 16)
            load_all(sp, first_units, 0)

            load_all(sp, gate_up_units("dense", 0, 0), FFN_UNIT)
            load_all(sp, gate_up_units("dense", 0, 1), FFN_UNIT + GATE_UNITS)
            load_all(sp, down_units("dense", 0, 0), FFN_UNIT + 2 * GATE_UNITS)
            loop_base = GATE_UNITS + CHUNK_UNITS
            with sp.Fori(LOOP_FIRST, FC) as c:
                load_all(sp, gate_up_units("dense", 0, c), FFN_UNIT + loop_base, c - LOOP_FIRST)
                load_all(sp, down_units("dense", 0, c - 1), FFN_UNIT + loop_base + GATE_UNITS, c - LOOP_FIRST)
            load_all(sp, down_units("dense", 0, FC - 1), FFN_UNIT + PASS_UNITS - DOWN_UNITS)

            load_all(sp, odd_units, ODD_UNIT)

            load_all(sp, gate_up_units("moe", 0, 0), MOE_UNIT)

            def passes(lo, hi):
                with sp.Fori(lo, hi) as p:
                    lap = p * FC
                    e = p if lo == 0 else p - EXPERTS
                    load_all(sp, gate_up_units("moe", e, 1), MOE_UNIT + GATE_UNITS, lap)
                    load_all(sp, down_units("moe", e, 0), MOE_UNIT + 2 * GATE_UNITS, lap, True)
                    with sp.Fori(LOOP_FIRST, FC) as c:
                        load_all(sp, gate_up_units("moe", e, c), MOE_UNIT + loop_base, lap + c - LOOP_FIRST)
                        load_all(sp, down_units("moe", e, c - 1), MOE_UNIT + loop_base + GATE_UNITS, lap + c - LOOP_FIRST)
                    load_all(sp, down_units("moe", e, FC - 1), MOE_UNIT + PASS_UNITS - DOWN_UNITS, lap)
                    nxt = (e + 1) % EXPERTS
                    load_all(sp, gate_up_units("moe", nxt, 0), MOE_UNIT + PASS_UNITS, lap)

            def quiet(n_pass):
                for i in range(RING):
                    last = max(n for n in range(MOE_UNIT + n_pass * PASS_UNITS + GATE_UNITS) if n % RING == i)
                    sp.wait_ge(raw_landed[i], 16 * (last // RING + 1))

            passes(0, EXPERTS)
            quiet(EXPERTS)
            sp.wait_ge(most_done, 1)
            full = sp.value_load(most_i[0:1, 0:1])
            with sp.If(full > SLOTS):
                passes(EXPERTS, 2 * EXPERTS)
                quiet(2 * EXPERTS)
            for t in range(NT):
                sp.wait_ge(out_ready, t + 1)
                sp.dma_start(out[0, t * P:(t + 1) * P, :], xn[:, t, :]).then_inc(out_stored, 16)
            sp.wait_ge(out_stored, 16 * NT)

        @block.gpsimd
        def _(pool):
            step = [0]

            def link(ins):
                step[0] += 1
                ins.then_inc(pool_step, 1)
                pool.wait_ge(pool_step, step[0])

            def load_gain(stage, row):
                pool.wait_ge(xn_done, NT * stage)
                pool.dma_start(gain[:, :], row.partition_broadcast(P)).then_inc(gain_landed, 16)

            link(pool.memset(ident[:, :], 0.0))
            pool.affine_select(out=ident[:, :], in_=ident[:, :], compare_op=ALU.not_equal, fill=1.0, base=0,
                               pattern=[[-1, P]], channel_multiplier=1).then_inc(ident_done, 1)
            pool.dma_start(pos_i[:, :], g["positions"][0].rearrange("(t p) -> p t", p=P),
                           allow_slow_non_contiguous=True).then_inc(pos_landed, 16)
            pool.dma_start(lat_gain[:, 0:Q_LORA], g["even_q_norm"][0].partition_broadcast(P)).then_inc(lat_gain_landed, 16)
            pool.dma_start(lat_gain[:, Q_LORA:], g["even_kv_norm"][0].partition_broadcast(P)).then_inc(lat_gain_landed, 16)
            pool.dma_start(sinks, g["even_sinks"][0].partition_broadcast(P)).then_inc(sinks_landed, 16)
            pool.dma_start(conv_rows[:, :], g["odd_conv_w"][0].rearrange("j (k p) -> (j k) p", p=P)).then_inc(conv_landed, 16)
            pool.dma_start(router[:, :, :], g["odd_router"][0].rearrange("(k p) e -> p k e", p=P)).then_inc(router_landed, 16)
            for i in range(ROPE_HALF):
                f = float(np.float32(ROPE_THETA) ** (-np.float32(2 * i) / np.float32(B_ROPE)))
                ins = pool.memset(inv_freq[:, i:i + 1], f)
            ins.then_inc(freq_done, 1)
            link(pool.iota(dist[:, :], pattern=[[-1, SEQ]], base=P, channel_multiplier=1, allow_small_or_imprecise_dtypes=True))
            link(pool.tensor_scalar(rope_tmp[:, 0:SEQ], dist[:, :], 0.0, 2.0, ALU.max, ALU.mult))
            link(pool.tensor_tensor(dist[:, :], rope_tmp[:, 0:SEQ], dist[:, :], ALU.subtract))
            link(pool.memset(dist[0:CHUNK, SEQ - CHUNK:SEQ], MASKED))
            link(pool.memset(dist[CHUNK:P, 0:CHUNK], MASKED))
            for h in range(A_HEADS):
                slope = 2.0 ** (-8.0 * (h + 1) / A_HEADS)
                ins = pool.tensor_scalar(bias[:, (h % 2) * 4 + h // 2, :], dist[:, :], -slope / A_SCALE, None, ALU.mult)
            ins.then_inc(bias_done, 1)
            pool.wait_ge(bias_done, 1)
            link(pool.iota(dist[:, :], pattern=[[1, SEQ]], base=0, channel_multiplier=-1, allow_small_or_imprecise_dtypes=True))
            pool.affine_select(out=dist[:, :], in_=dist[:, :], compare_op=ALU.is_ge, fill=1.0e6, base=0,
                               pattern=[[1, SEQ]], channel_multiplier=-1).then_inc(dist_done, 1)
            load_gain(1, g["even_norm_ffn"][0])

            pool.wait_ge(in_act, 3)
            pool.wait_ge(in_dve, 3)
            pool.wait_ge(trig_done, 2)
            tmp = rope_tmp[:, 0:NT * ROPE_HALF].rearrange("p (t n) -> p t n", t=NT)
            k1, k2 = proj[:, :, COL_KR:COL_KR + ROPE_HALF], proj[:, :, COL_KR + ROPE_HALF:EVEN_IN]
            r1, r2 = kr_rot[:, :, 0:ROPE_HALF], kr_rot[:, :, ROPE_HALF:]
            pool.tensor_tensor(r1, k1, cos, ALU.mult)
            link(pool.tensor_tensor(tmp, k2, sin, ALU.mult))
            link(pool.tensor_tensor(r1, r1, tmp, ALU.subtract))
            pool.tensor_tensor(r2, k2, cos, ALU.mult)
            link(pool.tensor_tensor(tmp, k1, sin, ALU.mult))
            link(pool.tensor_tensor(r2, r2, tmp, ALU.add))
            for t in range(NT):
                pool.tensor_copy(k96[:, t, :, B_NOPE:], kr_rot[:, t, None, :].to_broadcast([P, B_HEADS, B_ROPE]))
            pool.wait_ge(lat_done, 2 * NT)
            pool.dma_start(gn_gain, g["odd_ret_gn"][0].partition_broadcast(P)).then_inc(gn_gain_landed, 16)
            pool.wait_ge(uq_act, 2)
            pool.wait_ge(uq_dve, 2)
            for t in range(NT):
                n = B_HEADS * ROPE_HALF
                a, b = (rope_tmp[:, i * n:(i + 1) * n].rearrange("p (h n) -> p h n", h=B_HEADS) for i in range(2))
                q1 = q96[:, t, :, B_NOPE:B_NOPE + ROPE_HALF]
                q2 = q96[:, t, :, B_NOPE + ROPE_HALF:]
                cs = cos[:, t, None, :].to_broadcast([P, B_HEADS, ROPE_HALF])
                sn = sin[:, t, None, :].to_broadcast([P, B_HEADS, ROPE_HALF])
                pool.tensor_tensor(a, q2, sn, ALU.mult)
                link(pool.tensor_tensor(b, q1, sn, ALU.mult))
                pool.tensor_tensor(q1, q1, cs, ALU.mult)
                link(pool.tensor_tensor(q2, q2, cs, ALU.mult))
                pool.tensor_tensor(q1, q1, a, ALU.subtract)
                ins = pool.tensor_tensor(q2, q2, b, ALU.add)
                if t < NT - 1:
                    link(ins)
            ins.then_inc(rope_done, 1)
            pool.wait_ge(mix_lo, 4)
            link(pool.memset(ones, 1.0))
            pool.affine_select(out=before, in_=ones, compare_op=ALU.is_gt, fill=0.0, base=0,
                               pattern=[[1, P]], channel_multiplier=-1)
            pool.iota(iota8, pattern=[[1, EXPERTS]], base=0, channel_multiplier=0, allow_small_or_imprecise_dtypes=True)
            pool.iota(iota_slot, pattern=[[1, SLOTS]], base=0, channel_multiplier=0,
                      allow_small_or_imprecise_dtypes=True).then_inc(route_consts, 1)
            load_gain(2, g["odd_norm_mix"][0])
            load_gain(3, g["odd_norm_ffn"][0])
            load_gain(4, g["final_norm"])

        @block.tensor
        def _(pe):
            pe.wait_ge(ident_done, 1)

            def norm_turn(stage, t):
                pe.wait_ge(xn_done, NT * stage + t + 1)
                for half in range(2):
                    for i in range(4):
                        kt = 4 * half + i
                        mm = turn(pe, 2 * t + half, i * P, xn[:, t, kt * P:(kt + 1) * P])
                    mm.then_inc(xnT_done, 1)

            def first_product(stage, base, banks, n):
                norm_turn(stage, 0)
                for t in range(NT):
                    for u in range(4):
                        if t == 0 and u == (2 if stage else 0):
                            norm_turn(stage, 1)
                        b_hi, b_lo = take(pe, base + u)
                        if u % 2 == 0:
                            pe.wait_ge(tok_lo_done, 4 * stage + 2 * t + u // 2 + 1)
                        for i in range(2):
                            a_hi, a_lo = tokens(2 * u + i, t)
                            mm = product(pe, ps[:, banks[t], 0:n], a_hi, a_lo, b_hi[:, i * n:(i + 1) * n],
                                         b_lo[:, i * n:(i + 1) * n], start=(u == 0 and i == 0), stop=(u == 3 and i == 1))
                        if t == NT - 1:
                            mm.then_inc(piece_used, 1)

            in_banks = [(4, 5), (6, 7), (0, 1)]
            first_product(0, 0, in_banks[0], IN_CHUNK)
            for j in range(1, 3):
                for u in range(4):
                    mm = weight_product(pe, 4 * j + u, 0, in_banks[j], (2 * u, 2 * u + 1), IN_CHUNK, tokens, NT,
                                        u == 0, u == 3)

            pe.wait_ge(in_act, 3)
            pe.wait_ge(in_dve, 3)
            for t in range(NT):
                for j in range(4):
                    mm = turn(pe, 2 + t, j * P, proj[:, t, j * P:(j + 1) * P])
                mm.then_inc(qaT_done, 1)
            pe.wait_ge(ka_doubled, 1)
            for t in range(NT):
                for kv in range(A_KV):
                    mm = turn(pe, 4, kv * SEQ + t * P, ka_twice[:, t, kv * P:(kv + 1) * P])
            mm.then_inc(qaT_done, 1)
            def scores_a(t):
                nk = P * (t + 1)
                per = HALF // nk
                for h in range(A_HEADS):
                    pos = (h % 2) * 4 + h // 2
                    off = (h % 2) * A_DIM
                    mm = pe.matmul(ps[:, SCORE_BANK[t] + pos // per, (pos % per) * nk:(pos % per + 1) * nk],
                                   qaT[off:off + A_DIM, h // 2, t * P:(t + 1) * P],
                                   kaT[off:off + A_DIM, h // 4, 0:nk], start=True, stop=True)
                mm.then_inc(scored, 1)

            def scores_b(t):
                nk = P * (t + 1)
                per = HALF // nk
                for h in range(B_HEADS):
                    mm = pe.matmul(ps[:, SCORE_BANK[2 + t] + h // per, (h % per) * nk:(h % per + 1) * nk],
                                   qbT[0:B_DIM, h, t * P:(t + 1) * P], kbT[0:B_DIM, h, 0:nk], start=True, stop=True)
                mm.then_inc(scored, 1)

            def attend(inst):
                kind, t = "AABB"[inst], inst % 2
                pe.wait_ge(probs_done, inst + 1)
                n_banks = 2 * (t + 1)
                for b in range(n_banks):
                    for i in range(4):
                        block_no = 4 * b + i
                        mm = turn(pe, PROBS_BANKS[inst][b], i * P, probs_of[inst][:, block_no * P:(block_no + 1) * P])
                    mm.then_inc(pT_done, 1)
                for b in range(n_banks - 2, n_banks):
                    pe.wait_ge(pT_act if copied_by_act(inst, b) else pT_dve, copies(inst, b))
                for h in range(8):
                    pos = (h % 2) * 4 + h // 2 if kind == "A" else h
                    off = (h % 2) * 64
                    for kk in range(t + 1):
                        v = (proj[:, kk, COL_V + (h // 4) * A_DIM:COL_V + (h // 4 + 1) * A_DIM] if kind == "A"
                             else v64[:, kk, h, :])
                        at = pos * (t + 1) + kk
                        mm = pe.matmul(ps[off:off + 64, MIXED_BANK[inst], (h // 2) * P:(h // 2 + 1) * P], v,
                                       probsT_of[inst][at // 4][:, (at % 4) * P:(at % 4 + 1) * P],
                                       start=(kk == 0), stop=(kk == t))
                mm.then_inc(mixed, 1)

            pe.wait_ge(qaT_act, 1)
            pe.wait_ge(qaT_dve, 2)
            scores_a(0)
            scores_a(1)
            pe.wait_ge(lat_done, 2 * NT)
            for t in range(NT):
                for j in range(3):
                    mm = turn(pe, 6 + t, j * P, proj[:, t, COL_CQ + j * P:COL_CQ + (j + 1) * P])
                mm.then_inc(latT_done, 1)
            pe.wait_ge(biased, 1)
            for t in range(NT):
                for j in range(2):
                    mm = turn(pe, 0, j * SEQ + t * P, proj[:, t, COL_CKV + j * P:COL_CKV + (j + 1) * P])
            mm.then_inc(latT_done, 1)
            pe.wait_ge(latT_lo, 3)

            def latent_q(kt, t):
                return fT_hi[:, kt, t * P:(t + 1) * P], fT_lo[:, kt, t * P:(t + 1) * P]

            def latent_kv(kt, t):
                return latkv_hi[:, kt, t * P:(t + 1) * P], latkv_lo[:, kt, t * P:(t + 1) * P]

            p0 = 2 * U_IN
            weight_product(pe, p0, 0, (6, 7), (0, 1), HALF, latent_q, NT, True, False)
            weight_product(pe, p0 + 1, 0, (6, 7), (2,), HALF, latent_q, NT, False, True)
            weight_product(pe, p0 + 2, 0, (0, 1), (0, 1), 256, latent_q, NT, True, False)
            weight_product(pe, p0 + 3, 0, (0, 1), (2,), 256, latent_q, NT, False, True)
            pe.wait_ge(biased, 2)
            for i in range(2):
                b_hi, b_lo = take(pe, p0 + 4 + i)
                for t in range(NT):
                    a_hi, a_lo = latent_kv(i, t)
                    for half in range(2):
                        mm = product(pe, ps[:, 2 + 2 * t + half, :], a_hi, a_lo,
                                     b_hi[:, half * HALF:(half + 1) * HALF], b_lo[:, half * HALF:(half + 1) * HALF],
                                     start=(i == 0), stop=(i == 1))
                mm.then_inc(piece_used, 1)
            pe.wait_ge(uq_act, 2)
            pe.wait_ge(uq_dve, 2)
            attend(0)
            pe.wait_ge(ukv_act, 1)
            pe.wait_ge(ukv_dve, 1)
            attend(1)
            pe.wait_ge(rope_done, 1)
            for i in range(8):
                src = q96 if i < 4 else k96
                t, h0 = (i % 4) // 2, (i % 2) * 4
                bank = 2 + i % 4
                if i >= 4:
                    pe.wait_ge(kqT_act if i % 2 == 0 else kqT_dve, (i - 4) // 2 + 1)
                for k in range(4):
                    mm = turn(pe, bank, k * P, src[:, t, h0 + k, :], rows=B_DIM)
                mm.then_inc(kqT_done, 1)
            pe.wait_ge(kqT_act, 4)
            pe.wait_ge(kqT_dve, 4)
            scores_b(0)
            pe.wait_ge(mix_lo, 2)
            scores_b(1)

            def output_projection(base, banks, units, second_half, k_order=range(KD), left=tokens):
                for u in units:
                    weight_product(pe, base + u, 0, banks[0:2], k_order[2 * u:2 * u + 2], HALF, left, NT, u == 0, u == 3)
                if not second_half:
                    return
                for t in range(NT):
                    for u in range(4):
                        b_hi, b_lo = take(pe, base + 4 + u)
                        for i in range(2):
                            a_hi, a_lo = left(k_order[2 * u + i], t)
                            mm = product(pe, ps[:, banks[2 + t], :], a_hi, a_lo, b_hi[:, i * HALF:(i + 1) * HALF],
                                         b_lo[:, i * HALF:(i + 1) * HALF], start=(u == 0 and i == 0),
                                         stop=(u == 3 and i == 1))
                        if t == NT - 1:
                            mm.then_inc(piece_used, 1)
                    if t == 0:
                        mm.then_inc(tile0_done, 1)

            even_out = 2 * (U_IN + U_UQ + U_UKV)
            output_projection(even_out, EVEN_OUT_BANKS, (0, 1), False)
            attend(2)
            attend(3)
            pe.wait_ge(mix_lo, 4)
            output_projection(even_out, EVEN_OUT_BANKS, (2, 3), True)

            def gate_up(sig, q, base, laps, which, middle=None):
                tiles = sig.tiles
                banks = sig.gate_banks if which == 0 else sig.up_banks
                for u in range(4):
                    if u == 2 and middle is not None:
                        middle()
                    weight_product(pe, base + 4 * which + u, laps, banks, (2 * u, 2 * u + 1), HALF, tokens, tiles,
                                   u == 0, u == 3)

            def turn_hidden(sig, q):
                for t in range(sig.tiles):
                    pe.wait_ge(sig.act_done, q * sig.tiles + t + 1)
                    for i in range(4):
                        mm = turn(pe, sig.turned_banks[t], i * P, hid[:, t, i * P:(i + 1) * P])
                    mm.then_inc(sig.turned, 1)

            def down(sig, q, base, laps, first, last):
                pe.wait_ge(sig.turned_lo, (q + 1) * sig.tiles)
                for kt in range(4):
                    b_hi, b_lo = take(pe, base + kt, laps)
                    for t in range(sig.tiles):
                        a_hi, a_lo = fT_hi[:, kt, t * P:(t + 1) * P], fT_lo[:, kt, t * P:(t + 1) * P]
                        for half in range(2):
                            mm = product(pe, ps[:, sig.y_banks[2 * t + half], :], a_hi, a_lo,
                                         b_hi[:, half * HALF:(half + 1) * HALF],
                                         b_lo[:, half * HALF:(half + 1) * HALF],
                                         start=first and kt == 0, stop=last and kt == 3)
                    mm.then_inc(piece_used, 1)

            def ffn(sig, q, base, lap, between, before_last, middle=None):
                if sig.tiles == 1:
                    gate_up(sig, q, base, lap, 0, middle)
                gate_up(sig, q, base, lap, 1)
                between()
                at = base + 2 * GATE_UNITS
                if sig.tiles == NT:
                    pe.wait_ge(sig.silu_done, (q + 1) * sig.tiles)
                    gate_up(sig, q + 1, at, lap, 0, lambda: turn_hidden(sig, q))
                else:
                    turn_hidden(sig, q)
                    gate_up(sig, q + 1, at, lap, 0)
                if sig.tiles == NT:
                    pe.wait_ge(sig.turned_lo, (q + 1) * sig.tiles)
                gate_up(sig, q + 1, at, lap, 1)
                down(sig, q, at + 2 * GATE_UNITS, lap, True, False)
                turn_hidden(sig, q + 1)
                at += CHUNK_PIECES
                with pe.Fori(LOOP_FIRST, FC) as c:
                    laps = lap + c - LOOP_FIRST
                    gate_up(sig, q + c, at, laps, 0)
                    if sig.tiles == NT:
                        pe.wait_ge(sig.turned_lo, (q + c) * sig.tiles)
                    gate_up(sig, q + c, at, laps, 1)
                    down(sig, q + c - 1, at + 2 * GATE_UNITS, laps, False, False)
                    turn_hidden(sig, q + c)
                before_last()
                at = base + PASS_PIECES - 2 * DOWN_UNITS
                if sig.tiles == 1:
                    down(sig, q + FC - 1, at, lap, False, True)
                    return
                for t in range(NT):
                    pe.wait_ge(sig.turned_lo, (q + FC) * NT - 1 + t)
                    for kt in range(4):
                        b_hi, b_lo = take(pe, at + kt, lap)
                        a_hi, a_lo = fT_hi[:, kt, t * P:(t + 1) * P], fT_lo[:, kt, t * P:(t + 1) * P]
                        for half in range(2):
                            mm = product(pe, ps[:, sig.y_banks[2 * t + half], :], a_hi, a_lo,
                                         b_hi[:, half * HALF:(half + 1) * HALF],
                                         b_lo[:, half * HALF:(half + 1) * HALF], start=False, stop=kt == 3)
                        if t == NT - 1:
                            mm.then_inc(piece_used, 1)
                    if t == 0:
                        mm.then_inc(tile0_done, 1)

            first_product(1, 2 * FFN_UNIT, dense.gate_banks, HALF)
            ffn(dense, 0, 2 * FFN_UNIT, 0, lambda: None, lambda: None)

            def turn_odd(i, src, t):
                for k in range(4):
                    mm = turn(pe, i % 4, k * P, src[:, t, k * P:(k + 1) * P])
                mm.then_inc(oddT_done, 1)

            def turn_conv_rows():
                pe.wait_ge(conv_landed, 16)
                pe.transpose(ps[:, 0, 0:CONV_W * 4], conv_rows[:, :],
                             ident[0:CONV_W * 4, 0:CONV_W * 4]).then_inc(conv_turned, 1)

            def turn_conv():
                pe.wait_ge(dve_conv, 1)
                pe.wait_ge(odd_act, 2)
                pe.wait_ge(odd_dve, 3)
                for i in range(4):
                    turn_odd(i, bc_nat[:, i // 2], i % 2)

            def turn_q():
                pe.wait_ge(odd_act, 3)
                pe.wait_ge(odd_dve, 4)
                pe.wait_ge(oddT_act, 1)
                pe.wait_ge(oddT_dve, 1)
                for i in range(2):
                    turn_odd(i, qk_nat[:, 0], i)

            def turn_k():
                pe.wait_ge(odd_act, 4)
                pe.wait_ge(odd_dve, 5)
                pe.wait_ge(oddT_act, 2)
                pe.wait_ge(oddT_dve, 2)
                for i in range(2):
                    turn_odd(2 + i, qk_nat[:, 1], i)

            def retention_scores():
                pe.wait_ge(oddT_act, 4)
                pe.wait_ge(oddT_dve, 4)
                for h in range(C_HEADS):
                    mm = pe.matmul(ps[:, h // 2, (h % 2) * SEQ:(h % 2 + 1) * SEQ], kT[:, h, 0:P], qT[:, h, :],
                                   start=True, stop=True)
                    if h % 2:
                        mm.then_inc(ret_scored, 1)
                for h in range(C_HEADS):
                    mm = pe.matmul(ps[:, 2, h * P:(h + 1) * P], kT[:, h, P:SEQ], qT[:, h, P:SEQ], start=True, stop=True)
                mm.then_inc(ret_scored, 1)

            def retention_values():
                pe.wait_ge(odd_act, 5)
                pe.wait_ge(odd_dve, 6)
                for t in range(NT):
                    pe.wait_ge(ret_decayed, 2 if t == 0 else 3)
                    for h in range(C_HEADS):
                        for kk in range(t + 1):
                            a = sT0[:, h, t * P:(t + 1) * P] if kk == 0 else sT1[:, h, :]
                            mm = pe.matmul(ps[:, RET_BANKS[t], h * P:(h + 1) * P], a, val[:, kk, h, :],
                                           start=(kk == 0), stop=(kk == t))
                    mm.then_inc(ret_out, 1)

            between = {(1, 1): turn_conv_rows, (3, 1): turn_conv, (4, 1): turn_q, (5, 1): turn_k, (5, 3): retention_scores, (6, 1): retention_values}
            first_product(2, 2 * ODD_UNIT, (4, 5), HALF)
            for j in range(1, ODD_IN_CHUNKS):
                if j >= 2:
                    pe.wait_ge(odd_act, (1, 2, 2, 3, 4)[j - 2])
                    pe.wait_ge(odd_dve, j - 1)
                for u in range(4):
                    if (j, u) in between:
                        between[j, u]()
                    weight_product(pe, 2 * ODD_UNIT + 4 * j + u, 0, ((4, 5), (6, 7))[j % 2],
                                   (2 * u, 2 * u + 1), HALF, tokens, NT, u == 0, u == 3)

            def odd_mixed(kt, t):
                if kt < 4:
                    return tokens(kt, t)
                return fT_hi[:, kt - 4, t * P:(t + 1) * P], fT_lo[:, kt - 4, t * P:(t + 1) * P]

            odd_out = 2 * (ODD_UNIT + 2 * ODD_IN_CHUNKS)
            k_order = (4, 5, 6, 7, 0, 1, 2, 3)
            pe.wait_ge(mix_lo, 5)
            output_projection(odd_out, ODD_OUT_BANKS, (0,), False, k_order, odd_mixed)
            for t in range(NT):
                pe.wait_ge(yr_done, t + 1)
                for k in range(4):
                    mm = turn(pe, (7, 0)[t], k * P, yr[:, t, k * P:(k + 1) * P])
                mm.then_inc(yrT_done, 1)
            output_projection(odd_out, ODD_OUT_BANKS, (1,), False, k_order, odd_mixed)
            pe.wait_ge(mix_lo, 7)
            output_projection(odd_out, ODD_OUT_BANKS, (2, 3), True, k_order, odd_mixed)

            for t in range(NT):
                norm_turn(3, t)
            pe.wait_ge(router_lo_done, 1)
            for kt in range(KD):
                if kt % 4 == 0:
                    pe.wait_ge(tok_lo_done, 12 + 3 + kt // 4)
                mm = product(pe, ps[0:EXPERTS, 4, 0:SEQ], router_hi[:, kt, :], router_lo[:, kt, :], tok_hi[:, kt, :],
                             tok_lo[:, kt, :], start=(kt == 0), stop=(kt == KD - 1))
            mm.then_inc(logitsT_done, 1)
            pe.wait_ge(logitsT_out, 1)
            for t in range(NT):
                mm = pe.transpose(ps[:, 5, t * EXPERTS:(t + 1) * EXPERTS], logits_T[:, t * P:(t + 1) * P],
                                  ident[0:EXPERTS, 0:EXPERTS])
            mm.then_inc(logits_done, 1)
            pe.wait_ge(chosen_done, 1)
            pe.wait_ge(route_consts, 1)
            pe.matmul(ps[:, 7, 0:EXPERTS], before, chosen[:, 0, :], start=True, stop=True)
            pe.matmul(ps[:, 7, EXPERTS:2 * EXPERTS], ones, chosen[:, 0, :], start=True, stop=False)
            pe.matmul(ps[:, 7, EXPERTS:2 * EXPERTS], before, chosen[:, 1, :], start=False, stop=True).then_inc(counted, 1)
            pe.matmul(ps[:, 4, 0:EXPERTS], ones, chosen[:, 0, :], start=True, stop=False)
            pe.matmul(ps[:, 4, 0:EXPERTS], ones, chosen[:, 1, :], start=False,
                      stop=True).then_inc(all_counted, 1)

            def gather(p):
                pe.wait_ge(pick_done, p + 1)
                for kt in range(KD):
                    for t in range(NT):
                        mm = pe.matmul(ps[:, GATHER_BANKS[kt // 4], (kt % 4) * SLOTS:(kt % 4 + 1) * SLOTS],
                                       xn[:, t, kt * P:(kt + 1) * P], pick[:, t, :], start=(t == 0), stop=(t == NT - 1))
                    if kt % 4 == 3:
                        mm.then_inc(gathered, 1)

            def turn_weights(p):
                pe.wait_ge(weigh_done, p + 1)
                for t in range(NT):
                    mm = turn(pe, WEIGHT_BANK, t * P, weigh[:, t, :])
                mm.then_inc(weighT_done, 1)

            def scatter(done):
                for t in range(NT):
                    for half in range(2):
                        pe.matmul(ps[:, SCATTER_BANKS[2 * t + half], :], weigh_T[:, t * P:(t + 1) * P],
                                  y_sb[:, half * HALF:(half + 1) * HALF], start=True, stop=True).then_inc(done, 1)

            def scatter_before(p):
                pe.wait_ge(weighT_out, p + 1)
                pe.wait_ge(y_act, p + 1)
                pe.wait_ge(y_dve, p + 1)
                scatter(scattered)

            def late(p):
                turn_weights(p)
                gather(p + 1)

            def passes(lo, hi):
                with pe.Fori(lo, hi) as p:
                    pe.wait_ge(gather_lo, 2 * p + 1)
                    ffn(moe, p * FC, 2 * MOE_UNIT, p * FC, lambda: scatter_before(p), lambda: late(p),
                        lambda: pe.wait_ge(gather_lo, 2 * p + 2))

            gather(0)
            passes(0, EXPERTS)
            pe.wait_ge(most_done, 1)
            full = pe.value_load(most_i[0:1, 0:1])
            with pe.If(full > SLOTS):
                passes(EXPERTS, 2 * EXPERTS)
            pe.wait_ge(last_act, 1)
            pe.wait_ge(last_dve, 1)
            scatter(last_scattered)

        @block.scalar
        def _(act):
            split_until, split_skip = splitter(split_hi, act)

            def square(stage, t, half):
                if stage == 0:
                    act.wait_ge(x_landed[t], 16)
                else:
                    act.wait_ge(x_updated, 4 * (stage - 1) + norm_order(stage).index((t, half)) + 1)
                at = (2 * t + half) * HALF
                scratch = spare[:, at:at + HALF] if stage < 4 else final_scratch[:, t, half, :]
                act.activation(scratch, x[:, t, half * HALF:(half + 1) * HALF], ACT.Square,
                               accum_out=sumsq[:, t, half:half + 1]).then_inc(sumsq_done, 1)

            def norm_root(stage, t):
                act.wait_ge(inv_done, NT * stage + t + 1)
                act.activation(rstd[:, t:t + 1], inv[:, t:t + 1], ACT.Sqrt, scale=float(D)).then_inc(rstd_done, 1)

            def norm_hi(stage, t):
                for half in range(2):
                    act.wait_ge(xnT_done, 4 * stage + 2 * t + half + 1)
                    act.activation(tok_hi[:, 4 * half:4 * half + 4, t * P:(t + 1) * P],
                                   ps[:, 2 * t + half, :].rearrange("p (k n) -> p k n", k=4), ACT.Copy).then_inc(tok_hi_done, 1)

            def norm(stage, base):
                squares = norm_order(stage)
                first = squares.index((0, 1)) + 1
                for t, half in squares[0:first]:
                    square(stage, t, half)
                norm_root(stage, 0)
                split_until(base + 4)
                if stage < 3:
                    norm_hi(stage, 0)
                for t, half in squares[first:]:
                    square(stage, t, half)
                norm_root(stage, 1)
                if stage < 3:
                    split_until(base + 5)
                else:
                    norm_hi(stage, 0)
                norm_hi(stage, 1)
                split_until(base + AHEAD)

            act.wait_ge(ident_done, 1)
            act.activation(warm, ident[:, 0:1], ACT.Sqrt)
            for t in range(NT):
                square(0, t, 0)
                square(0, t, 1)
                norm_root(0, t)
            for t in range(NT):
                split_until(1 + t)
                norm_hi(0, t)
            split_until(AHEAD)
            act.wait_ge(angle_done, 1)
            act.activation(sin, angle, ACT.Sin).then_inc(trig_done, 1)
            act.activation(cos, turns, ACT.Sin).then_inc(trig_done, 1)
            in_banks = (4, 6, 0)
            for j in range(3):
                multiplied(act, 4 * j + 3)
                act.activation(proj[:, 0, j * IN_CHUNK:(j + 1) * IN_CHUNK], ps[:, in_banks[j], 0:IN_CHUNK],
                               ACT.Copy).then_inc(in_act, 1)
                if j < 2:
                    split_until(4 * (j + 1) + AHEAD)
            act.wait_ge(in_dve, 3)
            act.wait_ge(in_act, 3)
            for t in range(NT):
                for i, (at, n) in enumerate(((COL_CQ, Q_LORA), (COL_CKV, KV_LORA))):
                    scratch = spare[:, t * D + i * HALF:t * D + i * HALF + n]
                    ins = act.activation(scratch, proj[:, t, at:at + n], ACT.Square,
                                         accum_out=lat_sumsq[:, t, i:i + 1])
                if t == 0:
                    act.wait_ge(qaT_done, 1)
                    act.activation(qaT[:, :, 0:P], ps[:, 2, :].rearrange("p (k n) -> p k n", k=4),
                                   ACT.Copy).then_inc(qaT_act, 1)
            ins.then_inc(lat_sq, 1)
            act.wait_ge(lat_inv, 1)
            act.activation(lat_rstd, lat_rstd, ACT.Sqrt).then_inc(lat_std, 1)
            split_until(2 * (U_IN + U_UQ + U_UKV))

            def exps(inst):
                kind, nk = "AABB"[inst], P * (inst % 2 + 1)
                neg_max, den, sink_e = (v[:, inst % 2, :] for v in (neg_maxes, dens, sink_es))
                act.wait_ge(max_done, inst + 1)
                scale = A_SCALE if kind == "A" else B_SCALE
                probs = probs_of[inst]
                src = probs if kind == "A" else flat_ps[:, SCORE_BANK[inst] * HALF:]
                for pos in range(8):
                    ins = act.activation(probs[:, pos * nk:(pos + 1) * nk], src[:, pos * nk:(pos + 1) * nk], ACT.Exp,
                                         bias=neg_max[:, pos:pos + 1], scale=scale, accum_out=den[:, pos:pos + 1])
                if kind == "A":
                    act.wait_ge(sink_arg, inst + 1)
                    ins = act.activation(sink_e, sink_e, ACT.Exp)
                ins.then_inc(exp_done, 1)

            def probs_out(inst):
                for b in range(2 * (inst % 2 + 1)):
                    if copied_by_act(inst, b):
                        act.wait_ge(pT_done, PROBS_ORDER.index((inst, b)) + 1)
                        act.activation(probsT_of[inst][b], ps[:, PROBS_BANKS[inst][b], :], ACT.Copy).then_inc(pT_act, 1)

            def mix_out(inst):
                k0, t = 4 * (inst // 2), inst % 2
                act.wait_ge(mixed, inst + 1)
                act.activation(tok_hi[:, k0:k0 + 4, t * P:(t + 1) * P],
                               ps[:, MIXED_BANK[inst], :].rearrange("p (k n) -> p k n", k=4), ACT.Copy).then_inc(mix_hi, 1)

            for t in range(NT):
                act.wait_ge(latT_done, t + 1)
                act.activation(fT_hi[:, 0:3, t * P:(t + 1) * P], ps[:, 6 + t, 0:3 * P].rearrange("p (k n) -> p k n", k=3),
                               ACT.Copy).then_inc(latT_hi, 1)
            act.wait_ge(latT_done, 3)
            act.activation(latkv_hi, ps[:, 0, :].rearrange("p (k n) -> p k n", k=2), ACT.Copy).then_inc(latT_hi, 1)
            exps(0)
            multiplied(act, 2 * U_IN + 1)
            q_flat = q96[:, 0, :, :].rearrange("p h n -> p (h n)")
            act.activation(q_flat[:, 0:HALF], ps[:, 6, :], ACT.Copy).then_inc(uq_act, 1)
            multiplied(act, 2 * U_IN + 3)
            act.activation(q_flat[:, HALF:], ps[:, 0, 0:256], ACT.Copy).then_inc(uq_act, 1)
            exps(1)
            base = 2 * (U_IN + U_UQ + U_UKV)
            probs_out(0)
            multiplied(act, base - 1)
            for half in range(2):
                kv = ps[:, 2 + half, :].rearrange("p (h n) -> p h n", h=4)
                act.activation(k96[:, 0, 4 * half:4 * half + 4, 0:B_NOPE], kv[:, :, 0:B_NOPE], ACT.Copy)
                ins = act.activation(v64[:, 0, 4 * half:4 * half + 4, :], kv[:, :, B_NOPE:], ACT.Copy)
            ins.then_inc(ukv_act, 1)
            mix_out(0)
            probs_out(1)
            split_until(base + 2)
            mix_out(1)
            for i in range(0, 8, 2):
                act.wait_ge(kqT_done, i + 1)
                dst = qbT if i < 4 else kbT
                t = (i % 4) // 2
                act.activation(dst[0:B_DIM, 0:4, t * P:(t + 1) * P],
                               ps[0:B_DIM, 2 + i % 4, :].rearrange("p (k n) -> p k n", k=4), ACT.Copy).then_inc(kqT_act, 1)
            split_until(base + 3)
            exps(2)
            exps(3)
            mix_out(2)
            probs_out(3)
            split_until(base + 5)
            mix_out(3)

            act.wait_ge(mix_lo, 4)
            act.wait_ge(dist_done, 1)
            for h in range(C_HEADS):
                log_gamma = math.log(1.0 - 2.0 ** (-5.0 - h))
                ins = act.activation(decay[:, h, :], dist[:, :], ACT.Exp, scale=log_gamma)
            ins.then_inc(decay_exp, 1)
            split_until(2 * (U_IN + U_UQ + U_UKV) + 4 + AHEAD)

            def chunk(sig, q, base, laps, with_down, before_turn=None):
                n = CHUNK_PIECES if with_down else 2 * GATE_UNITS
                for j in range(n):
                    if j == 3:
                        multiplied(act, base + 3, laps)
                        for t in range(sig.tiles):
                            act.activation(hid[:, t, :], ps[:, sig.gate_banks[t], :], ACT.Silu).then_inc(sig.silu_done, 1)
                    if j == n - 1:
                        if before_turn is not None:
                            before_turn()
                        for t in range(sig.tiles):
                            act.wait_ge(sig.turned, q * sig.tiles + t + 1)
                            act.activation(fT_hi[:, :, t * P:(t + 1) * P],
                                           ps[:, sig.turned_banks[t], :].rearrange("p (k n) -> p k n", k=4),
                                           ACT.Copy).then_inc(sig.turned_hi, 1)
                    split_hi(act, base + j + AHEAD, laps)

            def ffn(sig, q, base, lap, between, before_last, at_end=None):
                chunk(sig, q, base, lap, False, between)
                at = base + 2 * GATE_UNITS
                chunk(sig, q + 1, at, lap, True)
                at += CHUNK_PIECES
                with act.Fori(LOOP_FIRST, FC) as c:
                    chunk(sig, q + c, at, lap + c - LOOP_FIRST, True)
                if sig.tiles == NT:
                    return
                before_last()
                for j in range(2 * DOWN_UNITS):
                    if j == 2 * DOWN_UNITS - 1:
                        at_end()
                    split_hi(act, base + PASS_PIECES - 2 * DOWN_UNITS + j + AHEAD, lap)

            norm(1, 2 * FFN_UNIT)
            ffn(dense, 0, 2 * FFN_UNIT, 0, None, None)
            split_skip(2 * ODD_UNIT + 2)

            norm(2, 2 * ODD_UNIT)

            def turned_out(i):
                act.wait_ge(oddT_done, 2 * i + 1)
                act.activation((bT, uT, qT, kT)[i][:, :, 0:P], ps[:, 2 * (i % 2), :].rearrange("p (k n) -> p k n", k=4),
                               ACT.Copy).then_inc(oddT_act, 1)

            for j in range(ODD_IN_CHUNKS - 1):
                multiplied(act, 2 * ODD_UNIT + 4 * j + 3)
                src = ps[:, (4, 6)[j % 2], :]
                dst = (bc_nat[:, 0, 0, :], bc_nat[:, 1, 0, :], None, qk_nat[:, 0, 0, :], qk_nat[:, 1, 0, :],
                       val[:, 0, :, :].rearrange("p h n -> p (h n)"))[j]
                if dst is not None:
                    act.activation(dst, src, ACT.Copy).then_inc(odd_act, 1)
                split_until(2 * ODD_UNIT + 4 * (j + 1) + AHEAD)
                if j == 2:
                    turned_out(0)
                    turned_out(1)
                elif j == 3:
                    turned_out(2)
                elif j == 4:
                    turned_out(3)
                    act.wait_ge(conv_done, 1)
                    act.activation(fT_hi[:, :, :], conv, ACT.Copy).then_inc(mix_hi, 1)
            act.wait_ge(router_landed, 16)
            act.activation(router_hi[:, :, :], router[:, :, :], ACT.Copy).then_inc(router_hi_done, 1)
            odd_out = 2 * (ODD_UNIT + 2 * ODD_IN_CHUNKS)
            act.wait_ge(gn_inv, 1)
            act.activation(gn_rstd, gn_rstd, ACT.Sqrt).then_inc(gn_std, 1)
            split_until(odd_out + 4)
            multiplied(act, odd_out - 1)
            for t in range(NT):
                act.activation(gate[:, t, :], ps[:, 4 + t, :], ACT.Silu).then_inc(odd_act, 1)
            split_until(odd_out + 5)
            for t in range(NT):
                act.wait_ge(yrT_done, t + 1)
                act.activation(tok_hi[:, 0:4, t * P:(t + 1) * P], ps[:, (7, 0)[t], :].rearrange("p (k n) -> p k n", k=4),
                               ACT.Copy).then_inc(mix_hi, 1)
            split_until(odd_out + 4 + AHEAD)

            norm(3, 2 * MOE_UNIT)
            act.wait_ge(logitsT_done, 1)
            act.activation(logits_T, ps[0:EXPERTS, 4, 0:SEQ], ACT.Copy).then_inc(logitsT_out, 1)
            act.wait_ge(gap_done, 1)
            act.activation(gate1, gap, ACT.Exp).then_inc(gap_exp, 1)

            def gather_out(p):
                for i in range(2):
                    act.wait_ge(gathered, 2 * p + i + 1)
                    act.activation(tok_hi[:, 4 * i:4 * i + 4, 0:SLOTS],
                                   ps[:, GATHER_BANKS[i], :].rearrange("p (k n) -> p k n", k=4),
                                   ACT.Copy).then_inc(gather_hi, 1)

            def weights_out(p):
                act.wait_ge(weighT_done, p + 1)
                act.activation(weigh_T, ps[:, WEIGHT_BANK, 0:SEQ], ACT.Copy).then_inc(weighT_out, 1)

            def late(p):
                weights_out(p)
                gather_out(p + 1)

            def y_out(p):
                multiplied(act, 2 * MOE_UNIT + PASS_PIECES - 1, p * FC)
                act.activation(y_sb[:, 0:HALF], ps[:, moe.y_banks[0], :], ACT.Copy).then_inc(y_act, 1)

            def passes(lo, hi):
                with act.Fori(lo, hi) as p:
                    ffn(moe, p * FC, 2 * MOE_UNIT, p * FC, None, lambda: late(p), lambda: y_out(p))

            act.wait_ge(y_dve, 1)
            act.activation(weigh_T, y_sb[:, HALF:HALF + SEQ], ACT.Copy).then_inc(weighT_out, 1)
            act.activation(y_sb[:, 0:HALF], y_sb[:, HALF:D], ACT.Copy).then_inc(y_act, 1)
            gather_out(0)
            passes(0, EXPERTS)
            act.wait_ge(most_done, 1)
            full = act.value_load(most_i[0:1, 0:1])
            with act.If(full > SLOTS):
                passes(EXPERTS, 2 * EXPERTS)
            act.drain().then_inc(last_act, 1)
            act.wait_ge(last_act, 1)
            act.activation(warm, ident[:, 0:1], ACT.Sqrt)
            for t in range(NT):
                square(4, t, 0)
                square(4, t, 1)
                norm_root(4, t)

        @block.vector
        def _(dve):
            split_until, split_skip = splitter(split_lo, dve)
            step = [0]

            def link(ins):
                step[0] += 1
                ins.then_inc(dve_step, 1)
                dve.wait_ge(dve_step, step[0])

            def norm_mean(stage, t):
                done = 4 if t else norm_order(stage).index((0, 1)) + 1
                dve.wait_ge(sumsq_done, 4 * stage + done)
                link(dve.scalar_tensor_tensor(out=inv[:, t:t + 1], in0=sumsq[:, t, 0:1], scalar=EPS * D,
                                              in1=sumsq[:, t, 1:2], op0=ALU.add, op1=ALU.add))
                dve.reciprocal(inv[:, t:t + 1], inv[:, t:t + 1]).then_inc(inv_done, 1)

            def norm_apply(stage, t):
                dve.wait_ge(rstd_done, NT * stage + t + 1)
                if stage == 0:
                    dve.wait_ge(first_gain_landed, 16)
                else:
                    dve.wait_ge(gain_landed, 16 * stage)
                dve.scalar_tensor_tensor(out=xn[:, t, :], in0=x[:, t, :], scalar=rstd[:, t:t + 1],
                                         in1=gain[:, :], op0=ALU.mult, op1=ALU.mult)\
                   .then_inc(xn_done if stage < 4 else out_ready, 1)

            def norm_lo(stage, t):
                for half in range(2):
                    dst = (slice(None), slice(4 * half, 4 * half + 4), slice(t * P, (t + 1) * P))
                    dve.wait_ge(tok_hi_done, 4 * stage + 2 * t + half + 1)
                    dve.tensor_tensor(tok_lo[dst], ps[:, 2 * t + half, :].rearrange("p (k n) -> p k n", k=4),
                                      tok_hi[dst].bitcast(F32), ALU.subtract).then_inc(tok_lo_done, 1)

            def residual_norm(stage, base, banks, n_before):
                order = norm_order(stage)
                first = order.index((0, 1)) + 1

                def add(i):
                    t, half = order[i]
                    xs = x[:, t, half * HALF:(half + 1) * HALF]
                    dve.tensor_tensor(xs, xs, ps[:, banks[i], :], ALU.add).then_inc(x_updated, 1)

                if first == 3:
                    split_until(base)
                    multiplied(dve, base - 5)
                    add(0)
                    add(1)
                    split_until(base + 2)
                dve.wait_ge(tile0_done, n_before)
                for i in range(2 if first == 3 else 0, first):
                    add(i)
                norm_mean(stage, 0)
                norm_apply(stage, 0)
                split_until(base + 3)
                multiplied(dve, base - 1)
                add(first)
                if stage < 3:
                    norm_lo(stage, 0)
                for i in range(first + 1, 4):
                    add(i)
                norm_mean(stage, 1)
                norm_apply(stage, 1)
                if stage < 3:
                    split_until(base + 5)
                else:
                    norm_lo(stage, 0)
                norm_lo(stage, 1)
                split_until(base + AHEAD)

            for t in range(NT):
                norm_mean(0, t)
                norm_apply(0, t)
            for t in range(NT):
                split_until(1 + t)
                norm_lo(0, t)
            split_until(AHEAD)
            dve.wait_ge(pos_landed, 16)
            dve.wait_ge(freq_done, 1)
            link(dve.tensor_copy(pos_f, pos_i[:, :]))
            for t in range(NT):
                ins = dve.tensor_scalar(angle[:, t, :], inv_freq, pos_f[:, t:t + 1], None, ALU.mult)
            link(ins)
            link(dve.tensor_scalar(turns, angle, 1.0 / (2.0 * math.pi), None, ALU.mult))
            whole = 1.5 * 2.0 ** 23
            link(dve.tensor_scalar(turns, turns, whole, whole, ALU.add, ALU.subtract))
            two_pi = 2.0 * math.pi
            c1 = 6.28125
            c2 = float(np.float32(np.round((two_pi - c1) * 2.0 ** 21) / 2.0 ** 21))
            c3 = two_pi - c1 - c2
            for c in (c1, c2, c3):
                link(dve.scalar_tensor_tensor(out=angle, in0=turns, scalar=-c, in1=angle, op0=ALU.mult, op1=ALU.add))
            link(dve.tensor_scalar(angle, angle, math.pi, -math.pi, ALU.min, ALU.max))
            link(dve.scalar_tensor_tensor(out=turns, in0=angle, scalar=-1.0, in1=angle, op0=ALU.mult, op1=ALU.max))
            dve.tensor_scalar(turns, turns, -1.0, math.pi / 2.0, ALU.mult, ALU.add).then_inc(angle_done, 1)
            in_banks = (5, 7, 1)
            for j in range(3):
                multiplied(dve, 4 * j + 3)
                dve.tensor_copy(proj[:, 1, j * IN_CHUNK:(j + 1) * IN_CHUNK], ps[:, in_banks[j], 0:IN_CHUNK])\
                   .then_inc(in_dve, 1)
                if j < 2:
                    split_until(4 * (j + 1) + AHEAD)
            dve.wait_ge(in_act, 3)
            dve.wait_ge(in_dve, 3)
            for t in range(NT):
                dst = ka_twice[:, t, :].rearrange("p (g a n) -> p g a n", g=A_KV, a=2)
                src = proj[:, t, COL_K:COL_V].rearrange("p (g n) -> p g n", g=A_KV)
                for a in range(2):
                    ins = dve.tensor_copy(dst[:, :, a, :], src)
            ins.then_inc(ka_doubled, 1)
            dve.wait_ge(qaT_done, 2)
            dve.tensor_copy(qaT[:, :, P:SEQ], ps[:, 3, :].rearrange("p (k n) -> p k n", k=4)).then_inc(qaT_dve, 1)
            dve.wait_ge(qaT_done, 3)
            dve.tensor_copy(kaT, ps[:, 4, :].rearrange("p (k n) -> p k n", k=2)).then_inc(qaT_dve, 1)
            dve.wait_ge(lat_sq, 1)
            for i, n in enumerate((Q_LORA, KV_LORA)):
                ins = dve.tensor_scalar(lat_rstd[:, :, i], lat_sumsq[:, :, i], 1.0 / n, EPS, ALU.mult, ALU.add)
            link(ins)
            dve.reciprocal(lat_rstd, lat_rstd).then_inc(lat_inv, 1)
            split_until(2 * U_IN + 3)
            dve.wait_ge(lat_std, 1)
            dve.wait_ge(lat_gain_landed, 32)
            for t in range(NT):
                for i, (at, n, go) in enumerate(((COL_CQ, Q_LORA, 0), (COL_CKV, KV_LORA, Q_LORA))):
                    dve.scalar_tensor_tensor(out=proj[:, t, at:at + n], in0=proj[:, t, at:at + n],
                                             scalar=lat_rstd[:, t, i:i + 1], in1=lat_gain[:, go:go + n],
                                             op0=ALU.mult, op1=ALU.mult).then_inc(lat_done, 1)
            dve.wait_ge(sinks_landed, 16)
            sinks_pos = sinks.rearrange("p (j a) -> p a j", a=2)
            by_pos = lambda v: v.rearrange("p (a j) -> p a j", a=2)

            def softmax_start(inst):
                kind, t = "AABB"[inst], inst % 2
                nk = P * (t + 1)
                probs = probs_of[inst]
                row_max, neg_max, sink_e = (v[:, inst % 2, :] for v in (row_maxes, neg_maxes, sink_es))
                dve.wait_ge(scored, inst + 1)
                if kind == "A":
                    dve.wait_ge(bias_done, 1)
                    dve.wait_ge(lat_sq, 1)
                    for b in range(2 * (t + 1)):
                        if t == 0:
                            tab = bias[:, 4 * b:4 * b + 4, P:SEQ]
                            s = ps[:, SCORE_BANK[inst] + b, :].rearrange("p (h n) -> p h n", h=4)
                            o = probs[:, b * HALF:(b + 1) * HALF].rearrange("p (h n) -> p h n", h=4)
                        else:
                            tab = bias[:, 2 * b:2 * b + 2, :]
                            s = ps[:, SCORE_BANK[inst] + b, :].rearrange("p (h n) -> p h n", h=2)
                            o = probs[:, b * HALF:(b + 1) * HALF].rearrange("p (h n) -> p h n", h=2)
                        ins = dve.tensor_tensor(o, s, tab, ALU.add)
                    ins.then_inc(biased, 1)
                    dve.wait_ge(biased, inst + 1)
                    link(dve.tensor_reduce(row_max, probs[:, 0:8 * nk].rearrange("p (h n) -> p h n", h=8), AX.X, ALU.max))
                    link(dve.scalar_tensor_tensor(out=by_pos(row_max), in0=sinks_pos, scalar=1.0 / A_SCALE,
                                                  in1=by_pos(row_max), op0=ALU.mult, op1=ALU.max))
                    dve.tensor_scalar(neg_max, row_max, -A_SCALE, None, ALU.mult).then_inc(max_done, 1)
                    dve.wait_ge(max_done, inst + 1)
                    dve.tensor_tensor(by_pos(sink_e), sinks_pos, by_pos(neg_max), ALU.add).then_inc(sink_arg, 1)
                else:
                    s = flat_ps[:, SCORE_BANK[inst] * HALF:SCORE_BANK[inst] * HALF + 8 * nk].rearrange("p (h n) -> p h n", h=8)
                    link(dve.memset(s[0:CHUNK, :, nk - CHUNK:nk], -1.0e30))
                    link(dve.tensor_reduce(row_max, s, AX.X, ALU.max))
                    dve.tensor_scalar(neg_max, row_max, -B_SCALE, None, ALU.mult).then_inc(max_done, 1)

            def softmax_end(inst):
                kind, nk = "AABB"[inst], P * (inst % 2 + 1)
                den, sink_e = dens[:, inst % 2, :], sink_es[:, inst % 2, :]
                dve.wait_ge(exp_done, inst + 1)
                if kind == "A":
                    link(dve.tensor_tensor(den, den, sink_e, ALU.add))
                link(dve.reciprocal(den, den))
                pr = probs_of[inst][:, 0:8 * nk].rearrange("p (h n) -> p h n", h=8)
                dve.tensor_tensor(pr, pr, den[:, :, None].to_broadcast([P, 8, nk]), ALU.mult).then_inc(probs_done, 1)

            def probs_out(inst):
                for b in range(2 * (inst % 2 + 1)):
                    if not copied_by_act(inst, b):
                        dve.wait_ge(pT_done, PROBS_ORDER.index((inst, b)) + 1)
                        dve.tensor_copy(probsT_of[inst][b], ps[:, PROBS_BANKS[inst][b], :]).then_inc(pT_dve, 1)

            def mix_out(inst):
                k0, t = 4 * (inst // 2), inst % 2
                dve.wait_ge(mix_hi, inst + 1)
                dst = (slice(None), slice(k0, k0 + 4), slice(t * P, (t + 1) * P))
                dve.tensor_tensor(tok_lo[dst], ps[:, MIXED_BANK[inst], :].rearrange("p (k n) -> p k n", k=4),
                                  tok_hi[dst].bitcast(F32), ALU.subtract).then_inc(mix_lo, 1)

            softmax_start(0)
            base = 2 * (U_IN + U_UQ + U_UKV)
            for t in range(NT):
                dve.wait_ge(latT_hi, t + 1)
                dve.tensor_tensor(fT_lo[:, 0:3, t * P:(t + 1) * P], ps[:, 6 + t, 0:3 * P].rearrange("p (k n) -> p k n", k=3),
                                  fT_hi[:, 0:3, t * P:(t + 1) * P].bitcast(F32), ALU.subtract).then_inc(latT_lo, 1)
            dve.wait_ge(latT_hi, 3)
            dve.tensor_tensor(latkv_lo, ps[:, 0, :].rearrange("p (k n) -> p k n", k=2), latkv_hi.bitcast(F32),
                              ALU.subtract).then_inc(latT_lo, 1)
            split_until(base)
            softmax_start(1)
            multiplied(dve, 2 * U_IN + 1)
            q_flat = q96[:, 1, :, :].rearrange("p h n -> p (h n)")
            dve.tensor_copy(q_flat[:, 0:HALF], ps[:, 7, :]).then_inc(uq_dve, 1)
            softmax_end(0)
            multiplied(dve, 2 * U_IN + 3)
            dve.tensor_copy(q_flat[:, HALF:], ps[:, 1, 0:256]).then_inc(uq_dve, 1)
            softmax_end(1)
            multiplied(dve, base - 1)
            for half in range(2):
                kv = ps[:, 4 + half, :].rearrange("p (h n) -> p h n", h=4)
                dve.tensor_copy(k96[:, 1, 4 * half:4 * half + 4, 0:B_NOPE], kv[:, :, 0:B_NOPE])
                ins = dve.tensor_copy(v64[:, 1, 4 * half:4 * half + 4, :], kv[:, :, B_NOPE:])
            ins.then_inc(ukv_dve, 1)
            probs_out(0)
            mix_out(0)
            probs_out(1)
            split_until(base + 2)
            mix_out(1)
            for i in range(1, 8, 2):
                dve.wait_ge(kqT_done, i + 1)
                dst = qbT if i < 4 else kbT
                t = (i % 4) // 2
                dve.tensor_copy(dst[0:B_DIM, 4:8, t * P:(t + 1) * P],
                                ps[0:B_DIM, 2 + i % 4, :].rearrange("p (k n) -> p k n", k=4)).then_inc(kqT_dve, 1)
            softmax_start(2)
            split_until(base + 3)
            softmax_start(3)
            softmax_end(2)
            probs_out(2)
            softmax_end(3)
            mix_out(2)
            probs_out(3)
            split_until(base + 5)
            mix_out(3)

            def chunk(sig, q, base, laps, with_down, before_turn=None):
                n = CHUNK_PIECES if with_down else 2 * GATE_UNITS
                for j in range(n):
                    if j == 7:
                        multiplied(dve, base + 7, laps)
                        for t in range(sig.tiles):
                            dve.wait_ge(sig.silu_done, q * sig.tiles + t + 1)
                            dve.tensor_tensor(hid[:, t, :], hid[:, t, :], ps[:, sig.up_banks[t], :], ALU.mult)\
                               .then_inc(sig.act_done, 1)
                    if j == n - 1:
                        if before_turn is not None:
                            before_turn()
                        for t in range(sig.tiles):
                            dve.wait_ge(sig.turned_hi, q * sig.tiles + t + 1)
                            dve.tensor_tensor(fT_lo[:, :, t * P:(t + 1) * P],
                                              ps[:, sig.turned_banks[t], :].rearrange("p (k n) -> p k n", k=4),
                                              fT_hi[:, :, t * P:(t + 1) * P].bitcast(F32), ALU.subtract)\
                               .then_inc(sig.turned_lo, 1)
                    split_lo(dve, base + j + AHEAD, laps)

            def ffn(sig, q, base, lap, between, before_last, at_end=None):
                chunk(sig, q, base, lap, False, between)
                at = base + 2 * GATE_UNITS
                chunk(sig, q + 1, at, lap, True)
                at += CHUNK_PIECES
                with dve.Fori(LOOP_FIRST, FC) as c:
                    chunk(sig, q + c, at, lap + c - LOOP_FIRST, True)
                if sig.tiles == NT:
                    return
                before_last()
                for j in range(2 * DOWN_UNITS):
                    if j == 2 * DOWN_UNITS - 1:
                        at_end()
                    split_lo(dve, base + PASS_PIECES - 2 * DOWN_UNITS + j + AHEAD, lap)

            residual_norm(1, 2 * FFN_UNIT, EVEN_OUT_BANKS, 1)
            dve.wait_ge(decay_exp, 1)
            dve.tensor_scalar(decay, decay, float(C_DIM) ** -0.5, None, ALU.mult)
            ffn(dense, 0, 2 * FFN_UNIT, 0, None, None)
            split_skip(2 * ODD_UNIT + 2)

            residual_norm(2, 2 * ODD_UNIT, dense.y_banks, 2)

            def turned_out(i):
                dve.wait_ge(oddT_done, 2 * i + 2)
                dve.tensor_copy((bT, uT, qT, kT)[i][:, :, P:SEQ], ps[:, 2 * (i % 2) + 1, :].rearrange("p (k n) -> p k n", k=4))\
                   .then_inc(oddT_dve, 1)

            def convolve(shift):
                for k in range(4):
                    w = conv_w[:, CONV_W - 1 - shift, k:k + 1]
                    if shift == 0:
                        ins = dve.tensor_scalar(conv[:, k, :], uT[:, k, :], w, None, ALU.mult)
                    else:
                        ins = dve.scalar_tensor_tensor(out=conv[:, k, shift:], in0=uT[:, k, 0:SEQ - shift], scalar=w,
                                                       in1=conv[:, k, shift:], op0=ALU.mult, op1=ALU.add)
                link(ins)

            def decay_scores():
                for i in range(3):
                    dve.wait_ge(ret_scored, i + 1)
                    if i < 2:
                        dve.tensor_tensor(sT0[:, 2 * i:2 * i + 2, :], ps[:, i, :].rearrange("p (h n) -> p h n", h=2),
                                          decay[:, 2 * i:2 * i + 2, :], ALU.mult).then_inc(ret_decayed, 1)
                    else:
                        dve.tensor_tensor(sT1, ps[:, 2, :].rearrange("p (h n) -> p h n", h=C_HEADS), decay[:, :, 0:P],
                                          ALU.mult).then_inc(ret_decayed, 1)

            for j in range(ODD_IN_CHUNKS - 1):
                base = 2 * ODD_UNIT + 4 * j
                if j == 5:
                    decay_scores()
                multiplied(dve, base + 3)
                src = ps[:, (5, 7)[j % 2], :]
                if j == 2:
                    dve.wait_ge(odd_act, 2)
                    dve.wait_ge(odd_dve, 2)
                    for t in range(NT):
                        ins = dve.tensor_tensor(bc_nat[:, 1, t, :], bc_nat[:, 1, t, :], ps[:, 4 + t, :], ALU.mult)
                    ins.then_inc(odd_dve, 1)
                else:
                    dst = (bc_nat[:, 0, 1, :], bc_nat[:, 1, 1, :], None, qk_nat[:, 0, 1, :], qk_nat[:, 1, 1, :],
                           val[:, 1, :, :].rearrange("p h n -> p (h n)"))[j]
                    dve.tensor_copy(dst, src).then_inc(odd_dve, 1)
                if j == 1:
                    dve.wait_ge(conv_turned, 1)
                    dve.tensor_copy(conv_w, ps[:, 0, 0:CONV_W * 4].rearrange("p (j k) -> p j k", j=CONV_W))\
                       .then_inc(dve_conv, 1)
                split_until(base + 4 + AHEAD - 1)
                if j == 2:
                    turned_out(0)
                    turned_out(1)
                    dve.wait_ge(oddT_act, 2)
                    dve.wait_ge(oddT_dve, 2)
                    dve.wait_ge(dve_conv, 1)
                    convolve(0)
                elif j == 3:
                    turned_out(2)
                    convolve(1)
                    convolve(2)
                    dve.tensor_tensor(conv, conv, bT, ALU.mult).then_inc(conv_done, 1)
                elif j == 4:
                    turned_out(3)
                    dve.wait_ge(mix_hi, 5)
                    dve.wait_ge(conv_done, 1)
                    dve.tensor_tensor(fT_lo[:, :, :], conv, fT_hi[:, :, :].bitcast(F32), ALU.subtract).then_inc(mix_lo, 1)
                if j < 5:
                    split_until(base + 4 + AHEAD)
            odd_out = 2 * (ODD_UNIT + 2 * ODD_IN_CHUNKS)
            split_until(odd_out + 2)
            dve.wait_ge(router_hi_done, 1)
            dve.tensor_tensor(router_lo[:, :, :], router[:, :, :], router_hi[:, :, :].bitcast(F32), ALU.subtract)\
               .then_inc(router_lo_done, 1)
            for t in range(NT):
                dve.wait_ge(ret_out, t + 1)
                for h in range(C_HEADS):
                    ins = dve.bn_stats(bn[:, t * C_HEADS + h, :], ps[:, RET_BANKS[t], h * P:(h + 1) * P])
            link(ins)
            for i in range(NT * C_HEADS):
                ins = dve.bn_aggr(mv[:, i, :], bn[:, i, :])
            link(ins)
            link(dve.tensor_scalar(gn_rstd, mv[:, :, 1], EPS, None, ALU.add))
            dve.reciprocal(gn_rstd, gn_rstd).then_inc(gn_inv, 1)
            dve.wait_ge(gn_std, 1)
            for t in range(NT):
                for h in range(C_HEADS):
                    i = t * C_HEADS + h
                    ins = dve.tensor_scalar(yr[:, t, h * P:(h + 1) * P], ps[:, RET_BANKS[t], h * P:(h + 1) * P],
                                            mv[:, i, 0:1], gn_rstd[:, i:i + 1], ALU.subtract, ALU.mult)
            link(ins)
            dve.wait_ge(gn_gain_landed, 16)
            link(dve.tensor_tensor(yr, yr, gn_gain[:, None, :].to_broadcast([P, NT, HALF]), ALU.mult))
            for t in range(NT):
                dve.wait_ge(odd_act, 6 + t)
                dve.tensor_tensor(yr[:, t, :], yr[:, t, :], gate[:, t, :], ALU.mult).then_inc(yr_done, 1)
            split_until(odd_out + 3)
            for t in range(NT):
                dve.wait_ge(mix_hi, 6 + t)
                dst = (slice(None), slice(0, 4), slice(t * P, (t + 1) * P))
                dve.tensor_tensor(tok_lo[dst], ps[:, (7, 0)[t], :].rearrange("p (k n) -> p k n", k=4),
                                  tok_hi[dst].bitcast(F32), ALU.subtract).then_inc(mix_lo, 1)
            residual_norm(3, 2 * MOE_UNIT, ODD_OUT_BANKS, 3)
            dve.wait_ge(logits_done, 1)
            dve.wait_ge(route_consts, 1)
            logits = ps[:, 5, 0:NT * EXPERTS].rearrange("p (t e) -> p t e", t=NT)
            for t in range(NT):
                ins = dve.max(top[:, t, :], logits[:, t, :])
            link(ins)
            for t in range(NT):
                ins = dve.max_index(idx_u[:, t, :], top[:, t, :], logits[:, t, :])
            link(ins)
            dve.tensor_tensor(gap, top[:, :, 1], top[:, :, 0], ALU.subtract).then_inc(gap_done, 1)
            link(dve.tensor_copy(idx_f, idx_u[:, :, 0:2]))
            every = lambda v: v.to_broadcast([P, NT, EXPERTS])
            dve.tensor_tensor(pick1, every(iota8[:, None, :]), every(idx_f[:, :, 0:1]), ALU.is_equal)
            link(dve.tensor_tensor(pick2, every(iota8[:, None, :]), every(idx_f[:, :, 1:2]), ALU.is_equal))
            dve.tensor_tensor(chosen, pick1, pick2, ALU.add).then_inc(chosen_done, 1)
            dve.wait_ge(gap_exp, 1)
            link(dve.tensor_scalar(gate2, gate1, 1.0, None, ALU.add))
            link(dve.reciprocal(gate2, gate2))
            link(dve.tensor_tensor(gate1, gate1, gate2, ALU.mult))
            for t in range(NT):
                link(dve.tensor_scalar(pick1[:, t, :], pick1[:, t, :], gate2[:, t:t + 1], None, ALU.mult))
                ins = dve.scalar_tensor_tensor(out=share[:, t, 0:EXPERTS], in0=pick2[:, t, :], scalar=gate1[:, t:t + 1],
                                               in1=pick1[:, t, :], op0=ALU.mult, op1=ALU.add)
            link(ins)
            dve.memset(share[:, :, 2 * EXPERTS:], 0.0)
            dve.memset(place[:, :, 2 * EXPERTS:], -1.0)
            link(dve.tensor_copy(share[:, :, EXPERTS:2 * EXPERTS], share[:, :, 0:EXPERTS]))
            dve.wait_ge(counted, 1)
            dve.wait_ge(chosen_done, 1)
            link(dve.scalar_tensor_tensor(out=place1, in0=ps[:, 7, 0:NT * EXPERTS].rearrange("p (t e) -> p t e", t=NT),
                                          scalar=1.0, in1=chosen, op0=ALU.add, op1=ALU.mult))
            link(dve.tensor_scalar(place[:, :, 0:EXPERTS], place1, -1.0, None, ALU.add))

            def make_pick(p):
                for t in range(NT):
                    ins = dve.tensor_scalar(pick[:, t, :], iota_slot, place[:, t, bass.ds(p, 1)], None, ALU.is_equal)
                ins.then_inc(pick_done, 1)

            def make_weigh(p):
                for t in range(NT):
                    ins = dve.tensor_scalar(weigh[:, t, :], iota_slot, place[:, t, bass.ds(p, 1)],
                                            share[:, t, bass.ds(p, 1)], ALU.is_equal, ALU.mult)
                ins.then_inc(weigh_done, 1)

            def gather_out(p):
                for i in range(2):
                    dst = (slice(None), slice(4 * i, 4 * i + 4), slice(0, SLOTS))
                    dve.wait_ge(gather_hi, 2 * p + i + 1)
                    dve.tensor_tensor(tok_lo[dst], ps[:, GATHER_BANKS[i], :].rearrange("p (k n) -> p k n", k=4),
                                      tok_hi[dst].bitcast(F32), ALU.subtract).then_inc(gather_lo, 1)

            def add_scattered(done, first, halves, signal):
                for i in halves:
                    t, half = i // 2, i % 2
                    xs = x[:, t, half * HALF:(half + 1) * HALF]
                    dve.wait_ge(done, first + i + 1)
                    dve.tensor_tensor(xs, xs, ps[:, SCATTER_BANKS[i], :], ALU.add).then_inc(signal, 1)

            def y_out(p):
                multiplied(dve, 2 * MOE_UNIT + PASS_PIECES - 1, p * FC)
                dve.tensor_copy(y_sb[:, HALF:D], ps[:, moe.y_banks[1], :]).then_inc(y_dve, 1)

            def passes(lo, hi):
                with dve.Fori(lo, hi) as p:
                    make_weigh(p)
                    make_pick(p + 1)
                    ffn(moe, p * FC, 2 * MOE_UNIT, p * FC, lambda: add_scattered(scattered, 4 * p, range(4), moe_added),
                        lambda: gather_out(p + 1), lambda: y_out(p))

            make_pick(0)
            dve.tensor_scalar(place[:, :, EXPERTS:2 * EXPERTS], place1, -1.0 - SLOTS, None, ALU.add)
            dve.wait_ge(all_counted, 1)
            link(dve.tensor_reduce(most, ps[:, 4, 0:EXPERTS], AX.X, ALU.max))
            dve.tensor_copy(most_i[:, :], most).then_inc(most_done, 1)
            dve.wait_ge(most_done, 1)
            dve.memset(y_sb[:, HALF:D], 0.0).then_inc(y_dve, 1)
            gather_out(0)
            passes(0, EXPERTS)
            full = dve.value_load(most_i[0:1, 0:1])
            with dve.If(full > SLOTS):
                passes(EXPERTS, 2 * EXPERTS)
            dve.drain().then_inc(last_dve, 1)
            dve.wait_ge(last_dve, 1)
            for t in range(NT):
                add_scattered(last_scattered, 0, (2 * t, 2 * t + 1), x_updated)
                norm_mean(4, t)
            for t in range(NT):
                norm_apply(4, t)


_NAMES = ["x", "positions", "even_norm_mix", "even_w_in", "even_sinks", "even_q_norm", "even_w_uq", "even_kv_norm",
          "even_w_ukv", "even_w_out", "even_norm_ffn", "even_w_gate", "even_w_up", "even_w_down", "odd_norm_mix",
          "odd_w_in", "odd_ret_gn", "odd_conv_w", "odd_w_out", "odd_norm_ffn", "odd_router", "odd_we_gate", "odd_we_up",
          "odd_we_down", "final_norm"]


def kernel(**inputs):
    import concourse.bacc as bacc
    from concourse.bass_utils import run_bass_kernel_spmd

    nc = bacc.Bacc("TRN2", target_bir_lowering=False, num_devices=1)
    arrays, aps = {}, {}
    for name in _NAMES:
        a = np.ascontiguousarray(inputs[name])
        arrays[f"in_{name}"] = a
        aps[name] = nc.dram_tensor(f"in_{name}", a.shape, mybir.dt.from_np(a.dtype), kind="ExternalInput").ap()
    out = nc.dram_tensor("out_y", (1, SEQ, D), F32, kind="ExternalOutput").ap()
    build_trunk(nc, aps, out)
    r = run_bass_kernel_spmd(nc, [arrays], core_ids=[0])
    return r.results[0]["out_y"]
```
